# Optimizing a Trainium2 kernel written in Bass

```python
import math
import jax, jax.numpy as jnp
from jax import lax
import numpy as np

D_MODEL = 2048
BATCH = 1
SEQ = 256
DEPTH = 1

GRID_W = 64
NA_HEADS = 8
NA_HEAD_DIM = 128
NA_WIDTH = NA_HEADS * NA_HEAD_DIM
NA_MAX_ROWS = 8
NA_COLS = 16
S5_GROUP = 16
S5_GROUPS = 64
S5_WIDTH = S5_GROUP * S5_GROUPS
S5_STATE = 64
D_FF = 256 * (-(-8 * D_MODEL // (3 * 256)))
IN_COLS = 3 * NA_WIDTH + S5_WIDTH + 2 * D_MODEL
LN_EPS = 1e-5
DEEPNORM_ALPHA = (2.0 * DEPTH) ** 0.25
DEEPNORM_BETA = (8.0 * DEPTH) ** -0.25

kernel_name = "hybrid_natten_s5_gated_deepnorm"

def _layer_norm(x, g, b):
    xf = x.astype(jnp.float32)
    mu = jnp.mean(xf, axis=-1, keepdims=True)
    var = jnp.mean(jnp.square(xf - mu), axis=-1, keepdims=True)
    y = (xf - mu) * lax.rsqrt(var + LN_EPS) * g.astype(jnp.float32) + b.astype(jnp.float32)
    return y.astype(x.dtype)

def _neighbourhood_attention(q, k, v, rpb):
    bsz, seq = q.shape[0], q.shape[1]
    rows = seq // GRID_W
    kh = min(NA_MAX_ROWS, rows)
    kw = NA_COLS
    grid = lambda t: t.reshape(bsz, rows, GRID_W, NA_HEADS, NA_HEAD_DIM)
    qg, kg, vg = grid(q), grid(k), grid(v)
    cols = jnp.arange(GRID_W)
    col_start = jnp.clip(cols - kw // 2, 0, GRID_W - kw)
    col_mask = (cols[None, :] >= col_start[:, None]) & (cols[None, :] < col_start[:, None] + kw)
    col_idx = jnp.clip(cols[None, :] - cols[:, None], -(kw - 1), kw - 1) + (NA_COLS - 1)
    rpb32 = rpb.astype(jnp.float32)
    scale = NA_HEAD_DIM ** -0.5

    def row_block(r):
        r0 = jnp.clip(r - kh // 2, 0, rows - kh)
        q_r = lax.dynamic_index_in_dim(qg, r, axis=1, keepdims=False)
        k_b = lax.dynamic_slice_in_dim(kg, r0, kh, axis=1)
        v_b = lax.dynamic_slice_in_dim(vg, r0, kh, axis=1)
        s = jnp.einsum("bqhd,bikhd->bhqik", q_r, k_b).astype(jnp.float32) * scale
        row_idx = r0 + jnp.arange(kh) - r + (NA_MAX_ROWS - 1)
        bias = rpb32[:, row_idx][:, :, col_idx].transpose(0, 2, 1, 3)
        s = jnp.where(col_mask[None, None, :, None, :], s + bias[None], -1e30)
        p = jax.nn.softmax(s.reshape(bsz, NA_HEADS, GRID_W, kh * GRID_W), axis=-1)
        p = p.reshape(s.shape).astype(v.dtype)
        return jnp.einsum("bhqik,bikhd->bqhd", p, v_b)

    out = lax.map(row_block, jnp.arange(rows))
    return out.transpose(1, 0, 2, 3, 4).reshape(bsz, seq, NA_WIDTH)

def _s5_scan(u, a_re, a_im, log_dt, b_re, b_im, c_re, c_im, reverse):
    f32 = jnp.float32
    lam = lax.complex(a_re.astype(f32), a_im.astype(f32))
    dt = jnp.exp(log_dt.astype(f32))[:, None]
    lam_bar = jnp.exp(lam * dt)
    b = lax.complex(b_re.astype(f32), b_im.astype(f32))
    b_bar = ((lam_bar - 1.0) / lam)[..., None] * b
    bu = jnp.einsum("blgc,gpc->blgp", u.astype(jnp.complex64), b_bar)
    a = jnp.broadcast_to(lam_bar, bu.shape)

    def combine(e1, e2):
        a1, s1 = e1
        a2, s2 = e2
        return a1 * a2, a2 * s1 + s2

    _, states = lax.associative_scan(combine, (a, bu), reverse=reverse, axis=1)
    return (jnp.einsum("blgp,gcp->blgc", states.real, c_re.astype(f32))
            - jnp.einsum("blgp,gcp->blgc", states.imag, c_im.astype(f32)))

def setup_inputs(seed: int = 0) -> dict:
    key = jax.random.key(seed)
    ks = jax.random.split(key, 32)
    f32 = jnp.float32
    L = DEPTH
    nrm = lambda k, shape, sc: jax.random.normal(k, shape, f32) * sc
    n = jnp.arange(S5_STATE, dtype=f32)
    return {
        "x": nrm(ks[0], (BATCH, SEQ, D_MODEL), 1.0),
        "w_in": nrm(ks[1], (L, D_MODEL, IN_COLS), D_MODEL ** -0.5),
        "b_gate": nrm(ks[2], (L, 2 * D_MODEL), 0.02),
        "na_rpb": nrm(ks[3], (L, NA_HEADS, 2 * NA_MAX_ROWS - 1, 2 * NA_COLS - 1), 0.1),
        "w_na_out": nrm(ks[4], (L, NA_WIDTH, D_MODEL), NA_WIDTH ** -0.5),
        "s5_a_re": -0.5 + nrm(ks[5], (L, 2, S5_GROUPS, S5_STATE), 0.01),
        "s5_a_im": math.pi * n + nrm(ks[6], (L, 2, S5_GROUPS, S5_STATE), 0.01),
        "s5_log_dt": jax.random.uniform(ks[7], (L, 2, S5_GROUPS), f32, math.log(1e-3), math.log(1e-1)),
        "s5_b_re": nrm(ks[8], (L, 2, S5_GROUPS, S5_STATE, S5_GROUP), (2 * S5_GROUP) ** -0.5),
        "s5_b_im": nrm(ks[9], (L, 2, S5_GROUPS, S5_STATE, S5_GROUP), (2 * S5_GROUP) ** -0.5),
        "s5_c_re": nrm(ks[10], (L, 2, S5_GROUPS, S5_GROUP, S5_STATE), (2 * S5_STATE) ** -0.5),
        "s5_c_im": nrm(ks[11], (L, 2, S5_GROUPS, S5_GROUP, S5_STATE), (2 * S5_STATE) ** -0.5),
        "s5_d": nrm(ks[12], (L, S5_GROUPS, S5_GROUP), 1.0),
        "w_glu": nrm(ks[13], (L, S5_WIDTH, S5_WIDTH), S5_WIDTH ** -0.5),
        "b_glu": nrm(ks[14], (L, S5_WIDTH), 0.02),
        "w_s5_out": nrm(ks[15], (L, S5_WIDTH, D_MODEL), S5_WIDTH ** -0.5),
        "w_out": nrm(ks[16], (L, D_MODEL, D_MODEL), DEEPNORM_BETA * D_MODEL ** -0.5),
        "ln1_g": 1.0 + nrm(ks[17], (L, D_MODEL), 0.02),
        "ln1_b": nrm(ks[18], (L, D_MODEL), 0.02),
        "w_ffn_gate": nrm(ks[19], (L, D_MODEL, D_FF), D_MODEL ** -0.5),
        "w_ffn_up": nrm(ks[20], (L, D_MODEL, D_FF), D_MODEL ** -0.5),
        "w_ffn_down": nrm(ks[21], (L, D_FF, D_MODEL), DEEPNORM_BETA * D_FF ** -0.5),
        "ln2_g": 1.0 + nrm(ks[22], (L, D_MODEL), 0.02),
        "ln2_b": nrm(ks[23], (L, D_MODEL), 0.02),
    }

def reference(x, w_in, b_gate, na_rpb, w_na_out, s5_a_re, s5_a_im, s5_log_dt, s5_b_re, s5_b_im,
              s5_c_re, s5_c_im, s5_d, w_glu, b_glu, w_s5_out, w_out, ln1_g, ln1_b,
              w_ffn_gate, w_ffn_up, w_ffn_down, ln2_g, ln2_b):
    bsz, seq, _ = x.shape
    splits = [NA_WIDTH, 2 * NA_WIDTH, 3 * NA_WIDTH, 3 * NA_WIDTH + S5_WIDTH,
              3 * NA_WIDTH + S5_WIDTH + D_MODEL]
    for l in range(DEPTH):
        proj = x @ w_in[l]
        q, k, v, u, g_att, g_ssm = jnp.split(proj, splits, axis=-1)
        g_att = jax.nn.sigmoid(g_att + b_gate[l, :D_MODEL])
        g_ssm = jax.nn.sigmoid(g_ssm + b_gate[l, D_MODEL:])

        heads = lambda t: t.reshape(bsz, seq, NA_HEADS, NA_HEAD_DIM)
        y_att = _neighbourhood_attention(heads(q), heads(k), heads(v), na_rpb[l]) @ w_na_out[l]

        ug = u.astype(jnp.float32).reshape(bsz, seq, S5_GROUPS, S5_GROUP)
        y_f = _s5_scan(ug, s5_a_re[l, 0], s5_a_im[l, 0], s5_log_dt[l, 0], s5_b_re[l, 0], s5_b_im[l, 0],
                       s5_c_re[l, 0], s5_c_im[l, 0], reverse=False)
        y_b = _s5_scan(ug, s5_a_re[l, 1], s5_a_im[l, 1], s5_log_dt[l, 1], s5_b_re[l, 1], s5_b_im[l, 1],
                       s5_c_re[l, 1], s5_c_im[l, 1], reverse=True)
        y_s = (y_f + y_b + s5_d[l].astype(jnp.float32) * ug).reshape(bsz, seq, S5_WIDTH).astype(x.dtype)
        y_s = jax.nn.gelu(y_s)
        y_s = y_s * jax.nn.sigmoid(y_s @ w_glu[l] + b_glu[l])
        y_ssm = y_s @ w_s5_out[l]

        mix = (g_att * y_att + g_ssm * y_ssm) @ w_out[l]
        h = _layer_norm(DEEPNORM_ALPHA * x + mix, ln1_g[l], ln1_b[l])

        ff = (jax.nn.silu(h @ w_ffn_gate[l]) * (h @ w_ffn_up[l])) @ w_ffn_down[l]
        x = _layer_norm(DEEPNORM_ALPHA * h + ff, ln2_g[l], ln2_b[l])
    return x


_drawn_inputs = setup_inputs


def setup_inputs(seed=0):
    import zlib

    import numpy as np

    out = dict(_drawn_inputs(seed))
    spreads = {}
    factors = {'b_gate': 52.792,
     'na_rpb': 8.0,
     's5_a_re': 64.0,
     's5_a_im': 60.592,
     's5_log_dt': 62.0,
     's5_b_re': 64.0,
     's5_b_im': 64.0,
     's5_c_re': 64.0,
     's5_c_im': 64.0,
     'b_glu': 56.612,
     'ln1_g': 2.712,
     'ln1_b': 2.726,
     'ln2_g': 8.015,
     'ln2_b': 8.153}
    for name, (base, spread) in spreads.items():
        noise = np.random.default_rng([zlib.crc32(name.encode()), seed]).standard_normal(out[name].shape)
        drawn = base * np.exp(spread * noise) if base else spread * noise
        out[name] = __import__('jax').numpy.asarray(drawn.astype(out[name].dtype))
    for name, factor in factors.items():
        out[name] = (out[name] * factor).astype(out[name].dtype)
    return out
```

```python
from contextlib import ExitStack

import numpy as np

import concourse.bass as bass
from concourse import mybir

F32 = mybir.dt.float32
F32R = mybir.dt.float32r
I32 = mybir.dt.int32
ALU = mybir.AluOpType
ACT = mybir.ActivationFunctionType
AX = mybir.AxisListType

P = 128
T = 256
TT = T // P
D = 2048
KD = D // P
HEADS = 8
DH = 128
GRID_W = 64
ROWS = T // GRID_W
WIN = 16
NW = HEADS * DH
SW = 1024
KS = SW // P
GROUPS = 64
GC = 16
NS = 64
DFF = 5632
KF = DFF // P
EPS = 1e-5
ALPHA = 2.0 ** 0.25
SCALE = DH ** -0.5

HC = 1024
RAW = 4
SPL = 3
PER_F = 12
TILES = 8
AT = 8
BT = 16
BASE = 3 * AT + 2 * BT + 4
O_A, O_B, O_R, O_KR, O_KI, O_NKI = 0, 3 * AT, BASE - 4, BASE - 3, BASE - 2, BASE - 1
PACK = 512 + 2 * TILES * 32 + 1

H_U = 0
H_V = H_U + 2 * KS
H_LOOP = H_V + 2 * KS
H_NA1 = H_LOOP + PER_F * HEADS
H_GLU = H_NA1 + 8
H_NA2 = H_GLU + 8
H_S5O = H_NA2 + 8
H_WO = H_S5O + KD
H_FF = H_WO + 4 * (KD // 2)
H_DN = H_FF + 4 * KF
H_END = H_DN + 4 * (KF // 2)

N_U, N_V, N_LOOP = 0, 8, 12
N_NA1 = N_LOOP + 6 * HEADS
N_GLU, N_NA2, N_S5O = N_NA1 + 8, N_NA1 + 16, N_NA1 + 24
N_WO = N_S5O + KD
N_FF = N_WO + 8
N_DN = N_FF + 2 * KF

EXP_C = [1 / 2, 1 / 6, 1 / 24, 1 / 120, 1 / 720, 1 / 5040]
SIN_C = [-1 / 6, 1 / 120, -1 / 5040, 1 / 362880, -1 / 39916800, 1 / 6227020800]
COS_C = [-1 / 2, 1 / 24, -1 / 720, 1 / 40320, -1 / 3628800, 1 / 479001600]
MAGIC = 12582912.0
LN2_HI, LN2_LO = 0.693359375, -2.12194440e-4
TWO_PI = [6.28125, 0.0019340515136718750, 1.2556659146753e-06]

BU_SLOT = [0, 1, 3, 4, 5, 7, 8, 9]
LAG = 2


def build(nc, wstream, xT, xtok, pack, params, bias, cols, lnrows, out):
    ctx = ExitStack()
    with ctx:
        B0 = (nc.sbuf_base + 63) // 32 * 32

        def at(name, shape, dt, kb):
            return nc.alloc_sbuf_tensor_at(name, shape, dt, offset=B0 + int(kb * 1024))

        def sem(name):
            return ctx.enter_context(nc.semaphore(name))

        raw = at("raw", [P, RAW, HC], F32, 0)
        whi = at("whi", [P, SPL, HC], F32R, 16)
        wlo = at("wlo", [P, SPL, HC], F32R, 28)
        act16 = at("act16", [P, KD, 2, T], F32R, 40)
        ident = at("ident", [P, P], F32, 72)
        mask = at("mask", [P, GRID_W], F32, 72.5)
        col = at("col", [P, 72], F32, 72.75)
        stats = at("stats", [P, TT, 4, 6], F32, 73.125)
        lnm = at("lnm", [P, TT, 5], F32, 73.375)
        eps1 = at("eps1", [P, 1], F32, 73.5)
        act8a = at("act8a", [P, KS, 2, T], F32R, 74)
        u = at("u", [P, KS, T], F32, 90)
        ga = at("ga", [P, KD, T], F32, 98)
        gs = at("gs", [P, KD, T], F32, 114)
        xraw = at("xraw", [P, KD, T], F32, 98)
        base_all = at("base_all", [P, GROUPS, BASE], F32, 114)
        scratch = at("scratch", [P, 32, GROUPS], F32, 185)
        vout = at("vout", [P, TT, 512], F32, 108)
        base = at("base", [P, 2, TILES, BASE], F32, 130)
        pk = at("pk", [P, 2, PACK], F32, 133.75)
        cmat = at("cmat", [P, 2, TILES, 3, 32], F32, 142)
        ctmp = at("ctmp", [P, 2, TILES, 32], F32, 148)
        ucur = at("ucur", [P, 2, 2, T], F32, 150)
        vcur = at("vcur", [P, 2, TT, DH], F32, 154)
        qk = at("qk", [P, 2, 2, T], F32, 156)
        bm = at("bm", [P, 2, TT, T], F32, 160)
        S = at("S", [P, TT, T], F32, 164)
        PT = at("PT", [P, TT, T], F32, 166)
        sm = at("sm", [P, 4, TT], F32, 168)
        fin_t = at("fin_t", [P, T], F32, 204.5)
        E = at("E", [P, 4, 2, T], F32, 168.5)
        tt12 = at("tt12", [P, 2, 2, P], F32, 176.5)
        m12 = at("m12", [P, 2, 2, T], F32, 178.5)
        wz = at("wz", [P, 2, T], F32, 182.5)
        z = at("z", [P, 2, 2, T], F32, 184.5)
        prod = at("prod", [P, 4, 4, T], F32, 188.5)
        act8b = at("act8b", [P, KS, 2, T], F32R, 130)
        mid = at("mid", [P, KF, 2, T], F32R, 74)
        hp = at("hp", [P, TT, D], F32, 162)
        lnrow = at("lnrow", [P, 2, D], F32, 178)
        ev = at("ev", [P, 4, T], F32, 194)
        ev2 = at("ev2", [P, 4, T], F32, 198)
        hT = at("hT", [P, 2, 2, T], F32, 202)

        ps = [ctx.enter_context(nc.psum_tensor(f"bank{i}", [P, 512], F32)) for i in range(8)]
        BU0, YB, AB, TB = 3, 5, 6, 7

        base_dram = nc.dram_tensor("base_dram", [P, GROUPS, BASE], F32, kind="Internal").ap()
        v_dram = nc.dram_tensor("v_dram", [T, NW], F32, kind="Internal").ap()

        raw_landed = [sem(f"raw_landed{i}") for i in range(RAW)]
        hi_ready, lo_ready, w_used = sem("hi_ready"), sem("lo_ready"), sem("w_used")
        uv_copied, loop_copied, res_added = sem("uv_copied"), sem("loop_copied"), sem("res_added")
        x_landed = [sem(f"x_landed{i}") for i in range(4)]
        x_hi, x_lo = sem("x_hi"), sem("x_lo")
        col_landed, par_landed = sem("col_landed"), sem("par_landed")
        const_step = sem("const_step")
        par_step, par_done, tab_step, base_stored = sem("par_step"), sem("par_done"), sem("tab_step"), sem("base_stored")
        v_stored = [sem("v_stored0"), sem("v_stored1")]
        pk_staged = [sem("pk_staged0"), sem("pk_staged1")]
        base_staged = [sem("base_staged0"), sem("base_staged1")]
        v_staged = [sem("v_staged0"), sem("v_staged1")]
        bias_staged = [sem("bias_staged0"), sem("bias_staged1")]
        ucur_ready, bu_ready, bu_read = sem("ucur_ready"), sem("bu_ready"), sem("bu_read")
        w_turned, z_ready = sem("w_turned"), sem("z_ready")
        tab_prod, tab_half, tab_ready = sem("tab_prod"), sem("tab_half"), sem("tab_ready")
        prod_ready, y_done, c_step, fin_step = sem("prod_ready"), sem("y_done"), sem("c_step"), sem("fin_step")
        bias_ready, sc_ready, soft_step, exp_ready = sem("bias_ready"), sem("sc_ready"), sem("soft_step"), sem("exp_ready")
        p_ready, tr_ready, pt_ready, pv_done = sem("p_ready"), sem("tr_ready"), sem("pt_ready"), sem("pv_done")
        att_hi, att_lo = sem("att_hi"), sem("att_lo")
        gelu_done, ys_hi, ys_lo = sem("gelu_done"), sem("ys_hi"), sem("ys_lo")
        ga_sig, gs_sig, na_gated = sem("ga_sig"), sem("gs_sig"), sem("na_gated")
        glu_sig, glu_y, glu_hi, glu_lo = (sem(n) for n in ("glu_sig", "glu_y", "glu_hi", "glu_lo"))
        so_gated, mix_ready, mix_hi, mix_lo = sem("so_gated"), sem("mix_ready"), sem("mix_hi"), sem("mix_lo")
        xtok_landed, ln1_landed, ln2_landed = sem("xtok_landed"), sem("ln1_landed"), sem("ln2_landed")
        stat_ready, var_ready, sd_ready, ln_step, norm_ready = (
            sem(n) for n in ("stat_ready", "var_ready", "sd_ready", "ln_step", "norm_ready"))
        hT_psum, hT_f32, hT_hi, hT_lo, h_step = (sem(n) for n in ("hT_psum", "hT_f32", "hT_hi", "hT_lo", "h_step"))
        g_silu, mid_ready, mid_hi, mid_lo = (sem(n) for n in ("g_silu", "mid_ready", "mid_hi", "mid_lo"))
        ln2_norm, ln2_gain, ln2_out, stored = sem("ln2_norm"), sem("ln2_gain"), sem("ln2_out"), sem("stored")

        block = ctx.enter_context(nc.Block())

        def bank_of(n):
            if n < N_WO:
                return n % 3
            if n < N_FF:
                return (3 + n - N_WO) % 8
            if n < N_DN:
                return (n - N_FF) % 6
            return (6 + n - N_DN) % 8

        def bank_before(n):
            return next((o for o in range(n - 1, -1, -1) if bank_of(o) == bank_of(n)), None)

        def taken(n):
            if n < N_LOOP:
                return uv_copied, n + 1
            if n < N_NA1:
                return loop_copied, n - N_LOOP + 1
            if n < N_GLU:
                return na_gated, n - N_NA1 + 1
            if n < N_NA2:
                return glu_sig, n - N_GLU + 1
            if n < N_S5O:
                return na_gated, n - N_NA2 + 9
            if n < N_WO:
                return so_gated, n - N_S5O + 1
            if n < N_FF:
                return res_added, n - N_WO + 1
            if n < N_DN:
                return (g_silu, mid_ready)[(n - N_FF) % 2], (n - N_FF) // 2 + 1
            return res_added, 8 + n - N_DN + 1

        @block.sync
        def _(sp):
            def load(m, c):
                if not (isinstance(m, int) and 12 * m + c < RAW):
                    sp.wait_ge(lo_ready, 12 * m + (c - RAW + 1))
                sp.dma_start(raw[:, c % RAW, :], wstream[bass.ds(12 * m + c, 1), :, :].rearrange("o p n -> p (o n)")
                             ).then_inc(raw_landed[c % RAW], 16)

            def stage(f, p):
                sp.dma_start(pk[:, p, :], pack[bass.ds(f, 1), :, :].rearrange("o p n -> p (o n)")).then_inc(pk_staged[p], 16)
                sp.dma_start(base[:, p, :, :], base_dram[:, bass.ds(TILES * f, TILES), :]).then_inc(base_staged[p], 16)
                sp.dma_start(vcur[:, p, :, :], v_dram[:, bass.ds(DH * f, DH)].rearrange("(t p) n -> p t n", p=P)
                             ).then_inc(v_staged[p], 16)
                sp.dma_start(bm[:, p, :, :], bias[bass.ds(f, 1), :, :].rearrange("o p (t n) -> p (o t) n", t=TT)
                             ).then_inc(bias_staged[p], 16)

            for i in range(4):
                sp.dma_start(xraw[:, 4 * i:4 * i + 4, :], xT[:, 4 * i:4 * i + 4, :]).then_inc(x_landed[i], 16)
                if i == 0:
                    for c in range(RAW):
                        load(0, c)
            sp.dma_start(col[:, :], cols).then_inc(col_landed, 16)
            for c in range(RAW, 12):
                load(0, c)
            for f in range(2):
                sp.dma_start(pk[:, f, :], pack[f, :, :]).then_inc(pk_staged[f], 16)
                sp.dma_start(bm[:, f, :, :], bias[f, :, :].rearrange("p (t n) -> p t n", t=TT)).then_inc(bias_staged[f], 16)
            for c in range(12, H_LOOP):
                load(0, c)

            def passes(k, last):
                for p in range(2):
                    for j in range(PER_F):
                        if j == 10 and not (p == 0 and isinstance(k, int) and k == 0) and not (p == 1 and last):
                            sp.wait_ge(fin_step, 2 * (2 * k + p))
                            sp.wait_ge(att_lo, 2 * k + p)
                            stage(2 * k + p + 1, 1 - p)
                        load(2 * k, H_LOOP + PER_F * p + j)

            sp.wait_ge(base_stored, 16)
            passes(0, False)
            with sp.Fori(1, HEADS // 2 - 1) as k:
                passes(k, False)
            passes(HEADS // 2 - 1, True)

            for c in range(H_NA1, H_S5O + KD):
                if c == H_S5O:
                    sp.wait_ge(ys_lo, 1)
                    sp.dma_start(hp[:, :, :], xtok.rearrange("(t p) n -> p t n", p=P)).then_inc(xtok_landed, 16)
                    for r in range(2):
                        sp.dma_start(lnrow[:, r, :], lnrows[r:r + 1, :].to_broadcast([P, D])).then_inc(ln1_landed, 16)
                load(0, c)
            for c in range(H_WO, H_FF + 4):
                load(0, c)
            n0 = (H_END - H_FF - 4) // 12
            c0 = H_FF + 4
            with sp.Fori(0, n0 // 2) as m:
                for c in range(c0, c0 + 12):
                    load(m, c)
            sp.wait_ge(h_step, 4)
            for r in range(2):
                sp.dma_start(lnrow[:, r, :], lnrows[2 + r:3 + r, :].to_broadcast([P, D])).then_inc(ln2_landed, 16)
            with sp.Fori(n0 // 2, n0) as m:
                for c in range(c0, c0 + 12):
                    load(m, c)
            for c in range(c0 + 12 * n0, H_END):
                load(0, c)
            for i in range(4):
                sp.wait_ge(ln2_out, i + 1)
                t, h = i // 2, i % 2
                sp.dma_start(out[t * P:(t + 1) * P, h * 1024:(h + 1) * 1024], hp[:, t, h * 1024:(h + 1) * 1024]
                             ).then_inc(stored, 16)
            sp.wait_ge(stored, 64)

        @block.gpsimd
        def _(pool):
            pool.memset(ident[:, :], 0.0).then_inc(const_step, 1)
            pool.memset(mask[:, :], 0.0).then_inc(const_step, 1)
            pool.memset(eps1[:, :], EPS).then_inc(const_step, 1)
            pool.wait_ge(const_step, 3)
            pool.affine_select(out=ident[:, :], in_=ident[:, :], compare_op=ALU.not_equal, fill=1.0, base=0,
                               pattern=[[-1, P]], channel_multiplier=1).then_inc(const_step, 1)
            for hf in range(2):
                lo = mask[64 * hf:64 * hf + 64, 0:GRID_W - WIN]
                hi = mask[64 * hf:64 * hf + 64, WIN:GRID_W]
                pool.wait_ge(const_step, 4 + 2 * hf)
                pool.affine_select(out=lo, in_=lo, compare_op=ALU.is_ge, fill=-1e30, base=WIN // 2,
                                   pattern=[[1, GRID_W - WIN]], channel_multiplier=-1).then_inc(const_step, 1)
                pool.wait_ge(const_step, 5 + 2 * hf)
                pool.affine_select(out=hi, in_=hi, compare_op=ALU.is_gt, fill=-1e30, base=WIN // 2 - WIN,
                                   pattern=[[-1, GRID_W - WIN]], channel_multiplier=1).then_inc(const_step, 1)
            pool.wait_ge(const_step, 8)

            pool.dma_start(scratch[:, 0:3, :], params).then_inc(par_landed, 16)
            pool.wait_ge(par_done, 1)
            done = [0]

            def step(ins):
                ins.then_inc(tab_step, 1)
                done[0] += 1
                pool.wait_ge(tab_step, done[0])

            def tt(o, a, b, op):
                step(pool.tensor_tensor(o, a, b, op))

            q1 = [scratch[:, 22 + i, :].rearrange("p (g o) -> p g o", o=1) for i in range(2)]
            big = [scratch[:, 24 + 4 * i:28 + 4 * i, :].rearrange("p a b -> p (a b)") for i in range(2)]

            def cmul(ore, oim, are, aim, bre, bim, n):
                t1, t2 = (b[:, 0:GROUPS * min(n, 4)].rearrange("p (g n) -> p g n", n=min(n, 4)) for b in big)
                for s in range(0, n, 4):
                    e = min(n, s + 4)
                    sl = lambda a: a[:, :, s:e]
                    bb = [b.to_broadcast([P, GROUPS, e - s]) for b in (bre, bim)]
                    tt(t1, sl(are), bb[0], ALU.mult)
                    tt(t2, sl(aim), bb[1], ALU.mult)
                    tt(sl(ore), t1, t2, ALU.subtract)
                    tt(t1, sl(are), bb[1], ALU.mult)
                    tt(t2, sl(aim), bb[0], ALU.mult)
                    tt(sl(oim), t1, t2, ALU.add)

            def square():
                t1 = big[0][:, 0:GROUPS].rearrange("p (g o) -> p g o", o=1)
                t2 = big[1][:, 0:GROUPS].rearrange("p (g o) -> p g o", o=1)
                tt(t1, q1[1], q1[1], ALU.mult)
                tt(t2, q1[0], q1[1], ALU.mult)
                tt(t2, t2, t2, ALU.add)
                tt(q1[0], q1[0], q1[0], ALU.mult)
                tt(q1[0], q1[0], t1, ALU.subtract)
                step(pool.tensor_copy(q1[1], t2))

            bc = base_all[:, :, O_B:O_B + BT]
            bs = base_all[:, :, O_B + BT:O_B + 2 * BT]
            ac = base_all[:, :, O_A + AT:O_A + 2 * AT]
            as_ = base_all[:, :, O_A + 2 * AT:O_A + 3 * AT]
            ans = base_all[:, :, O_A:O_A + AT]
            step(pool.tensor_copy(q1[0], bc[:, :, 1:2]))
            step(pool.tensor_copy(q1[1], bs[:, :, 1:2]))
            n = 2
            while n < BT:
                square()
                cmul(bc[:, :, n:2 * n], bs[:, :, n:2 * n], bc[:, :, 0:n], bs[:, :, 0:n], q1[0], q1[1], n)
                n *= 2
            square()
            n = 1
            while n < AT:
                cmul(ac[:, :, n:2 * n], as_[:, :, n:2 * n], ac[:, :, 0:n], as_[:, :, 0:n], q1[0], q1[1], n)
                n *= 2
                if n < AT:
                    square()
            step(pool.tensor_scalar(ans, as_, -1.0, None, ALU.mult))
            pool.dma_start(base_dram, base_all[:, :, :]).then_inc(base_stored, 16)
            for f in range(2):
                step(pool.tensor_copy(base[:, f, :, :], base_all[:, TILES * f:TILES * f + TILES, :]))

            def table(f, p, i):
                s = TILES * f + i
                row = base[:, p, i, :]
                a = [row[:, O_A + AT * j:O_A + AT * j + 2 * AT].rearrange("p (c a o) -> p c a o", c=2, o=1)
                     .to_broadcast([P, 2, AT, BT]) for j in (1, 0)]
                for j in range(2):
                    b = row[:, O_B + BT * j:O_B + BT * j + BT].rearrange("p (c a b) -> p c a b", c=1, a=1)
                    pool.tensor_tensor(tt12[:, j, :, :].rearrange("p c (a b) -> p c a b", b=BT), a[j],
                                       b.to_broadcast([P, 2, AT, BT]), ALU.mult).then_inc(tab_prod, 1)
                pool.wait_ge(tab_prod, 2 * s + 2)
                pool.tensor_tensor(E[:, i % 4, :, P:T], tt12[:, 0, :, :], tt12[:, 1, :, :], ALU.add).then_inc(tab_half, 1)
                pool.wait_ge(tab_half, s + 1)

            def products(f, p, i):
                s = TILES * f + i
                pool.wait_ge(z_ready, 2 * s + 2)
                if i >= 4 or not (isinstance(f, int) and f == 0):
                    pool.wait_ge(y_done, 2 * f + i // 4)
                zc, e, o = z[:, i % 2, :, :], E[:, i % 4, :, :], prod[:, i % 4, :, :]
                for j in range(2):
                    pool.tensor_tensor(o[:, 2 * j:2 * j + 2, :], zc, e[:, j:j + 1, :].to_broadcast([P, 2, T]), ALU.mult
                                       ).then_inc(prod_ready, 1)
                pool.wait_ge(prod_ready, 2 * s + 2)

            def c_matrices(f, p):
                c = pk[:, p, 512:512 + 2 * TILES * 32].rearrange("p (i r n) -> p i r n", i=TILES, r=2)
                kr, ki, nki = (base[:, p, :, o:o + 1].to_broadcast([P, TILES, 32]) for o in (O_KR, O_KI, O_NKI))
                t1, t2 = ctmp[:, 0, :, :], ctmp[:, 1, :, :]
                n = 7 * f
                pool.tensor_tensor(t1, c[:, :, 0, :], kr, ALU.mult).then_inc(c_step, 1)
                pool.tensor_tensor(t2, c[:, :, 1, :], ki, ALU.mult).then_inc(c_step, 1)
                pool.wait_ge(c_step, n + 2)
                pool.tensor_tensor(cmat[:, p, :, 0, :], t1, t2, ALU.subtract).then_inc(c_step, 1)
                pool.tensor_tensor(cmat[:, p, :, 2, :], t2, t1, ALU.subtract).then_inc(c_step, 1)
                pool.wait_ge(c_step, n + 4)
                pool.tensor_tensor(t1, c[:, :, 0, :], nki, ALU.mult).then_inc(c_step, 1)
                pool.tensor_tensor(t2, c[:, :, 1, :], kr, ALU.mult).then_inc(c_step, 1)
                pool.wait_ge(c_step, n + 6)
                pool.tensor_tensor(cmat[:, p, :, 1, :], t1, t2, ALU.subtract).then_inc(c_step, 1)
                pool.wait_ge(c_step, n + 7)

            def one_pass(k, p):
                f = 2 * k + p
                pool.wait_ge(pk_staged[p], 16 * k + 16)
                if not (isinstance(f, int) and f < 2):
                    pool.wait_ge(base_staged[p], 16 * k)
                if not (isinstance(f, int) and f < 2):
                    pool.wait_ge(fin_step, 2 * f - 2)
                table(f, p, 0)
                table(f, p, 1)
                c_matrices(f, p)
                pool.wait_ge(bias_staged[p], 16 * k + 16)
                b = bm[:, p, :, :].rearrange("p t (r c) -> p (t r) c", c=GRID_W)
                pool.tensor_tensor(b, b, mask[:, :].rearrange("p (o c) -> p o c", o=1).to_broadcast([P, TT * ROWS, GRID_W]),
                                   ALU.add).then_inc(bias_ready, 1)
                for i in range(TILES):
                    if i + 2 < TILES:
                        table(f, p, i + 2)
                    products(f, p, i)

            one_pass(0, 0)
            one_pass(0, 1)
            with pool.Fori(1, HEADS // 2) as k:
                one_pass(k, 0)
                one_pass(k, 1)

            pool.wait_ge(ln1_landed, 32)
            pool.wait_ge(hT_psum, 8)
            for t in range(TT):
                pool.tensor_tensor(hp[:, t, :], hp[:, t, :], lnrow[:, 0, :], ALU.mult).then_inc(h_step, 1)
                pool.wait_ge(h_step, 2 * t + 1)
                pool.tensor_tensor(hp[:, t, :], hp[:, t, :], lnrow[:, 1, :], ALU.add).then_inc(h_step, 1)

        @block.scalar
        def _(act):
            def split_hi(m, c):
                act.wait_ge(raw_landed[c % RAW], 48 * m + 16 * (c // RAW + 1))
                if not (isinstance(m, int) and 12 * m + c < SPL):
                    act.wait_ge(w_used, 12 * m + (c - SPL + 1))
                act.activation(whi[:, c % SPL, :], raw[:, c % RAW, :], ACT.Copy).then_inc(hi_ready, 1)

            def store_v(b):
                act.wait_ge(uv_copied, KS + 2 * b + 2)
                act.dma_start(v_dram[:, 512 * b:512 * b + 512].rearrange("(t p) n -> p t n", p=P), vout[:, :, :]
                              ).then_inc(v_stored[b], 16)

            for i in range(4):
                act.wait_ge(x_landed[i], 16)
                act.activation(act16[:, 4 * i:4 * i + 4, 0, :], xraw[:, 4 * i:4 * i + 4, :], ACT.Copy).then_inc(x_hi, 1)
                if i == 0:
                    split_hi(0, 0)
                    split_hi(0, 1)
            for c in range(2, H_LOOP):
                split_hi(0, c)
                if c == H_V + 12:
                    store_v(0)

            def stage_u(k, p):
                f = 2 * k + p
                if isinstance(f, int) and f == 0:
                    act.wait_ge(uv_copied, KS)
                if not (isinstance(f, int) and f < 2):
                    act.wait_ge(bu_ready, TILES * f - TILES)
                src = u[:, bass.ds(f, 1), :]
                act.activation(ucur[:, p, 0:1, :], src, ACT.Copy).then_inc(ucur_ready, 1)
                act.wait_ge(ucur_ready, 2 * f + 1)
                act.activation(ucur[:, p, 1, :], ucur[:, p, 0, ::-1], ACT.Copy).then_inc(ucur_ready, 1)

            def stage_v01():
                for b in range(2):
                    act.wait_ge(v_stored[b], 16)
                for f in range(2):
                    act.dma_start(vcur[:, f, :, :], v_dram[:, DH * f:DH * f + DH].rearrange("(t p) n -> p t n", p=P)
                                  ).then_inc(v_staged[f], 16)

            def table_rev(k, p, i):
                s = TILES * (2 * k + p) + i
                act.wait_ge(tab_half, s + 1)
                act.activation(E[:, i % 4, 0, 0:P], E[:, i % 4, 0, T - 1:P - 1:-1], ACT.Copy).then_inc(tab_ready, 1)
                act.activation(E[:, i % 4, 1, 0:P], E[:, i % 4, 1, T - 1:P - 1:-1], ACT.Copy, scale=-1.0).then_inc(tab_ready, 1)

            def softmax_exp(k, p):
                f = 2 * k + p
                act.wait_ge(soft_step, 3 * f + 3)
                for t in range(TT):
                    act.activation(S[:, t, :], S[:, t, :], ACT.Exp, bias=sm[:, 1, t:t + 1],
                                   accum_out=sm[:, 2, t:t + 1]).then_inc(exp_ready, 1)

            def pt_copy(f):
                act.wait_ge(tr_ready, f + 1)
                if not (isinstance(f, int) and f == 0):
                    act.wait_ge(pv_done, f)
                act.activation(PT[:, :, :].rearrange("p t n -> p (t n)"), ps[TB][:, :], ACT.Copy).then_inc(pt_ready, 1)

            def attn_hi(f):
                act.wait_ge(pv_done, f + 1)
                act.activation(act8a[:, bass.ds(f, 1), 0, :], ps[AB][:, 0:T].rearrange("p (o n) -> p o n", o=1), ACT.Copy
                               ).then_inc(att_hi, 1)

            def loop_copy(k, p, o):
                f = 2 * k + p
                act.wait_ge(w_used, PER_F * f + (H_LOOP + 2 * o + 2))
                src = ps[bank_of(N_LOOP + o)][:, 0:T].rearrange("p (o n) -> p o n", o=1)
                if o < 2:
                    if not (isinstance(f, int) and f < 2):
                        act.wait_ge(sc_ready, f - 1)
                    dst = qk[:, p, o:o + 1, :]
                else:
                    g = ga if o < 4 else gs
                    dst = g[:, bass.ds(2 * f + o % 2, 1), :]
                act.activation(dst, src, ACT.Copy).then_inc(loop_copied, 1)

            def one_pass(k, p, first):
                c0 = H_LOOP + PER_F * p
                for j in range(PER_F):
                    split_hi(2 * k, c0 + j)
                    if j == 1 and not first:
                        loop_copy(*((k, 0) if p else (k - 1, 1)), 5)
                    if j >= 1 + LAG and (j - 1 - LAG) % 2 == 0:
                        loop_copy(k, p, (j - 1 - LAG) // 2)
                    if j == 0:
                        stage_u(k, p)
                    if j == 3 and first:
                        store_v(1)
                    if j == 7 and first:
                        stage_v01()
                    if j == 1 and not first:
                        pt_copy(2 * k + p - 1)
                    if j == 4 and not first:
                        attn_hi(2 * k + p - 1)
                    if j == 8:
                        softmax_exp(k, p)
                    for i in range(TILES):
                        if BU_SLOT[i] + LAG - 1 == j:
                            table_rev(k, p, i)

            one_pass(0, 0, True)
            one_pass(0, 1, False)
            with act.Fori(1, HEADS // 2) as k:
                one_pass(k, 0, False)
                one_pass(k, 1, False)

            act.wait_ge(col_landed, 16)
            loop_copy(HEADS // 2 - 1, 1, 5)
            pt_copy(HEADS - 1)
            for j in range(8):
                split_hi(0, H_NA1 + j)
                if j == 0:
                    attn_hi(HEADS - 1)
                if j == 3:
                    act.wait_ge(fin_step, 2 * KS)
                    uf = u[:, :, :]
                    act.activation(uf, uf, ACT.Gelu_apprx_tanh).then_inc(gelu_done, 1)
                    act.wait_ge(gelu_done, 1)
                    act.activation(act8b[:, :, 0, :], uf, ACT.Copy).then_inc(ys_hi, 1)
                if j >= 4:
                    for t in (2 * (j - 4), 2 * (j - 4) + 1):
                        g = ga[:, t, :]
                        act.activation(g, g, ACT.Sigmoid, bias=col[:, t:t + 1]).then_inc(ga_sig, 1)

            def glu_act(t):
                act.wait_ge(w_used, H_GLU + t + 1)
                if t >= 4:
                    act.wait_ge(glu_y, t - 3)
                act.activation(ev2[:, t % 4, :], ps[bank_of(N_GLU + t)][:, 0:T], ACT.Sigmoid, bias=col[:, 32 + t:33 + t]
                               ).then_inc(glu_sig, 1)

            def glu_split(t):
                act.wait_ge(glu_y, t + 1)
                act.activation(act8a[:, t, 0, :], u[:, t, :], ACT.Copy).then_inc(glu_hi, 1)

            def mix_split(t):
                act.wait_ge(mix_ready, t + 1)
                act.activation(act16[:, t, 0, :], ga[:, t, :], ACT.Copy).then_inc(mix_hi, 1)

            for j in range(8):
                split_hi(0, H_GLU + j)
                t = 8 + j
                act.activation(ga[:, t, :], ga[:, t, :], ACT.Sigmoid, bias=col[:, t:t + 1]).then_inc(ga_sig, 1)
                if j >= LAG:
                    glu_act(j - LAG)
            for j in range(8):
                split_hi(0, H_NA2 + j)
                if j < LAG:
                    glu_act(8 - LAG + j)
                for t in (2 * j, 2 * j + 1):
                    act.activation(gs[:, t, :], gs[:, t, :], ACT.Sigmoid, bias=col[:, 16 + t:17 + t]).then_inc(gs_sig, 1)
            act.wait_ge(w_used, H_S5O)
            for t in range(KS):
                glu_split(t)
            for j in range(KD):
                split_hi(0, H_S5O + j)
                if j >= LAG + 1:
                    mix_split(j - LAG - 1)
            for j in range(32):
                split_hi(0, H_WO + j)
                if j < LAG + 1:
                    mix_split(KD - LAG - 1 + j)

            def sd(e):
                act.wait_ge(var_ready, 2 * e + 2)
                if e > 0:
                    act.wait_ge(ln_step, 2 * e)
                act.activation(lnm[:, :, 4:5], lnm[:, :, 1:2], ACT.Sqrt, bias=eps1[:, :]).then_inc(sd_ready, 1)

            split_hi(0, H_FF)
            split_hi(0, H_FF + 1)
            act.wait_ge(const_step, 3)
            sd(0)
            for g in range(8):
                act.wait_ge(hT_psum, g + 1)
                if g >= 2:
                    act.wait_ge(hT_lo, g - 1)
                for e in range(2):
                    t = 2 * g + e
                    act.activation(hT[:, g % 2, e, :], ps[4 + g % 4][:, e * T:(e + 1) * T], ACT.Identity,
                                   scale=col[:, 40 + t:41 + t], bias=col[:, 56 + t:57 + t]).then_inc(hT_f32, 1)
                act.wait_ge(hT_f32, 2 * g + 2)
                act.activation(act16[:, 2 * g:2 * g + 2, 0, :], hT[:, g % 2, :, :], ACT.Copy).then_inc(hT_hi, 1)

            def ff(m, i, skip, last_n=3):
                for i in range(last_n):
                    for q in range(4):
                        c = H_FF + 4 * i + q
                        if not (skip and i == 0 and q < 2):
                            split_hi(m, c)
                        if q == 2 and not (skip and i == 0):
                            n = 3 * m + i - 1
                            act.wait_ge(mid_ready, n + 1)
                            act.activation(mid[:, bass.ds(n, 1), 0, :], ev2[:, (i - 1) % 3:(i - 1) % 3 + 1, :], ACT.Copy
                                           ).then_inc(mid_hi, 1)
                        if q == 3:
                            act.wait_ge(w_used, 12 * m + (H_FF + 4 * i + 2))
                            if not (skip):
                                act.wait_ge(mid_ready, 3 * m + i - 2)
                            act.activation(ev[:, i, :], ps[bank_of(N_FF + 2 * i)][:, 0:T], ACT.Silu).then_inc(g_silu, 1)

            ff(0, 0, True)
            with act.Fori(1, KF // 3) as m:
                ff(m, 0, False)
            ff(KF // 3, 0, False, KF % 3)
            for c in range(4):
                split_hi(0, H_DN + c)
                if c == 2:
                    n = KF - 1
                    act.wait_ge(mid_ready, n + 1)
                    act.activation(mid[:, n, 0, :], ev2[:, n % 3, :], ACT.Copy).then_inc(mid_hi, 1)
            with act.Fori(0, (H_END - H_DN - 4) // 12) as m:
                for c in range(12):
                    split_hi(m, H_DN + 4 + c)
            sd(1)
            act.wait_ge(ln_step, 4)
            for t in range(TT):
                for h in range(2):
                    v = hp[:, t, h * 1024:(h + 1) * 1024]
                    act.activation(v, v, ACT.Identity, scale=lnm[:, t, 2:3], bias=lnm[:, t, 3:4]).then_inc(ln2_norm, 1)

        @block.vector
        def _(dve):
            def split_lo(m, c):
                dve.wait_ge(hi_ready, 12 * m + (c + 1))
                dve.tensor_tensor(wlo[:, c % SPL, :], raw[:, c % RAW, :], whi[:, c % SPL, :].bitcast(F32), ALU.subtract
                                  ).then_inc(lo_ready, 1)

            def low(o, full, hi, s):
                dve.tensor_tensor(o, full, hi.bitcast(F32), ALU.subtract).then_inc(s, 1)

            done = [0]

            def step(ins):
                ins.then_inc(par_step, 1)
                done[0] += 1
                dve.wait_ge(par_step, done[0])

            (ARE, AIM, DT, X, Y, NI, RR, EM, EX, H1, H2, SH, CH, CY, SY, KR, KI, T0, T1, T2, P0, P1) = (
                scratch[:, i, :] for i in range(22))

            def ts(o, a, s1, s2, *ops):
                step(dve.tensor_scalar(o, a, s1, s2, *ops))

            def tt(o, a, b, op):
                step(dve.tensor_tensor(o, a, b, op))

            def stt(o, a, s, b, op0, op1):
                step(dve.scalar_tensor_tensor(out=o, in0=a, scalar=s, in1=b, op0=op0, op1=op1))

            def expm1(o_em, o_ex, v):
                ts(T0, v, -87.0, 88.5, ALU.max, ALU.min)
                ts(NI, T0, 1.4426950408889634, MAGIC, ALU.mult, ALU.add)
                ts(NI, NI, MAGIC, None, ALU.subtract)
                stt(RR, NI, -LN2_HI, T0, ALU.mult, ALU.add)
                stt(RR, NI, -LN2_LO, RR, ALU.mult, ALU.add)
                ts(P0, RR, EXP_C[-1], None, ALU.mult)
                for c in EXP_C[-2::-1]:
                    stt(P0, P0, c, RR, ALU.add, ALU.mult)
                stt(P0, P0, 1.0, RR, ALU.add, ALU.mult)
                ts(T1.bitcast(I32), NI, 127.0, 8388608.0, ALU.add, ALU.mult)
                if o_em is not None:
                    ts(T2, T1, -1.0, None, ALU.add)
                    tt(o_em, P0, T1, ALU.mult)
                    tt(o_em, o_em, T2, ALU.add)
                stt(o_ex, P0, 1.0, T1, ALU.add, ALU.mult)

            def time_steps():
                expm1(None, DT, DT)

            def decays():
                tt(X, ARE, DT, ALU.mult)
                tt(Y, AIM, DT, ALU.mult)
                expm1(EM, EX, X)

            def sines():
                ts(NI, Y, 1.0 / (2 * np.pi), MAGIC, ALU.mult, ALU.add)
                ts(NI, NI, MAGIC, None, ALU.subtract)
                for c in TWO_PI:
                    stt(Y, NI, -c, Y, ALU.mult, ALU.add)
                ts(H1, Y, 0.5, None, ALU.mult)
                tt(H2, H1, H1, ALU.mult)
                ts(P0, H2, SIN_C[-1], None, ALU.mult)
                for c in SIN_C[-2::-1]:
                    stt(P0, P0, c, H2, ALU.add, ALU.mult)
                stt(SH, P0, 1.0, H1, ALU.add, ALU.mult)

            def cosines():
                ts(P0, H2, COS_C[-1], None, ALU.mult)
                for c in COS_C[-2::-1]:
                    stt(P0, P0, c, H2, ALU.add, ALU.mult)
                ts(CH, P0, 1.0, None, ALU.add)
                stt(SY, SH, 2.0, CH, ALU.mult, ALU.mult)
                stt(P1, SH, -2.0, SH, ALU.mult, ALU.mult)
                ts(CY, P1, 1.0, None, ALU.add)

            def gains():
                tt(H1, EM, CY, ALU.mult)
                tt(H1, H1, P1, ALU.add)
                tt(H2, EX, SY, ALU.mult)
                tt(T0, ARE, ARE, ALU.mult)
                tt(T1, AIM, AIM, ALU.mult)
                tt(T2, T0, T1, ALU.add)
                step(dve.reciprocal(T2, T2))
                tt(T0, H1, ARE, ALU.mult)
                tt(T1, H2, AIM, ALU.mult)
                tt(T0, T0, T1, ALU.add)
                tt(KR, T0, T2, ALU.mult)
                tt(T0, H2, ARE, ALU.mult)
                tt(T1, H1, AIM, ALU.mult)
                tt(T0, T0, T1, ALU.subtract)
                tt(KI, T0, T2, ALU.mult)

            def first_entries():
                def put(o, src):
                    step(dve.tensor_copy(base_all[:, :, o], src))

                put(O_R, EX)
                put(O_KR, KR)
                put(O_KI, KI)
                step(dve.tensor_scalar(base_all[:, :, O_NKI], KI, -1.0, None, ALU.mult))
                step(dve.memset(base_all[:, :, O_B], 1.0))
                step(dve.memset(base_all[:, :, O_B + BT], 0.0))
                put(O_B + 1, CY)
                put(O_B + BT + 1, SY)
                put(O_A + AT, CH)
                dve.tensor_copy(base_all[:, :, O_A + 2 * AT], SH).then_inc(par_done, 1)

            parts = {3: time_steps, 5: decays, 7: sines, 9: cosines, 11: gains, 13: first_entries}
            dve.wait_ge(x_hi, 1)
            for i in range(4):
                dve.wait_ge(x_hi, i + 1)
                low(act16[:, 4 * i:4 * i + 4, 1, :], xraw[:, 4 * i:4 * i + 4, :], act16[:, 4 * i:4 * i + 4, 0, :], x_lo)
                if i == 0:
                    split_lo(0, 0)
                    split_lo(0, 1)
            for j in range(2, H_V + LAG):
                split_lo(0, j)
                if j >= 1 + LAG and (j - 1 - LAG) % 2 == 0:
                    t = (j - 1 - LAG) // 2
                    dve.wait_ge(w_used, 2 * t + 2)
                    dve.tensor_copy(u[:, t, :], ps[bank_of(N_U + t)][:, 0:T]).then_inc(uv_copied, 1)
                if j in parts:
                    if j == 3:
                        dve.wait_ge(par_landed, 16)
                    parts[j]()
            for j in range(LAG, 16):
                split_lo(0, H_V + j)
                if j == 8 + LAG:
                    dve.wait_ge(w_used, H_V + 8)
                    for t in range(TT):
                        dve.tensor_copy(vout[:, t, :], ps[bank_of(N_V + t)][:, :]).then_inc(uv_copied, 1)

            def v_last():
                dve.wait_ge(w_used, H_V + 16)
                dve.wait_ge(v_stored[0], 16)
                for t in range(TT):
                    dve.tensor_copy(vout[:, t, :], ps[bank_of(N_V + 2 + t)][:, :]).then_inc(uv_copied, 1)

            def turn(k, p, i):
                s = TILES * (2 * k + p) + i
                dve.wait_ge(tab_ready, 2 * s + 2)
                dve.wait_ge(bu_ready, s + 1)
                bu = ps[BU0 + i % 2][:, :].rearrange("p (c n) -> p c n", c=2)
                for j in range(2):
                    dve.tensor_tensor(m12[:, j, :, :], bu, E[:, i % 4, j:j + 1, :].to_broadcast([P, 2, T]), ALU.mult
                                      ).then_inc(bu_read, 1)
                dve.wait_ge(bu_read, 2 * s + 2)
                if not (isinstance(s, int) and s == 0):
                    dve.wait_ge(z_ready, 2 * s)
                dve.tensor_tensor(wz[:, 0, :], m12[:, 0, 0, :], m12[:, 1, 1, :], ALU.add).then_inc(w_turned, 1)
                dve.tensor_tensor(wz[:, 1, :], m12[:, 0, 1, :], m12[:, 1, 0, :], ALU.subtract).then_inc(w_turned, 1)
                dve.wait_ge(w_turned, 2 * s + 2)
                if not (isinstance(s, int) and s < 2):
                    dve.wait_ge(prod_ready, 2 * s - 2)
                r = base[:, p, i, O_R:O_R + 1].to_broadcast([P, T])
                for j in range(2):
                    dve.tensor_tensor_scan(z[:, i % 2, j, :], r, wz[:, j, :], 0.0, ALU.mult, ALU.add).then_inc(z_ready, 1)

            def finish(f, p):
                dve.wait_ge(y_done, 2 * f + 2)
                uf = u[:, bass.ds(f, 1), :]
                ft = fin_t[:, :].rearrange("p (o n) -> p o n", o=1)
                dve.scalar_tensor_tensor(out=ft, in0=uf, scalar=pk[:, p, PACK - 1:PACK],
                                         in1=ps[YB][:, 0:T].rearrange("p (o n) -> p o n", o=1), op0=ALU.mult,
                                         op1=ALU.add).then_inc(fin_step, 1)
                dve.wait_ge(fin_step, 2 * f + 1)
                dve.tensor_tensor(uf, ft, ps[YB][:, T:2 * T][:, ::-1].rearrange("p (o n) -> p o n", o=1), ALU.add
                                  ).then_inc(fin_step, 1)

            def softmax_max(k, p):
                f = 2 * k + p
                dve.wait_ge(bias_ready, f + 1)
                dve.wait_ge(sc_ready, f + 1)
                if not (isinstance(f, int) and f == 0):
                    dve.wait_ge(tr_ready, f)
                dve.scalar_tensor_tensor(out=S[:, :, :], in0=ps[AB][:, :].rearrange("p (t n) -> p t n", t=TT), scalar=SCALE,
                                         in1=bm[:, p, :, :], op0=ALU.mult, op1=ALU.add).then_inc(soft_step, 1)
                dve.wait_ge(soft_step, 3 * f + 1)
                dve.tensor_reduce(sm[:, 0, :], S[:, :, :], AX.X, ALU.max).then_inc(soft_step, 1)
                dve.wait_ge(soft_step, 3 * f + 2)
                dve.tensor_scalar(sm[:, 1, :], sm[:, 0, :], -1.0, None, ALU.mult).then_inc(soft_step, 1)

            def softmax_norm(k, p):
                f = 2 * k + p
                dve.wait_ge(exp_ready, 2 * f + 2)
                dve.reciprocal(sm[:, 3, :], sm[:, 2, :]).then_inc(p_ready, 1)
                dve.wait_ge(p_ready, 3 * f + 1)
                for t in range(TT):
                    dve.tensor_scalar(S[:, t, :], S[:, t, :], sm[:, 3, t:t + 1], None, ALU.mult).then_inc(p_ready, 1)

            def attn_low(f):
                dve.wait_ge(att_hi, f + 1)
                low(act8a[:, bass.ds(f, 1), 1, :], ps[AB][:, 0:T].rearrange("p (o n) -> p o n", o=1),
                    act8a[:, bass.ds(f, 1), 0, :], att_lo)

            def one_pass(k, p, first):
                c0 = H_LOOP + PER_F * p
                for j in range(PER_F):
                    split_lo(2 * k, c0 + j)
                    if j == 1 and first:
                        v_last()
                    if j == 4 and not first:
                        finish(2 * k + p - 1, 1 - p)
                    if j == 5 and not first:
                        attn_low(2 * k + p - 1)
                    if j == 8:
                        softmax_max(k, p)
                    if j == 10:
                        softmax_norm(k, p)
                    for i in range(TILES):
                        if BU_SLOT[i] + LAG == j:
                            turn(k, p, i)

            one_pass(0, 0, True)
            one_pass(0, 1, False)
            with dve.Fori(1, HEADS // 2) as k:
                one_pass(k, 0, False)
                one_pass(k, 1, False)

            def na_gate(t, h):
                dve.wait_ge(w_used, h + 1)
                dve.wait_ge(ga_sig, t + 1)
                dve.tensor_tensor(ga[:, t, :], ps[bank_of(N_NA1 + t if t < 8 else N_NA2 + t - 8)][:, 0:T], ga[:, t, :],
                                  ALU.mult).then_inc(na_gated, 1)

            for j in range(8):
                split_lo(0, H_NA1 + j)
                if j == 0:
                    attn_low(HEADS - 1)
                if j == 2:
                    finish(HEADS - 1, 1)
                if j == 4:
                    dve.wait_ge(ys_hi, 1)
                    low(act8b[:, :, 1, :], u[:, :, :], act8b[:, :, 0, :], ys_lo)
                if j >= LAG:
                    na_gate(j - LAG, H_NA1 + j - LAG)

            def glu_mult(t):
                dve.wait_ge(glu_sig, t + 1)
                dve.tensor_tensor(u[:, t, :], u[:, t, :], ev2[:, t % 4, :], ALU.mult).then_inc(glu_y, 1)

            for j in range(8):
                split_lo(0, H_GLU + j)
                if j < LAG:
                    na_gate(8 - LAG + j, H_GLU - LAG + j)
                if j >= LAG + 1:
                    glu_mult(j - LAG - 1)
            for j in range(8):
                split_lo(0, H_NA2 + j)
                if j >= LAG:
                    na_gate(8 + j - LAG, H_NA2 + j - LAG)
                if j < LAG + 1:
                    glu_mult(8 - LAG - 1 + j)
            for t in range(16 - LAG, 16):
                na_gate(t, H_NA2 + t - 8)
            for t in range(KS):
                dve.wait_ge(glu_hi, t + 1)
                low(act8a[:, t, 1, :], u[:, t, :], act8a[:, t, 0, :], glu_lo)

            def s5o_evac(t):
                dve.wait_ge(w_used, H_S5O + t + 1)
                dve.wait_ge(gs_sig, t + 1)
                dve.tensor_tensor(gs[:, t, :], ps[bank_of(N_S5O + t)][:, 0:T], gs[:, t, :], ALU.mult).then_inc(so_gated, 1)
                dve.wait_ge(so_gated, t + 1)
                dve.tensor_tensor(ga[:, t, :], gs[:, t, :], ga[:, t, :], ALU.add).then_inc(mix_ready, 1)

            def mix_low(t):
                dve.wait_ge(mix_hi, t + 1)
                low(act16[:, t, 1, :], ga[:, t, :], act16[:, t, 0, :], mix_lo)

            for j in range(KD):
                split_lo(0, H_S5O + j)
                if j >= LAG:
                    s5o_evac(j - LAG)
                if j >= LAG + 2:
                    mix_low(j - LAG - 2)

            def residual(n, h, t, b):
                dve.wait_ge(w_used, h + 1)
                v = hp[:, t, b * 512:(b + 1) * 512]
                dve.scalar_tensor_tensor(out=v, in0=v, scalar=ALPHA, in1=ps[bank_of(n)][:, :], op0=ALU.mult, op1=ALU.add
                                         ).then_inc(res_added, 1)
                dve.wait_ge(*taken(n))
                dve.bn_stats(stats[:, t, b, :], v).then_inc(stat_ready, 1)

            def moments(e):
                dve.wait_ge(stat_ready, 8 * (e + 1))
                for t in range(TT):
                    dve.bn_aggr(lnm[:, t, 0:2], stats[:, t, :, :].rearrange("p a b -> p (a b)")).then_inc(var_ready, 1)
                dve.wait_ge(sd_ready, e + 1)
                dve.reciprocal(lnm[:, :, 2:3], lnm[:, :, 4:5]).then_inc(ln_step, 1)
                dve.wait_ge(ln_step, 2 * e + 1)
                dve.scalar_tensor_tensor(out=lnm[:, :, 3:4], in0=lnm[:, :, 0:1], scalar=-1.0, in1=lnm[:, :, 2:3],
                                         op0=ALU.mult, op1=ALU.mult).then_inc(ln_step, 1)
                dve.wait_ge(ln_step, 2 * e + 2)

            for j in range(32):
                split_lo(0, H_WO + j)
                if j < LAG:
                    s5o_evac(KD - LAG + j)
                if j < LAG + 2:
                    mix_low(KD - LAG - 2 + j)
                if j == 4:
                    dve.wait_ge(xtok_landed, 16)
                if j % 8 == 1 and j > 8:
                    for t in range(TT):
                        b = j // 8 - 1
                        residual(N_WO + 2 * b + t, H_WO + 8 * b + 7, t, b)
            split_lo(0, H_FF)
            split_lo(0, H_FF + 1)
            for t in range(TT):
                residual(N_WO + 6 + t, H_WO + 31, t, 3)
            moments(0)
            for b in range(4):
                for t in range(TT):
                    v = hp[:, t, b * 512:(b + 1) * 512]
                    dve.tensor_scalar(v, v, lnm[:, t, 2:3], lnm[:, t, 3:4], ALU.mult, ALU.add).then_inc(norm_ready, 1)
            for g in range(8):
                dve.wait_ge(hT_hi, g + 1)
                low(act16[:, 2 * g:2 * g + 2, 1, :], hT[:, g % 2, :, :], act16[:, 2 * g:2 * g + 2, 0, :], hT_lo)

            def ff(m, skip, count=3):
                for i in range(count):
                    for q in range(4):
                        if not (skip and i == 0 and q < 2):
                            split_lo(m, H_FF + 4 * i + q)
                        if q == 1 and not (skip and i == 0):
                            up(3 * m + i - 1, m, i - 1)
                        if q == 3 and not (skip and i == 0):
                            mid_low(3 * m + i - 1, (i - 1) % 3)

            def up(n, m, i):
                dve.wait_ge(w_used, 12 * m + (H_FF + 4 * i + 4))
                dve.wait_ge(g_silu, n + 1)
                dve.tensor_tensor(ev2[:, i % 3, :], ps[bank_of(N_FF + (2 * i + 1) % 6)][:, 0:T], ev[:, i % 3, :], ALU.mult
                                  ).then_inc(mid_ready, 1)

            def mid_low(n, r):
                dve.wait_ge(mid_hi, n + 1)
                low(mid[:, bass.ds(n, 1), 1, :], ev2[:, r:r + 1, :], mid[:, bass.ds(n, 1), 0, :], mid_lo)

            ff(0, True)
            with dve.Fori(1, KF // 3) as m:
                ff(m, False)
            ff(KF // 3, False, KF % 3)

            def dn_evac(b):
                for t in range(TT):
                    residual(N_DN + 2 * b + t, H_DN + 22 * b + 21, t, b)

            for c in range(4 * (KF // 2)):
                split_lo(0, H_DN + c)
                if c == 1:
                    up(KF - 1, KF // 3, KF % 3 - 1)
                if c == 3:
                    mid_low(KF - 1, (KF - 1) % 3)
                    dve.wait_ge(h_step, 4)
                if c >= 24 and (c - 24) % 22 == 0:
                    dn_evac((c - 24) // 22)
            dn_evac(3)
            moments(1)
            dve.wait_ge(ln2_landed, 32)
            for i in range(4):
                t, h = i // 2, i % 2
                s = slice(h * 1024, (h + 1) * 1024)
                dve.wait_ge(ln2_norm, i + 1)
                dve.tensor_tensor(hp[:, t, s], hp[:, t, s], lnrow[:, 0, s], ALU.mult).then_inc(ln2_gain, 1)
                dve.wait_ge(ln2_gain, i + 1)
                dve.tensor_tensor(hp[:, t, s], hp[:, t, s], lnrow[:, 1, s], ALU.add).then_inc(ln2_out, 1)

        @block.tensor
        def _(pe):
            def wait_split(m, c):
                pe.wait_ge(lo_ready, 12 * m + (c + 1))

            def prod_a(m, c, act, k0, kn, bank, start, stop):
                s = c % SPL
                for i in range(kn):
                    hi, lo = (w[:, s, i * P:(i + 1) * P] for w in (whi, wlo))
                    pe.matmul(bank[:, 0:T], hi, act[:, k0 + i, 0, :], start=start and i == 0, stop=False)
                    pe.matmul(bank[:, 0:T], hi, act[:, k0 + i, 1, :], start=False, stop=False)
                    mm = pe.matmul(bank[:, 0:T], lo, act[:, k0 + i, 0, :], start=False, stop=stop and i == kn - 1)
                mm.then_inc(w_used, 1)

            def prod_b(c, act, k0, banks, start, stop):
                s = c % SPL
                for i in range(2):
                    hi, lo = (w[:, s, i * 512:(i + 1) * 512] for w in (whi, wlo))
                    for t in range(TT):
                        a = act[:, k0 + i, 0, t * P:(t + 1) * P]
                        b = act[:, k0 + i, 1, t * P:(t + 1) * P]
                        pe.matmul(banks[t][:, :], a, hi, start=start and i == 0, stop=False)
                        pe.matmul(banks[t][:, :], a, lo, start=False, stop=False)
                        mm = pe.matmul(banks[t][:, :], b, hi, start=False, stop=stop and i == 1)
                mm.then_inc(w_used, 1)

            def wait_bank(n):
                o = bank_before(n)
                if o is not None:
                    pe.wait_ge(*taken(o))

            for j in range(2 * KS):
                if j % 2 == 0:
                    wait_bank(N_U + j // 2)
                wait_split(0, j)
                for q in range(2 * (j % 2), 2 * (j % 2) + 2):
                    pe.wait_ge(x_lo, q + 1)
                prod_a(0, j, act16, 8 * (j % 2), 8, ps[bank_of(N_U + j // 2)], j % 2 == 0, j % 2 == 1)
            for j in range(16):
                n = N_V + 2 * (j // 8)
                if j % 8 == 0:
                    wait_bank(n)
                    wait_bank(n + 1)
                wait_split(0, H_V + j)
                prod_b(H_V + j, act16, 2 * (j % 8), [ps[bank_of(n)], ps[bank_of(n + 1)]], j % 8 == 0, j % 8 == 7)

            def s5_in(k, p, i):
                f = 2 * k + p
                s = TILES * f + i
                d, q = i // 4, i % 4
                if i == 0:
                    pe.wait_ge(pk_staged[p], 16 * k + 16)
                    pe.wait_ge(ucur_ready, 2 * f + 2)
                if not (isinstance(s, int) and s < 2):
                    pe.wait_ge(bu_read, 2 * s - 2)
                rows = slice(32 * q, 32 * q + 32)
                for c in range(2):
                    o = (2 * d + c) * P
                    mm = pe.matmul(ps[BU0 + i % 2][:, c * T:(c + 1) * T], pk[rows, p, o:o + P], ucur[rows, p, d, :],
                                   start=True, stop=True)
                mm.then_inc(bu_ready, 1)

            def s5_out(f, p, d):
                pe.wait_ge(prod_ready, 16 * f + (8 * d + 8))
                pe.wait_ge(c_step, 7 * f + 7)
                if d == 0 and not (isinstance(f, int) and f == 0):
                    pe.wait_ge(fin_step, 2 * f)
                for e in range(4):
                    for q in range(4):
                        mm = pe.matmul(ps[YB][32 * q:32 * q + 32, d * T:(d + 1) * T],
                                       cmat[:, p, 4 * d + q, (0, 1, 1, 2)[e], :], prod[:, q, e, :],
                                       start=e == 0, stop=e == 3)
                mm.then_inc(y_done, 1)

            def scores(k, p):
                f = 2 * k + p
                pe.wait_ge(loop_copied, 6 * f + 2)
                if not (isinstance(f, int) and f == 0):
                    pe.wait_ge(att_lo, f)
                for t in range(TT):
                    mm = pe.matmul(ps[AB][:, t * T:(t + 1) * T], qk[:, p, 0, t * P:(t + 1) * P], qk[:, p, 1, :],
                                   start=True, stop=True)
                mm.then_inc(sc_ready, 1)

            def transposes(k, p):
                f = 2 * k + p
                pe.wait_ge(p_ready, 3 * f + 3)
                if isinstance(f, int) and f == 0:
                    pe.wait_ge(const_step, 4)
                else:
                    pe.wait_ge(pt_ready, f)
                for b in range(TT):
                    for t in range(TT):
                        mm = pe.transpose(ps[TB][:, (b * TT + t) * P:(b * TT + t + 1) * P], S[:, t, b * P:(b + 1) * P],
                                          ident[:, :])
                mm.then_inc(tr_ready, 1)

            def attend(f, k, p):
                pe.wait_ge(pt_ready, f + 1)
                pe.wait_ge(v_staged[p], 16 * k + 16)
                for b in range(TT):
                    mm = pe.matmul(ps[AB][:, 0:T], vcur[:, p, b, :], PT[:, b, :], start=b == 0, stop=b == TT - 1)
                mm.then_inc(pv_done, 1)

            def before(k, p):
                return (2 * k, k, 0) if p else (2 * k - 1, k - 1, 1)

            def one_pass(k, p, first):
                for j in range(PER_F):
                    o = j // 2
                    n = N_LOOP + o
                    if j % 2 == 0:
                        if first and o < 3:
                            wait_bank(n)
                        else:
                            pe.wait_ge(loop_copied, 6 * (2 * k + p) + (o - 2))
                    c = H_LOOP + PER_F * p + j
                    wait_split(2 * k, c)
                    prod_a(2 * k, c, act16, 8 * (j % 2), 8, ps[bank_of(n)], j % 2 == 0, j % 2 == 1)
                    if not first:
                        f1, k1, p1 = before(k, p)
                        if j == 1:
                            s5_out(f1, p1, 1)
                        if j == 2:
                            attend(f1, k1, p1)
                    if j == 6:
                        scores(k, p)
                    if j == 8:
                        s5_out(2 * k + p, p, 0)
                    for i in range(TILES):
                        if BU_SLOT[i] == j:
                            s5_in(k, p, i)
                    if j == 11:
                        transposes(k, p)

            one_pass(0, 0, True)
            one_pass(0, 1, False)
            with pe.Fori(1, HEADS // 2) as k:
                one_pass(k, 0, False)
                one_pass(k, 1, False)

            s5_out(HEADS - 1, 1, 1)
            attend(HEADS - 1, HEADS // 2 - 1, 1)
            pe.wait_ge(att_lo, HEADS)
            for j in range(24):
                h, n = H_NA1 + j, N_NA1 + j
                if j == 8:
                    pe.wait_ge(ys_lo, 1)
                wait_bank(n)
                wait_split(0, h)
                prod_a(0, h, act8b if 8 <= j < 16 else act8a, 0, 8, ps[bank_of(n)], True, True)
            for j in range(KD):
                wait_bank(N_S5O + j)
                wait_split(0, H_S5O + j)
                if j == 0:
                    pe.wait_ge(glu_lo, KS)
                prod_a(0, H_S5O + j, act8a, 0, 8, ps[bank_of(N_S5O + j)], True, True)
            for j in range(32):
                n = N_WO + 2 * (j // 8)
                if j % 8 == 0:
                    wait_bank(n)
                    wait_bank(n + 1)
                wait_split(0, H_WO + j)
                if j < 8:
                    pe.wait_ge(mix_lo, 2 * j + 2)
                prod_b(H_WO + j, act16, 2 * (j % 8), [ps[bank_of(n)], ps[bank_of(n + 1)]], j % 8 == 0, j % 8 == 7)
            for g in range(8):
                if g % 2 == 0:
                    pe.wait_ge(norm_ready, g + 2)
                pe.wait_ge(res_added, 8)
                if g >= 4:
                    pe.wait_ge(hT_hi, g - 3)
                for e in range(2):
                    for t in range(TT):
                        mm = pe.transpose(ps[4 + g % 4][:, e * T + t * P:e * T + (t + 1) * P],
                                          hp[:, t, (2 * g + e) * P:(2 * g + e + 1) * P], ident[:, :])
                mm.then_inc(hT_psum, 1)
            pe.wait_ge(hT_lo, 8)

            def ff(m, first, count=3):
                for i in range(count):
                    for q in range(4):
                        n = N_FF + 2 * i + q // 2
                        if q % 2 == 0:
                            if first:
                                wait_bank(n)
                            else:
                                pe.wait_ge(g_silu if q == 0 else mid_ready, 3 * m + (i - 2))
                        wait_split(m, H_FF + 4 * i + q)
                        prod_a(m, H_FF + 4 * i + q, act16, 8 * (q % 2), 8, ps[bank_of(n)], q % 2 == 0, q % 2 == 1)

            ff(0, True)
            with pe.Fori(1, KF // 3) as m:
                ff(m, False)
            ff(KF // 3, False, KF % 3)
            for j in range(4 * (KF // 2)):
                b, i = divmod(j, KF // 2)
                n = N_DN + 2 * b
                if i == 0:
                    wait_bank(n)
                    wait_bank(n + 1)
                wait_split(0, H_DN + j)
                if b == 0:
                    pe.wait_ge(mid_lo, 2 * i + 2)
                prod_b(H_DN + j, mid, 2 * i, [ps[bank_of(n)], ps[bank_of(n + 1)]], i == 0, i == KF // 2 - 1)


def kernel(**inputs):
    import concourse.bacc as bacc
    from concourse.bass_utils import run_bass_kernel_spmd

    a = {n: np.asarray(v) for n, v in inputs.items()}
    w = a["w_in"][0]

    def kind_a(m):
        k, n = m.shape
        return m.reshape(k // 1024, 8, P, n // P, P).transpose(3, 0, 2, 1, 4).reshape(-1, P, HC)

    def kind_b(m):
        k, n = m.shape
        return m.reshape(k // 256, 2, P, n // 512, 512).transpose(3, 0, 2, 1, 4).reshape(-1, P, HC)

    q, k, v, u, g1, g2 = np.split(w, [NW, 2 * NW, 3 * NW, 3 * NW + SW, 3 * NW + SW + D], axis=1)
    qa, ka = kind_a(q).reshape(8, 2, P, HC), kind_a(k).reshape(8, 2, P, HC)
    g1a, g2a = kind_a(g1).reshape(8, 4, P, HC), kind_a(g2).reshape(8, 4, P, HC)
    loop = np.concatenate([qa, ka, g1a, g2a], axis=1).reshape(-1, P, HC)
    na = kind_a(a["w_na_out"][0])
    ff = np.concatenate([kind_a(a["w_ffn_gate"][0]).reshape(KF, 2, P, HC),
                         kind_a(a["w_ffn_up"][0]).reshape(KF, 2, P, HC)], axis=1).reshape(-1, P, HC)
    wstream = np.concatenate([kind_a(u), kind_b(v), loop, na[:8], kind_a(a["w_glu"][0]), na[8:],
                              kind_a(a["w_s5_out"][0]), kind_b(a["w_out"][0]), ff, kind_b(a["w_ffn_down"][0])])

    x = a["x"][0]
    xT = x.T.reshape(KD, P, T).transpose(1, 0, 2)

    def states(m):
        return m.reshape(2, KS, 4, 2, NS).transpose(3, 4, 1, 0, 2).reshape(P, GROUPS)

    log_dt = np.broadcast_to(a["s5_log_dt"][0][:, :, None], (2, GROUPS, NS))
    params = np.stack([states(a["s5_a_re"][0]), states(a["s5_a_im"][0]), states(log_dt)], axis=1)
    pack = np.zeros((KS, P, PACK), np.float32)
    for ri, name in enumerate(("s5_b_re", "s5_b_im")):
        b = a[name][0].reshape(2, KS, 4, 2, NS, GC)
        for g in range(2):
            dst = pack[:, :, 0:512].reshape(KS, 4, 2, GC, 2, 2, 2, NS)
            dst[:, :, g, :, :, ri, g, :] = b[:, :, :, g].transpose(1, 2, 4, 0, 3)
            pack[:, :, 0:512] = dst.reshape(KS, P, 512)
    for ri, name in enumerate(("s5_c_re", "s5_c_im")):
        c = a[name][0].reshape(2, KS, 4, 2, GC, NS)
        dst = pack[:, :, 512:1024].reshape(KS, 2, NS, 2, 4, 2, 2, GC)
        for g in range(2):
            dst[:, g, :, :, :, ri, g, :] = c[:, :, :, g].transpose(1, 4, 0, 2, 3)
        pack[:, :, 512:1024] = dst.reshape(KS, P, 512)
    pack[:, :, 1024] = a["s5_d"][0].reshape(KS, P)

    rpb = np.pad(a["na_rpb"][0], ((0, 0), (0, 0), (GRID_W - WIN, GRID_W - WIN)))
    slide = np.lib.stride_tricks.sliding_window_view(rpb, GRID_W, axis=2)[:, :, ::-1]
    bias = np.empty((HEADS, 2, GRID_W, TT, ROWS, GRID_W), np.float32)
    for t in range(TT):
        for rl in range(2):
            for i in range(ROWS):
                bias[:, rl, :, t, i, :] = slide[:, i - (2 * t + rl) + 7]
    bias = bias.reshape(HEADS, P, TT * T)

    cols = np.concatenate([a["b_gate"][0].reshape(32, P), a["b_glu"][0].reshape(8, P), a["ln1_g"][0].reshape(KD, P),
                           a["ln1_b"][0].reshape(KD, P)]).T
    lnrows = np.stack([a["ln1_g"][0], a["ln1_b"][0], a["ln2_g"][0], a["ln2_b"][0]])

    arrays = {"wstream": wstream, "xT": xT, "xtok": x, "pack": pack, "params": params, "bias": bias, "cols": cols,
              "lnrows": lnrows}
    arrays = {n: np.ascontiguousarray(v) for n, v in arrays.items()}
    nc = bacc.Bacc("TRN2", target_bir_lowering=False, num_devices=1)
    args = {n: nc.dram_tensor(n, v.shape, F32, kind="ExternalInput").ap() for n, v in arrays.items()}
    out = nc.dram_tensor("out", (T, D), F32, kind="ExternalOutput").ap()
    build(nc, out=out, **args)
    r = run_bass_kernel_spmd(nc, [arrays], core_ids=[0])
    return r.results[0]["out"].reshape(1, T, D)
```

```python
from contextlib import ExitStack

import numpy as np

import concourse.bass as bass
from concourse import mybir

F32 = mybir.dt.float32
F32R = mybir.dt.float32r
I32 = mybir.dt.int32
ALU = mybir.AluOpType
ACT = mybir.ActivationFunctionType
AX = mybir.AxisListType

P = 128
T = 256
TT = T // P
D = 2048
KD = D // P
HEADS = 8
DH = 128
GRID_W = 64
ROWS = T // GRID_W
WIN = 16
NW = HEADS * DH
SW = 1024
KS = SW // P
GROUPS = 64
GC = 16
NS = 64
DFF = 5632
KF = DFF // P
EPS = 1e-5
ALPHA = 2.0 ** 0.25
SCALE = DH ** -0.5

X_TO_W = {0: 0, 3: 1, 5: 2, 7: 3}
XP = 8
HC = 1024
RAW = 4
SPL = 3
PER_F = 12
TILES = 8
AT = 8
BT = 16
BASE = 3 * AT + 2 * BT + 4
O_A, O_B, O_R, O_KR, O_KI, O_NKI = 0, 3 * AT, BASE - 4, BASE - 3, BASE - 2, BASE - 1
PACK = 512 + 2 * TILES * 32 + 1

H_U = 0
H_V = H_U + 2 * KS
H_LOOP = H_V + 2 * KS
H_NA1 = H_LOOP + PER_F * HEADS
H_GLU = H_NA1 + 8
H_NA2 = H_GLU + 8
H_S5O = H_NA2 + 8
H_WO = H_S5O + KD
H_FF = H_WO + 4 * (KD // 2)
H_DN = H_FF + 4 * KF
H_END = H_DN + 4 * (KF // 2)

N_U, N_V, N_LOOP = 0, 8, 12
N_NA1 = N_LOOP + 6 * HEADS
N_GLU, N_NA2, N_S5O = N_NA1 + 8, N_NA1 + 16, N_NA1 + 24
N_WO = N_S5O + KD
N_FF = N_WO + 8
N_DN = N_FF + 2 * KF

U_ORDER = [(0, 0), (1, 0), (2, 0), (0, 1), (1, 1), (2, 1)] + [(n, h) for n in range(3, KS) for h in range(2)]
FF_ORDER = [(0, 0), (1, 0), (2, 0), (3, 0), (0, 1), (1, 1), (2, 1), (3, 1), (4, 0), (4, 1), (5, 0), (5, 1)]

LN2_DVE, LN2_POOL = [0, 1, 2, 4, 5], [3, 6, 7]
LN2_STORES = [0, 3, 1, 2, 6, 4, 7, 5]

EXP_C = [1 / 2, 1 / 6, 1 / 24, 1 / 120, 1 / 720, 1 / 5040]
SIN_C = [-1 / 6, 1 / 120, -1 / 5040, 1 / 362880, -1 / 39916800, 1 / 6227020800]
COS_C = [-1 / 2, 1 / 24, -1 / 720, 1 / 40320, -1 / 3628800, 1 / 479001600]
MAGIC = 12582912.0
LN2_HI, LN2_LO = 0.693359375, -2.12194440e-4
TWO_PI = [6.28125, 0.0019340515136718750, 1.2556659146753e-06]

BU_SLOT = [0, 1, 3, 4, 5, 7, 8, 9]
LAG = 2


def build(nc, wstream, xT, xtok, pack, params, bias, cols, lnrows, out):
    ctx = ExitStack()
    with ctx:
        B0 = (nc.sbuf_base + 63) // 32 * 32

        def at(name, shape, dt, kb):
            return nc.alloc_sbuf_tensor_at(name, shape, dt, offset=B0 + int(kb * 1024))

        def sem(name):
            return ctx.enter_context(nc.semaphore(name))

        raw = at("raw", [P, RAW, HC], F32, 0)
        whi = at("whi", [P, SPL, HC], F32R, 16)
        wlo = at("wlo", [P, SPL, HC], F32R, 28)
        act16 = at("act16", [P, KD, 2, T], F32R, 40)
        ident = at("ident", [P, P], F32, 72)
        mask = at("mask", [P, GRID_W], F32, 72.5)
        col = at("col", [P, 72], F32, 72.75)
        stats = at("stats", [P, TT, 4, 6], F32, 73.125)
        lnm = at("lnm", [P, TT, 5], F32, 73.375)
        eps1 = at("eps1", [P, 1], F32, 73.5)
        act8a = at("act8a", [P, KS, 2, T], F32R, 74)
        u = at("u", [P, KS, T], F32, 90)
        ga = at("ga", [P, KD, T], F32, 98)
        gs = at("gs", [P, KD, T], F32, 114)
        xraw = at("xraw", [P, KD, T], F32, 98)
        base_all = at("base_all", [P, GROUPS, BASE], F32, 114)
        scratch = at("scratch", [P, 32, GROUPS], F32, 185)
        vout = at("vout", [P, TT, 512], F32, 108)
        base = at("base", [P, 2, TILES, BASE], F32, 130)
        pk = at("pk", [P, 2, PACK], F32, 133.75)
        cmat = at("cmat", [P, 2, TILES, 3, 32], F32, 142)
        ctmp = at("ctmp", [P, 2, TILES, 32], F32, 148)
        ucur = at("ucur", [P, 2, 2, T], F32, 150)
        vcur = at("vcur", [P, 2, TT, DH], F32, 154)
        qk = at("qk", [P, 2, 2, T], F32, 156)
        bm = at("bm", [P, 2, TT, T], F32, 160)
        S = at("S", [P, TT, T], F32, 164)
        PT = at("PT", [P, TT, T], F32, 166)
        sm = at("sm", [P, 4, TT], F32, 168)
        fin_t = at("fin_t", [P, T], F32, 204.5)
        E = at("E", [P, 4, 2, T], F32, 168.5)
        tt12 = at("tt12", [P, 2, 2, P], F32, 176.5)
        m12 = at("m12", [P, 2, 2, T], F32, 178.5)
        wz = at("wz", [P, 2, T], F32, 182.5)
        z = at("z", [P, 2, 2, T], F32, 184.5)
        prod = at("prod", [P, 4, 4, T], F32, 188.5)
        act8b = at("act8b", [P, KS, 2, T], F32R, 130)
        mid = at("mid", [P, KF, 2, T], F32R, 74)
        hp = at("hp", [P, TT, D], F32, 162)
        lnrow = at("lnrow", [P, 2, D], F32, 178)
        ev = at("ev", [P, 4, T], F32, 194)
        ev2 = at("ev2", [P, 4, T], F32, 198)
        hT = at("hT", [P, 2, 2, T], F32, 202)

        ps = [ctx.enter_context(nc.psum_tensor(f"bank{i}", [P, 512], F32)) for i in range(8)]
        BU0, YB, AB, TB = 3, 5, 6, 7

        base_dram = nc.dram_tensor("base_dram", [P, GROUPS, BASE], F32, kind="Internal").ap()
        v_dram = nc.dram_tensor("v_dram", [T, NW], F32, kind="Internal").ap()

        raw_landed = [sem(f"raw_landed{i}") for i in range(RAW)]
        hi_ready, lo_ready, w_used = sem("hi_ready"), sem("lo_ready"), sem("w_used")
        uv_copied, loop_copied, res_added = sem("uv_copied"), sem("loop_copied"), sem("res_added")
        x_landed = [sem(f"x_landed{i}") for i in range(XP)]
        x_hi, x_lo = sem("x_hi"), sem("x_lo")
        col_landed, par_landed = sem("col_landed"), sem("par_landed")
        const_step = sem("const_step")
        par_step, par_done, tab_step, base_stored = sem("par_step"), sem("par_done"), sem("tab_step"), sem("base_stored")
        v_stored = [sem("v_stored0"), sem("v_stored1")]
        pk_staged = [sem("pk_staged0"), sem("pk_staged1")]
        base_staged = [sem("base_staged0"), sem("base_staged1")]
        v_staged = [sem("v_staged0"), sem("v_staged1")]
        bias_staged = [sem("bias_staged0"), sem("bias_staged1")]
        ucur_ready, bu_ready, bu_read = sem("ucur_ready"), sem("bu_ready"), sem("bu_read")
        w_turned, z_ready = sem("w_turned"), sem("z_ready")
        tab_prod, tab_half, tab_ready = sem("tab_prod"), sem("tab_half"), sem("tab_ready")
        prod_ready, y_done, c_step, fin_step = sem("prod_ready"), sem("y_done"), sem("c_step"), sem("fin_step")
        bias_ready, sc_ready, soft_step, exp_ready = sem("bias_ready"), sem("sc_ready"), sem("soft_step"), sem("exp_ready")
        p_ready, tr_ready, pt_ready, pv_done = sem("p_ready"), sem("tr_ready"), sem("pt_ready"), sem("pv_done")
        att_hi, att_lo = sem("att_hi"), sem("att_lo")
        gelu_done, ys_hi, ys_lo = sem("gelu_done"), sem("ys_hi"), sem("ys_lo")
        ga_sig, gs_sig, na_gated = sem("ga_sig"), sem("gs_sig"), sem("na_gated")
        glu_sig, glu_y, glu_hi, glu_lo = (sem(n) for n in ("glu_sig", "glu_y", "glu_hi", "glu_lo"))
        so_gated, mix_ready, mix_hi, mix_lo = sem("so_gated"), sem("mix_ready"), sem("mix_hi"), sem("mix_lo")
        xtok_landed, ln1_landed, ln2_landed = sem("xtok_landed"), sem("ln1_landed"), sem("ln2_landed")
        stat_ready, var_ready, sd_ready, ln_step, norm_ready = (
            sem(n) for n in ("stat_ready", "var_ready", "sd_ready", "ln_step", "norm_ready"))
        hT_psum, hT_f32, hT_hi, hT_lo, h_step = (sem(n) for n in ("hT_psum", "hT_f32", "hT_hi", "hT_lo", "h_step"))
        g_silu, mid_ready, mid_hi, mid_lo = (sem(n) for n in ("g_silu", "mid_ready", "mid_hi", "mid_lo"))
        ln2_norm, ln2_gain, ln2_mul = sem("ln2_norm"), sem("ln2_gain"), sem("ln2_mul")
        ln2_dve, ln2_pool, stored = sem("ln2_dve"), sem("ln2_pool"), sem("stored")

        block = ctx.enter_context(nc.Block())

        def bank_of(n):
            if n < N_WO:
                return n % 3
            if n < N_FF:
                return (3 + n - N_WO) % 8
            if n < N_DN:
                return (n - N_FF) % 6
            return (6 + n - N_DN) % 8

        def bank_before(n):
            return next((o for o in range(n - 1, -1, -1) if bank_of(o) == bank_of(n)), None)

        def taken(n):
            if n < N_LOOP:
                return uv_copied, n + 1
            if n < N_NA1:
                return loop_copied, n - N_LOOP + 1
            if n < N_GLU:
                return na_gated, n - N_NA1 + 1
            if n < N_NA2:
                return glu_sig, n - N_GLU + 1
            if n < N_S5O:
                return na_gated, n - N_NA2 + 9
            if n < N_WO:
                return so_gated, n - N_S5O + 1
            if n < N_FF:
                return res_added, n - N_WO + 1
            if n < N_DN:
                return (g_silu, mid_ready)[(n - N_FF) % 2], (n - N_FF) // 2 + 1
            return res_added, 8 + n - N_DN + 1

        @block.sync
        def _(sp):
            def load(m, c):
                if not (isinstance(m, int) and 12 * m + c < RAW):
                    sp.wait_ge(lo_ready, 12 * m + (c - RAW + 1))
                sp.dma_start(raw[:, c % RAW, :], wstream[bass.ds(12 * m + c, 1), :, :].rearrange("o p n -> p (o n)")
                             ).then_inc(raw_landed[c % RAW], 16)

            def stage(f, p):
                sp.dma_start(pk[:, p, :], pack[bass.ds(f, 1), :, :].rearrange("o p n -> p (o n)")).then_inc(pk_staged[p], 16)
                sp.dma_start(base[:, p, :, :], base_dram[:, bass.ds(TILES * f, TILES), :]).then_inc(base_staged[p], 16)
                sp.dma_start(vcur[:, p, :, :], v_dram[:, bass.ds(DH * f, DH)].rearrange("(t p) n -> p t n", p=P)
                             ).then_inc(v_staged[p], 16)
                sp.dma_start(bm[:, p, :, :], bias[bass.ds(f, 1), :, :].rearrange("o p (t n) -> p (o t) n", t=TT)
                             ).then_inc(bias_staged[p], 16)

            for i in range(XP):
                sp.dma_start(xraw[:, 2 * i:2 * i + 2, :], xT[:, 2 * i:2 * i + 2, :]).then_inc(x_landed[i], 16)
                if i in X_TO_W:
                    load(0, X_TO_W[i])
            sp.dma_start(col[:, :], cols).then_inc(col_landed, 16)
            for c in range(RAW, 12):
                load(0, c)
            for f in range(2):
                sp.dma_start(pk[:, f, :], pack[f, :, :]).then_inc(pk_staged[f], 16)
                sp.dma_start(bm[:, f, :, :], bias[f, :, :].rearrange("p (t n) -> p t n", t=TT)).then_inc(bias_staged[f], 16)
            for c in range(12, H_LOOP):
                load(0, c)

            def passes(k, last):
                for p in range(2):
                    for j in range(PER_F):
                        if j == 10 and not (p == 0 and isinstance(k, int) and k == 0) and not (p == 1 and last):
                            sp.wait_ge(fin_step, 2 * (2 * k + p))
                            sp.wait_ge(att_lo, 2 * k + p)
                            stage(2 * k + p + 1, 1 - p)
                        load(2 * k, H_LOOP + PER_F * p + j)

            sp.wait_ge(base_stored, 16)
            passes(0, False)
            with sp.Fori(1, HEADS // 2 - 1) as k:
                passes(k, False)
            passes(HEADS // 2 - 1, True)

            for c in range(H_NA1, H_S5O + KD):
                if c == H_S5O:
                    sp.wait_ge(ys_lo, 1)
                    sp.dma_start(hp[:, :, :], xtok.rearrange("(t p) n -> p t n", p=P)).then_inc(xtok_landed, 16)
                    for r in range(2):
                        sp.dma_start(lnrow[:, r, :], lnrows[r:r + 1, :].to_broadcast([P, D])).then_inc(ln1_landed, 16)
                load(0, c)
            for c in range(H_WO, H_FF + 4):
                load(0, c)
            n0 = (H_END - H_FF - 4) // 12
            c0 = H_FF + 4
            with sp.Fori(0, n0 // 2) as m:
                for c in range(c0, c0 + 12):
                    load(m, c)
            sp.wait_ge(h_step, 4)
            for r in range(2):
                sp.dma_start(lnrow[:, r, :], lnrows[2 + r:3 + r, :].to_broadcast([P, D])).then_inc(ln2_landed, 16)
            with sp.Fori(n0 // 2, n0) as m:
                for c in range(c0, c0 + 12):
                    load(m, c)
            for c in range(c0 + 12 * n0, H_END):
                load(0, c)
            for i in LN2_STORES:
                if i in LN2_DVE:
                    sp.wait_ge(ln2_dve, LN2_DVE.index(i) + 1)
                else:
                    sp.wait_ge(ln2_pool, LN2_POOL.index(i) + 1)
                t, b = i // 4, slice(i % 4 * 512, i % 4 * 512 + 512)
                sp.dma_start(out[t * P:(t + 1) * P, b], hp[:, t, b]).then_inc(stored, 16)
            sp.wait_ge(stored, 16 * len(LN2_STORES))

        @block.gpsimd
        def _(pool):
            pool.memset(ident[:, :], 0.0).then_inc(const_step, 1)
            pool.memset(mask[:, :], 0.0).then_inc(const_step, 1)
            pool.memset(eps1[:, :], EPS).then_inc(const_step, 1)
            pool.wait_ge(const_step, 3)
            pool.affine_select(out=ident[:, :], in_=ident[:, :], compare_op=ALU.not_equal, fill=1.0, base=0,
                               pattern=[[-1, P]], channel_multiplier=1).then_inc(const_step, 1)
            for hf in range(2):
                lo = mask[64 * hf:64 * hf + 64, 0:GRID_W - WIN]
                hi = mask[64 * hf:64 * hf + 64, WIN:GRID_W]
                pool.wait_ge(const_step, 4 + 2 * hf)
                pool.affine_select(out=lo, in_=lo, compare_op=ALU.is_ge, fill=-1e30, base=WIN // 2,
                                   pattern=[[1, GRID_W - WIN]], channel_multiplier=-1).then_inc(const_step, 1)
                pool.wait_ge(const_step, 5 + 2 * hf)
                pool.affine_select(out=hi, in_=hi, compare_op=ALU.is_gt, fill=-1e30, base=WIN // 2 - WIN,
                                   pattern=[[-1, GRID_W - WIN]], channel_multiplier=1).then_inc(const_step, 1)
            pool.wait_ge(const_step, 8)

            pool.dma_start(scratch[:, 0:3, :], params).then_inc(par_landed, 16)
            pool.wait_ge(par_done, 1)
            done = [0]

            def step(ins):
                ins.then_inc(tab_step, 1)
                done[0] += 1
                pool.wait_ge(tab_step, done[0])

            def tt(o, a, b, op):
                step(pool.tensor_tensor(o, a, b, op))

            q1 = [scratch[:, 22 + i, :].rearrange("p (g o) -> p g o", o=1) for i in range(2)]
            big = [scratch[:, 24 + 4 * i:28 + 4 * i, :].rearrange("p a b -> p (a b)") for i in range(2)]

            def cmul(ore, oim, are, aim, bre, bim, n):
                t1, t2 = (b[:, 0:GROUPS * min(n, 4)].rearrange("p (g n) -> p g n", n=min(n, 4)) for b in big)
                for s in range(0, n, 4):
                    e = min(n, s + 4)
                    sl = lambda a: a[:, :, s:e]
                    bb = [b.to_broadcast([P, GROUPS, e - s]) for b in (bre, bim)]
                    tt(t1, sl(are), bb[0], ALU.mult)
                    tt(t2, sl(aim), bb[1], ALU.mult)
                    tt(sl(ore), t1, t2, ALU.subtract)
                    tt(t1, sl(are), bb[1], ALU.mult)
                    tt(t2, sl(aim), bb[0], ALU.mult)
                    tt(sl(oim), t1, t2, ALU.add)

            def square():
                t1 = big[0][:, 0:GROUPS].rearrange("p (g o) -> p g o", o=1)
                t2 = big[1][:, 0:GROUPS].rearrange("p (g o) -> p g o", o=1)
                tt(t1, q1[1], q1[1], ALU.mult)
                tt(t2, q1[0], q1[1], ALU.mult)
                tt(t2, t2, t2, ALU.add)
                tt(q1[0], q1[0], q1[0], ALU.mult)
                tt(q1[0], q1[0], t1, ALU.subtract)
                step(pool.tensor_copy(q1[1], t2))

            bc = base_all[:, :, O_B:O_B + BT]
            bs = base_all[:, :, O_B + BT:O_B + 2 * BT]
            ac = base_all[:, :, O_A + AT:O_A + 2 * AT]
            as_ = base_all[:, :, O_A + 2 * AT:O_A + 3 * AT]
            ans = base_all[:, :, O_A:O_A + AT]
            step(pool.tensor_copy(q1[0], bc[:, :, 1:2]))
            step(pool.tensor_copy(q1[1], bs[:, :, 1:2]))
            n = 2
            while n < BT:
                square()
                cmul(bc[:, :, n:2 * n], bs[:, :, n:2 * n], bc[:, :, 0:n], bs[:, :, 0:n], q1[0], q1[1], n)
                n *= 2
            square()
            n = 1
            while n < AT:
                cmul(ac[:, :, n:2 * n], as_[:, :, n:2 * n], ac[:, :, 0:n], as_[:, :, 0:n], q1[0], q1[1], n)
                n *= 2
                if n < AT:
                    square()
            step(pool.tensor_scalar(ans, as_, -1.0, None, ALU.mult))
            pool.dma_start(base_dram, base_all[:, :, :]).then_inc(base_stored, 16)
            for f in range(2):
                step(pool.tensor_copy(base[:, f, :, :], base_all[:, TILES * f:TILES * f + TILES, :]))

            def table(f, p, i):
                s = TILES * f + i
                row = base[:, p, i, :]
                a = [row[:, O_A + AT * j:O_A + AT * j + 2 * AT].rearrange("p (c a o) -> p c a o", c=2, o=1)
                     .to_broadcast([P, 2, AT, BT]) for j in (1, 0)]
                for j in range(2):
                    b = row[:, O_B + BT * j:O_B + BT * j + BT].rearrange("p (c a b) -> p c a b", c=1, a=1)
                    pool.tensor_tensor(tt12[:, j, :, :].rearrange("p c (a b) -> p c a b", b=BT), a[j],
                                       b.to_broadcast([P, 2, AT, BT]), ALU.mult).then_inc(tab_prod, 1)
                pool.wait_ge(tab_prod, 2 * s + 2)
                pool.tensor_tensor(E[:, i % 4, :, P:T], tt12[:, 0, :, :], tt12[:, 1, :, :], ALU.add).then_inc(tab_half, 1)
                pool.wait_ge(tab_half, s + 1)

            def products(f, p, i):
                s = TILES * f + i
                pool.wait_ge(z_ready, 2 * s + 2)
                if i >= 4 or not (isinstance(f, int) and f == 0):
                    pool.wait_ge(y_done, 2 * f + i // 4)
                zc, e, o = z[:, i % 2, :, :], E[:, i % 4, :, :], prod[:, i % 4, :, :]
                for j in range(2):
                    pool.tensor_tensor(o[:, 2 * j:2 * j + 2, :], zc, e[:, j:j + 1, :].to_broadcast([P, 2, T]), ALU.mult
                                       ).then_inc(prod_ready, 1)
                pool.wait_ge(prod_ready, 2 * s + 2)

            def c_matrices(f, p):
                c = pk[:, p, 512:512 + 2 * TILES * 32].rearrange("p (i r n) -> p i r n", i=TILES, r=2)
                kr, ki, nki = (base[:, p, :, o:o + 1].to_broadcast([P, TILES, 32]) for o in (O_KR, O_KI, O_NKI))
                t1, t2 = ctmp[:, 0, :, :], ctmp[:, 1, :, :]
                n = 7 * f
                pool.tensor_tensor(t1, c[:, :, 0, :], kr, ALU.mult).then_inc(c_step, 1)
                pool.tensor_tensor(t2, c[:, :, 1, :], ki, ALU.mult).then_inc(c_step, 1)
                pool.wait_ge(c_step, n + 2)
                pool.tensor_tensor(cmat[:, p, :, 0, :], t1, t2, ALU.subtract).then_inc(c_step, 1)
                pool.tensor_tensor(cmat[:, p, :, 2, :], t2, t1, ALU.subtract).then_inc(c_step, 1)
                pool.wait_ge(c_step, n + 4)
                pool.tensor_tensor(t1, c[:, :, 0, :], nki, ALU.mult).then_inc(c_step, 1)
                pool.tensor_tensor(t2, c[:, :, 1, :], kr, ALU.mult).then_inc(c_step, 1)
                pool.wait_ge(c_step, n + 6)
                pool.tensor_tensor(cmat[:, p, :, 1, :], t1, t2, ALU.subtract).then_inc(c_step, 1)
                pool.wait_ge(c_step, n + 7)

            def one_pass(k, p):
                f = 2 * k + p
                pool.wait_ge(pk_staged[p], 16 * k + 16)
                if not (isinstance(f, int) and f < 2):
                    pool.wait_ge(base_staged[p], 16 * k)
                if not (isinstance(f, int) and f < 2):
                    pool.wait_ge(fin_step, 2 * f - 2)
                table(f, p, 0)
                table(f, p, 1)
                c_matrices(f, p)
                pool.wait_ge(bias_staged[p], 16 * k + 16)
                b = bm[:, p, :, :].rearrange("p t (r c) -> p (t r) c", c=GRID_W)
                pool.tensor_tensor(b, b, mask[:, :].rearrange("p (o c) -> p o c", o=1).to_broadcast([P, TT * ROWS, GRID_W]),
                                   ALU.add).then_inc(bias_ready, 1)
                for i in range(TILES):
                    if i + 2 < TILES:
                        table(f, p, i + 2)
                    products(f, p, i)

            one_pass(0, 0)
            one_pass(0, 1)
            with pool.Fori(1, HEADS // 2) as k:
                one_pass(k, 0)
                one_pass(k, 1)

            pool.wait_ge(ln1_landed, 32)
            pool.wait_ge(hT_psum, 8)
            for t in range(TT):
                pool.tensor_tensor(hp[:, t, :], hp[:, t, :], lnrow[:, 0, :], ALU.mult).then_inc(h_step, 1)
                pool.wait_ge(h_step, 2 * t + 1)
                pool.tensor_tensor(hp[:, t, :], hp[:, t, :], lnrow[:, 1, :], ALU.add).then_inc(h_step, 1)
            pool.wait_ge(ln2_landed, 32)
            for n, i in enumerate(LN2_POOL):
                v, b = hp[:, i // 4, i % 4 * 512:i % 4 * 512 + 512], slice(i % 4 * 512, i % 4 * 512 + 512)
                pool.wait_ge(ln2_norm, n + 1)
                pool.tensor_tensor(v, v, lnrow[:, 0, b], ALU.mult).then_inc(ln2_mul, 1)
                pool.wait_ge(ln2_mul, n + 1)
                pool.tensor_tensor(v, v, lnrow[:, 1, b], ALU.add).then_inc(ln2_pool, 1)

        @block.scalar
        def _(act):
            def split_hi(m, c):
                act.wait_ge(raw_landed[c % RAW], 48 * m + 16 * (c // RAW + 1))
                if not (isinstance(m, int) and 12 * m + c < SPL):
                    act.wait_ge(w_used, 12 * m + (c - SPL + 1))
                act.activation(whi[:, c % SPL, :], raw[:, c % RAW, :], ACT.Copy).then_inc(hi_ready, 1)

            def store_v(b):
                act.wait_ge(uv_copied, KS + 2 * b + 2)
                act.dma_start(v_dram[:, 512 * b:512 * b + 512].rearrange("(t p) n -> p t n", p=P), vout[:, :, :]
                              ).then_inc(v_stored[b], 16)

            for i in range(XP):
                act.wait_ge(x_landed[i], 16)
                act.activation(act16[:, 2 * i:2 * i + 2, 0, :], xraw[:, 2 * i:2 * i + 2, :], ACT.Copy).then_inc(x_hi, 1)
                if i in X_TO_W and X_TO_W[i] < 3:
                    split_hi(0, X_TO_W[i])
            for c in range(3, H_LOOP):
                split_hi(0, c)
                if c == H_V + 12:
                    store_v(0)

            def stage_u(k, p):
                f = 2 * k + p
                if isinstance(f, int) and f == 0:
                    act.wait_ge(uv_copied, KS)
                if not (isinstance(f, int) and f < 2):
                    act.wait_ge(bu_ready, TILES * f - TILES)
                src = u[:, bass.ds(f, 1), :]
                act.activation(ucur[:, p, 0:1, :], src, ACT.Copy).then_inc(ucur_ready, 1)
                act.wait_ge(ucur_ready, 2 * f + 1)
                act.activation(ucur[:, p, 1, :], ucur[:, p, 0, ::-1], ACT.Copy).then_inc(ucur_ready, 1)

            def stage_v01():
                for b in range(2):
                    act.wait_ge(v_stored[b], 16)
                for f in range(2):
                    act.dma_start(vcur[:, f, :, :], v_dram[:, DH * f:DH * f + DH].rearrange("(t p) n -> p t n", p=P)
                                  ).then_inc(v_staged[f], 16)

            def table_rev(k, p, i):
                s = TILES * (2 * k + p) + i
                act.wait_ge(tab_half, s + 1)
                act.activation(E[:, i % 4, 0, 0:P], E[:, i % 4, 0, T - 1:P - 1:-1], ACT.Copy).then_inc(tab_ready, 1)
                act.activation(E[:, i % 4, 1, 0:P], E[:, i % 4, 1, T - 1:P - 1:-1], ACT.Copy, scale=-1.0).then_inc(tab_ready, 1)

            def softmax_exp(k, p):
                f = 2 * k + p
                act.wait_ge(soft_step, 3 * f + 3)
                for t in range(TT):
                    act.activation(S[:, t, :], S[:, t, :], ACT.Exp, bias=sm[:, 1, t:t + 1],
                                   accum_out=sm[:, 2, t:t + 1]).then_inc(exp_ready, 1)

            def pt_copy(f):
                act.wait_ge(tr_ready, f + 1)
                if not (isinstance(f, int) and f == 0):
                    act.wait_ge(pv_done, f)
                act.activation(PT[:, :, :].rearrange("p t n -> p (t n)"), ps[TB][:, :], ACT.Copy).then_inc(pt_ready, 1)

            def attn_hi(f):
                act.wait_ge(pv_done, f + 1)
                act.activation(act8a[:, bass.ds(f, 1), 0, :], ps[AB][:, 0:T].rearrange("p (o n) -> p o n", o=1), ACT.Copy
                               ).then_inc(att_hi, 1)

            def loop_copy(k, p, o):
                f = 2 * k + p
                act.wait_ge(w_used, PER_F * f + (H_LOOP + 2 * o + 2))
                src = ps[bank_of(N_LOOP + o)][:, 0:T].rearrange("p (o n) -> p o n", o=1)
                if o < 2:
                    if not (isinstance(f, int) and f < 2):
                        act.wait_ge(sc_ready, f - 1)
                    dst = qk[:, p, o:o + 1, :]
                else:
                    g = ga if o < 4 else gs
                    dst = g[:, bass.ds(2 * f + o % 2, 1), :]
                act.activation(dst, src, ACT.Copy).then_inc(loop_copied, 1)

            def one_pass(k, p, first):
                c0 = H_LOOP + PER_F * p
                for j in range(PER_F):
                    split_hi(2 * k, c0 + j)
                    if j == 1 and not first:
                        loop_copy(*((k, 0) if p else (k - 1, 1)), 5)
                    if j >= 1 + LAG and (j - 1 - LAG) % 2 == 0:
                        loop_copy(k, p, (j - 1 - LAG) // 2)
                    if j == 0:
                        stage_u(k, p)
                    if j == 3 and first:
                        store_v(1)
                    if j == 7 and first:
                        stage_v01()
                    if j == 11:
                        pt_copy(2 * k + p)
                    if j == 1 and not first:
                        attn_hi(2 * k + p - 1)
                    if j == 8:
                        softmax_exp(k, p)
                    for i in range(TILES):
                        if BU_SLOT[i] + LAG - 1 == j:
                            table_rev(k, p, i)

            one_pass(0, 0, True)
            one_pass(0, 1, False)
            with act.Fori(1, HEADS // 2) as k:
                one_pass(k, 0, False)
                one_pass(k, 1, False)

            act.wait_ge(col_landed, 16)
            loop_copy(HEADS // 2 - 1, 1, 5)
            for j in range(8):
                split_hi(0, H_NA1 + j)
                if j == 0:
                    attn_hi(HEADS - 1)
                if j == 5:
                    act.wait_ge(fin_step, 2 * KS)
                    uf = u[:, :, :]
                    act.activation(uf, uf, ACT.Gelu_apprx_tanh).then_inc(gelu_done, 1)
                    act.wait_ge(gelu_done, 1)
                    act.activation(act8b[:, :, 0, :], uf, ACT.Copy).then_inc(ys_hi, 1)
                if j >= 4:
                    for t in (2 * (j - 4), 2 * (j - 4) + 1):
                        g = ga[:, t, :]
                        act.activation(g, g, ACT.Sigmoid, bias=col[:, t:t + 1]).then_inc(ga_sig, 1)

            def glu_act(t):
                act.wait_ge(w_used, H_GLU + t + 1)
                if t >= 4:
                    act.wait_ge(glu_y, t - 3)
                act.activation(ev2[:, t % 4, :], ps[bank_of(N_GLU + t)][:, 0:T], ACT.Sigmoid, bias=col[:, 32 + t:33 + t]
                               ).then_inc(glu_sig, 1)

            def glu_split(t):
                act.wait_ge(glu_y, t + 1)
                act.activation(act8b[:, t, 0, :], u[:, t, :], ACT.Copy).then_inc(glu_hi, 1)

            def mix_split(t):
                act.wait_ge(mix_ready, t + 1)
                act.activation(act16[:, t, 0, :], ga[:, t, :], ACT.Copy).then_inc(mix_hi, 1)

            for j in range(8):
                split_hi(0, H_GLU + j)
                t = 8 + j
                act.activation(ga[:, t, :], ga[:, t, :], ACT.Sigmoid, bias=col[:, t:t + 1]).then_inc(ga_sig, 1)
                if j >= LAG:
                    glu_act(j - LAG)
            for j in range(8):
                split_hi(0, H_NA2 + j)
                if j < LAG:
                    glu_act(8 - LAG + j)
                if j == 3:
                    act.wait_ge(w_used, H_NA2)
                if 3 <= j < 7:
                    glu_split(2 * (j - 3))
                    glu_split(2 * (j - 3) + 1)
                for t in (2 * j, 2 * j + 1):
                    act.activation(gs[:, t, :], gs[:, t, :], ACT.Sigmoid, bias=col[:, 16 + t:17 + t]).then_inc(gs_sig, 1)
            for j in range(KD):
                split_hi(0, H_S5O + j)
                if j >= LAG + 1:
                    mix_split(j - LAG - 1)
            for j in range(32):
                split_hi(0, H_WO + j)
                if j < LAG + 1:
                    mix_split(KD - LAG - 1 + j)

            def sd(e):
                act.wait_ge(var_ready, 2 * e + 2)
                if e > 0:
                    act.wait_ge(ln_step, 2 * e)
                act.activation(lnm[:, :, 4:5], lnm[:, :, 1:2], ACT.Sqrt, bias=eps1[:, :]).then_inc(sd_ready, 1)

            def mid_split_hi(n, b):
                act.wait_ge(mid_ready, n + 1)
                act.activation(mid[:, bass.ds(n, 1), 0, :], ev2[:, b:b + 1, :], ACT.Copy).then_inc(mid_hi, 1)

            def gate(m, i, c):
                act.wait_ge(w_used, 12 * m + (H_FF + c + 1))
                if not isinstance(m, int) or m > 0:
                    act.wait_ge(mid_ready, 3 * m + i - 2)
                act.activation(ev[:, i, :], ps[bank_of(N_FF + 2 * i)][:, 0:T], ACT.Silu).then_inc(g_silu, 1)

            for c in range(3):
                split_hi(0, H_FF + c)
            act.wait_ge(const_step, 3)
            sd(0)
            for g in range(8):
                act.wait_ge(hT_psum, g + 1)
                if g >= 2:
                    act.wait_ge(hT_lo, g - 1)
                for e in range(2):
                    t = 2 * g + e
                    act.activation(hT[:, g % 2, e, :], ps[4 + g % 4][:, e * T:(e + 1) * T], ACT.Identity,
                                   scale=col[:, 40 + t:41 + t], bias=col[:, 56 + t:57 + t]).then_inc(hT_f32, 1)
                act.wait_ge(hT_f32, 2 * g + 2)
                act.activation(act16[:, 2 * g:2 * g + 2, 0, :], hT[:, g % 2, :, :], ACT.Copy).then_inc(hT_hi, 1)
                if g == 5:
                    split_hi(0, H_FF + 3)
            for c in range(4, 12):
                split_hi(0, H_FF + c)
                if c == 8:
                    mid_split_hi(0, 0)
                if c in (6, 8, 11):
                    gate(0, (c - 5) // 2 if c < 11 else 2, (4, 6, 9)[(c - 5) // 2 if c < 11 else 2])
                if c == 10:
                    mid_split_hi(1, 1)

            def ff(m, count=3):
                for i in range(count):
                    for q in range(4):
                        split_hi(m, H_FF + 4 * i + q)
                        if q == 2:
                            mid_split_hi(3 * m + i - 1, (i - 1) % 3)
                        if q == 3:
                            gate(m, i, 4 * i + 1)

            with act.Fori(1, KF // 3) as m:
                ff(m)
            ff(KF // 3, KF % 3)
            for c in range(4):
                split_hi(0, H_DN + c)
                if c == 2:
                    mid_split_hi(KF - 1, (KF - 1) % 3)
            with act.Fori(0, (H_END - H_DN - 4) // 12) as m:
                for c in range(12):
                    split_hi(m, H_DN + 4 + c)
            sd(1)
            act.wait_ge(ln_step, 4)
            for i in LN2_POOL:
                t = i // 4
                v = hp[:, t, i % 4 * 512:i % 4 * 512 + 512]
                act.activation(v, v, ACT.Identity, scale=lnm[:, t, 2:3], bias=lnm[:, t, 3:4]).then_inc(ln2_norm, 1)

        @block.vector
        def _(dve):
            def split_lo(m, c):
                dve.wait_ge(hi_ready, 12 * m + (c + 1))
                dve.tensor_tensor(wlo[:, c % SPL, :], raw[:, c % RAW, :], whi[:, c % SPL, :].bitcast(F32), ALU.subtract
                                  ).then_inc(lo_ready, 1)

            def low(o, full, hi, s):
                dve.tensor_tensor(o, full, hi.bitcast(F32), ALU.subtract).then_inc(s, 1)

            done = [0]

            def step(ins):
                ins.then_inc(par_step, 1)
                done[0] += 1
                dve.wait_ge(par_step, done[0])

            (ARE, AIM, DT, X, Y, NI, RR, EM, EX, H1, H2, SH, CH, CY, SY, KR, KI, T0, T1, T2, P0, P1) = (
                scratch[:, i, :] for i in range(22))

            def ts(o, a, s1, s2, *ops):
                step(dve.tensor_scalar(o, a, s1, s2, *ops))

            def tt(o, a, b, op):
                step(dve.tensor_tensor(o, a, b, op))

            def stt(o, a, s, b, op0, op1):
                step(dve.scalar_tensor_tensor(out=o, in0=a, scalar=s, in1=b, op0=op0, op1=op1))

            def expm1(o_em, o_ex, v):
                ts(T0, v, -87.0, 88.5, ALU.max, ALU.min)
                ts(NI, T0, 1.4426950408889634, MAGIC, ALU.mult, ALU.add)
                ts(NI, NI, MAGIC, None, ALU.subtract)
                stt(RR, NI, -LN2_HI, T0, ALU.mult, ALU.add)
                stt(RR, NI, -LN2_LO, RR, ALU.mult, ALU.add)
                ts(P0, RR, EXP_C[-1], None, ALU.mult)
                for c in EXP_C[-2::-1]:
                    stt(P0, P0, c, RR, ALU.add, ALU.mult)
                stt(P0, P0, 1.0, RR, ALU.add, ALU.mult)
                ts(T1.bitcast(I32), NI, 127.0, 8388608.0, ALU.add, ALU.mult)
                if o_em is not None:
                    ts(T2, T1, -1.0, None, ALU.add)
                    tt(o_em, P0, T1, ALU.mult)
                    tt(o_em, o_em, T2, ALU.add)
                stt(o_ex, P0, 1.0, T1, ALU.add, ALU.mult)

            def time_steps():
                expm1(None, DT, DT)

            def decays():
                tt(X, ARE, DT, ALU.mult)
                tt(Y, AIM, DT, ALU.mult)
                expm1(EM, EX, X)

            def sines():
                ts(NI, Y, 1.0 / (2 * np.pi), MAGIC, ALU.mult, ALU.add)
                ts(NI, NI, MAGIC, None, ALU.subtract)
                for c in TWO_PI:
                    stt(Y, NI, -c, Y, ALU.mult, ALU.add)
                ts(H1, Y, 0.5, None, ALU.mult)
                tt(H2, H1, H1, ALU.mult)
                ts(P0, H2, SIN_C[-1], None, ALU.mult)
                for c in SIN_C[-2::-1]:
                    stt(P0, P0, c, H2, ALU.add, ALU.mult)
                stt(SH, P0, 1.0, H1, ALU.add, ALU.mult)

            def cosines():
                ts(P0, H2, COS_C[-1], None, ALU.mult)
                for c in COS_C[-2::-1]:
                    stt(P0, P0, c, H2, ALU.add, ALU.mult)
                ts(CH, P0, 1.0, None, ALU.add)
                stt(SY, SH, 2.0, CH, ALU.mult, ALU.mult)
                stt(P1, SH, -2.0, SH, ALU.mult, ALU.mult)
                ts(CY, P1, 1.0, None, ALU.add)

            def gains():
                tt(H1, EM, CY, ALU.mult)
                tt(H1, H1, P1, ALU.add)
                tt(H2, EX, SY, ALU.mult)
                tt(T0, ARE, ARE, ALU.mult)
                tt(T1, AIM, AIM, ALU.mult)
                tt(T2, T0, T1, ALU.add)
                step(dve.reciprocal(T2, T2))
                tt(T0, H1, ARE, ALU.mult)
                tt(T1, H2, AIM, ALU.mult)
                tt(T0, T0, T1, ALU.add)
                tt(KR, T0, T2, ALU.mult)
                tt(T0, H2, ARE, ALU.mult)
                tt(T1, H1, AIM, ALU.mult)
                tt(T0, T0, T1, ALU.subtract)
                tt(KI, T0, T2, ALU.mult)

            def first_entries():
                def put(o, src):
                    step(dve.tensor_copy(base_all[:, :, o], src))

                put(O_R, EX)
                put(O_KR, KR)
                put(O_KI, KI)
                step(dve.tensor_scalar(base_all[:, :, O_NKI], KI, -1.0, None, ALU.mult))
                step(dve.memset(base_all[:, :, O_B], 1.0))
                step(dve.memset(base_all[:, :, O_B + BT], 0.0))
                put(O_B + 1, CY)
                put(O_B + BT + 1, SY)
                put(O_A + AT, CH)
                dve.tensor_copy(base_all[:, :, O_A + 2 * AT], SH).then_inc(par_done, 1)

            parts = {3: time_steps, 5: decays, 7: sines, 9: cosines, 11: gains, 13: first_entries}
            for i in range(XP):
                dve.wait_ge(x_hi, i + 1)
                low(act16[:, 2 * i:2 * i + 2, 1, :], xraw[:, 2 * i:2 * i + 2, :], act16[:, 2 * i:2 * i + 2, 0, :], x_lo)
                if i in X_TO_W and X_TO_W[i] < 3:
                    split_lo(0, X_TO_W[i])
            for j in range(3, H_V + LAG):
                split_lo(0, j)
                if j >= LAG and U_ORDER[j - LAG][1] == 1:
                    t = U_ORDER[j - LAG][0]
                    dve.wait_ge(w_used, j - LAG + 1)
                    dve.tensor_copy(u[:, t, :], ps[bank_of(N_U + t)][:, 0:T]).then_inc(uv_copied, 1)
                if j in parts:
                    if j == 3:
                        dve.wait_ge(par_landed, 16)
                    parts[j]()
            for j in range(LAG, 16):
                split_lo(0, H_V + j)
                if j == 8 + LAG:
                    dve.wait_ge(w_used, H_V + 8)
                    for t in range(TT):
                        dve.tensor_copy(vout[:, t, :], ps[bank_of(N_V + t)][:, :]).then_inc(uv_copied, 1)

            def v_last():
                dve.wait_ge(w_used, H_V + 16)
                dve.wait_ge(v_stored[0], 16)
                for t in range(TT):
                    dve.tensor_copy(vout[:, t, :], ps[bank_of(N_V + 2 + t)][:, :]).then_inc(uv_copied, 1)

            def turn(k, p, i):
                s = TILES * (2 * k + p) + i
                dve.wait_ge(tab_ready, 2 * s + 2)
                dve.wait_ge(bu_ready, s + 1)
                bu = ps[BU0 + i % 2][:, :].rearrange("p (c n) -> p c n", c=2)
                for j in range(2):
                    dve.tensor_tensor(m12[:, j, :, :], bu, E[:, i % 4, j:j + 1, :].to_broadcast([P, 2, T]), ALU.mult
                                      ).then_inc(bu_read, 1)
                dve.wait_ge(bu_read, 2 * s + 2)
                if not (isinstance(s, int) and s == 0):
                    dve.wait_ge(z_ready, 2 * s)
                dve.tensor_tensor(wz[:, 0, :], m12[:, 0, 0, :], m12[:, 1, 1, :], ALU.add).then_inc(w_turned, 1)
                dve.tensor_tensor(wz[:, 1, :], m12[:, 0, 1, :], m12[:, 1, 0, :], ALU.subtract).then_inc(w_turned, 1)
                dve.wait_ge(w_turned, 2 * s + 2)
                if not (isinstance(s, int) and s < 2):
                    dve.wait_ge(prod_ready, 2 * s - 2)
                r = base[:, p, i, O_R:O_R + 1].to_broadcast([P, T])
                for j in range(2):
                    dve.tensor_tensor_scan(z[:, i % 2, j, :], r, wz[:, j, :], 0.0, ALU.mult, ALU.add).then_inc(z_ready, 1)

            def finish(f, p):
                dve.wait_ge(y_done, 2 * f + 2)
                uf = u[:, bass.ds(f, 1), :]
                ft = fin_t[:, :].rearrange("p (o n) -> p o n", o=1)
                dve.scalar_tensor_tensor(out=ft, in0=uf, scalar=pk[:, p, PACK - 1:PACK],
                                         in1=ps[YB][:, 0:T].rearrange("p (o n) -> p o n", o=1), op0=ALU.mult,
                                         op1=ALU.add).then_inc(fin_step, 1)
                dve.wait_ge(fin_step, 2 * f + 1)
                dve.tensor_tensor(uf, ft, ps[YB][:, T:2 * T][:, ::-1].rearrange("p (o n) -> p o n", o=1), ALU.add
                                  ).then_inc(fin_step, 1)

            def softmax_max(k, p):
                f = 2 * k + p
                dve.wait_ge(bias_ready, f + 1)
                dve.wait_ge(sc_ready, f + 1)
                if not (isinstance(f, int) and f == 0):
                    dve.wait_ge(tr_ready, f)
                dve.scalar_tensor_tensor(out=S[:, :, :], in0=ps[AB][:, :].rearrange("p (t n) -> p t n", t=TT), scalar=SCALE,
                                         in1=bm[:, p, :, :], op0=ALU.mult, op1=ALU.add).then_inc(soft_step, 1)
                dve.wait_ge(soft_step, 3 * f + 1)
                dve.tensor_reduce(sm[:, 0, :], S[:, :, :], AX.X, ALU.max).then_inc(soft_step, 1)
                dve.wait_ge(soft_step, 3 * f + 2)
                dve.tensor_scalar(sm[:, 1, :], sm[:, 0, :], -1.0, None, ALU.mult).then_inc(soft_step, 1)

            def softmax_norm(k, p):
                f = 2 * k + p
                dve.wait_ge(exp_ready, 2 * f + 2)
                dve.reciprocal(sm[:, 3, :], sm[:, 2, :]).then_inc(p_ready, 1)
                dve.wait_ge(p_ready, 3 * f + 1)
                for t in range(TT):
                    dve.tensor_scalar(S[:, t, :], S[:, t, :], sm[:, 3, t:t + 1], None, ALU.mult).then_inc(p_ready, 1)

            def attn_low(f):
                dve.wait_ge(att_hi, f + 1)
                low(act8a[:, bass.ds(f, 1), 1, :], ps[AB][:, 0:T].rearrange("p (o n) -> p o n", o=1),
                    act8a[:, bass.ds(f, 1), 0, :], att_lo)

            def one_pass(k, p, first):
                c0 = H_LOOP + PER_F * p
                for j in range(PER_F):
                    split_lo(2 * k, c0 + j)
                    if j == 1 and first:
                        v_last()
                    if j == 4 and not first:
                        finish(2 * k + p - 1, 1 - p)
                    if j == 2 and not first:
                        attn_low(2 * k + p - 1)
                    if j == 7:
                        softmax_max(k, p)
                    if j == 9:
                        softmax_norm(k, p)
                    for i in range(TILES):
                        if BU_SLOT[i] + LAG == j:
                            turn(k, p, i)

            one_pass(0, 0, True)
            one_pass(0, 1, False)
            with dve.Fori(1, HEADS // 2) as k:
                one_pass(k, 0, False)
                one_pass(k, 1, False)

            def na_gate(t, h):
                dve.wait_ge(w_used, h + 1)
                dve.wait_ge(ga_sig, t + 1)
                dve.tensor_tensor(ga[:, t, :], ps[bank_of(N_NA1 + t if t < 8 else N_NA2 + t - 8)][:, 0:T], ga[:, t, :],
                                  ALU.mult).then_inc(na_gated, 1)

            for j in range(8):
                split_lo(0, H_NA1 + j)
                if j == 0:
                    attn_low(HEADS - 1)
                if j == 4:
                    finish(HEADS - 1, 1)
                if j == 6:
                    dve.wait_ge(ys_hi, 1)
                    low(act8b[:, :, 1, :], u[:, :, :], act8b[:, :, 0, :], ys_lo)
                if j >= LAG:
                    na_gate(j - LAG, H_NA1 + j - LAG)

            def glu_mult(t):
                dve.wait_ge(glu_sig, t + 1)
                dve.tensor_tensor(u[:, t, :], u[:, t, :], ev2[:, t % 4, :], ALU.mult).then_inc(glu_y, 1)

            for j in range(8):
                split_lo(0, H_GLU + j)
                if j < LAG:
                    na_gate(8 - LAG + j, H_GLU - LAG + j)
                if j >= LAG + 1:
                    glu_mult(j - LAG - 1)
            for j in range(8):
                split_lo(0, H_NA2 + j)
                if j >= LAG:
                    na_gate(8 + j - LAG, H_NA2 + j - LAG)
                if j < LAG + 1:
                    glu_mult(8 - LAG - 1 + j)
                if j >= 4:
                    for t in (2 * (j - 4), 2 * (j - 4) + 1):
                        dve.wait_ge(glu_hi, t + 1)
                        low(act8b[:, t, 1, :], u[:, t, :], act8b[:, t, 0, :], glu_lo)
            for t in range(16 - LAG, 16):
                na_gate(t, H_NA2 + t - 8)

            def s5o_evac(t):
                dve.wait_ge(w_used, H_S5O + t + 1)
                dve.wait_ge(gs_sig, t + 1)
                dve.tensor_tensor(gs[:, t, :], ps[bank_of(N_S5O + t)][:, 0:T], gs[:, t, :], ALU.mult).then_inc(so_gated, 1)
                dve.wait_ge(so_gated, t + 1)
                dve.tensor_tensor(ga[:, t, :], gs[:, t, :], ga[:, t, :], ALU.add).then_inc(mix_ready, 1)

            def mix_low(t):
                dve.wait_ge(mix_hi, t + 1)
                low(act16[:, t, 1, :], ga[:, t, :], act16[:, t, 0, :], mix_lo)

            for j in range(KD):
                split_lo(0, H_S5O + j)
                if j >= LAG:
                    s5o_evac(j - LAG)
                if j >= LAG + 2:
                    mix_low(j - LAG - 2)

            def residual(n, h, t, b):
                dve.wait_ge(w_used, h + 1)
                v = hp[:, t, b * 512:(b + 1) * 512]
                dve.scalar_tensor_tensor(out=v, in0=v, scalar=ALPHA, in1=ps[bank_of(n)][:, :], op0=ALU.mult, op1=ALU.add
                                         ).then_inc(res_added, 1)
                dve.wait_ge(*taken(n))
                dve.bn_stats(stats[:, t, b, :], v).then_inc(stat_ready, 1)

            def centre(i):
                t, b = i // 4, slice(i % 4 * 512, i % 4 * 512 + 512)
                dve.scalar_tensor_tensor(out=hp[:, t, b], in0=hp[:, t, b], scalar=lnm[:, t, 0:1], in1=lnrow[:, 0, b],
                                         op0=ALU.subtract, op1=ALU.mult).then_inc(ln2_gain, 1)

            def moments(e, between=None):
                dve.wait_ge(stat_ready, 8 * (e + 1))
                for t in range(TT):
                    dve.bn_aggr(lnm[:, t, 0:2], stats[:, t, :, :].rearrange("p a b -> p (a b)")).then_inc(var_ready, 1)
                dve.wait_ge(var_ready, TT * (e + 1))
                if between:
                    between()
                dve.wait_ge(sd_ready, e + 1)
                dve.reciprocal(lnm[:, :, 2:3], lnm[:, :, 4:5]).then_inc(ln_step, 1)
                dve.wait_ge(ln_step, 2 * e + 1)
                dve.scalar_tensor_tensor(out=lnm[:, :, 3:4], in0=lnm[:, :, 0:1], scalar=-1.0, in1=lnm[:, :, 2:3],
                                         op0=ALU.mult, op1=ALU.mult).then_inc(ln_step, 1)
                dve.wait_ge(ln_step, 2 * e + 2)

            for j in range(32):
                split_lo(0, H_WO + j)
                if j < LAG:
                    s5o_evac(KD - LAG + j)
                if j < LAG + 2:
                    mix_low(KD - LAG - 2 + j)
                if j == 4:
                    dve.wait_ge(xtok_landed, 16)
                if j % 8 == 1 and j > 8:
                    for t in range(TT):
                        b = j // 8 - 1
                        residual(N_WO + 2 * b + t, H_WO + 8 * b + 7, t, b)
            for c in range(3):
                split_lo(0, H_FF + c)
            for t in range(TT):
                residual(N_WO + 6 + t, H_WO + 31, t, 3)
            moments(0)
            for b in range(4):
                for t in range(TT):
                    v = hp[:, t, b * 512:(b + 1) * 512]
                    dve.tensor_scalar(v, v, lnm[:, t, 2:3], lnm[:, t, 3:4], ALU.mult, ALU.add).then_inc(norm_ready, 1)
            for g in range(8):
                dve.wait_ge(hT_hi, g + 1)
                low(act16[:, 2 * g:2 * g + 2, 1, :], hT[:, g % 2, :, :], act16[:, 2 * g:2 * g + 2, 0, :], hT_lo)
                if g == 5:
                    split_lo(0, H_FF + 3)

            def ff(m, count=3):
                for i in range(count):
                    for q in range(4):
                        split_lo(m, H_FF + 4 * i + q)
                        if q == 1:
                            up(3 * m + i - 1, i - 1, 12 * m + (H_FF + 4 * i))
                        if q == 3:
                            mid_low(3 * m + i - 1, (i - 1) % 3)

            def up(n, i, used):
                dve.wait_ge(w_used, used)
                dve.wait_ge(g_silu, n + 1)
                dve.tensor_tensor(ev2[:, i % 3, :], ps[bank_of(N_FF + (2 * i + 1) % 6)][:, 0:T], ev[:, i % 3, :], ALU.mult
                                  ).then_inc(mid_ready, 1)

            def mid_low(n, r):
                dve.wait_ge(mid_hi, n + 1)
                low(mid[:, bass.ds(n, 1), 1, :], ev2[:, r:r + 1, :], mid[:, bass.ds(n, 1), 0, :], mid_lo)

            for c in range(4, 12):
                split_lo(0, H_FF + c)
                if c == 7:
                    up(0, 0, H_FF + 6)
                if c == 9:
                    mid_low(0, 0)
                    up(1, 1, H_FF + 8)
                if c == 11:
                    mid_low(1, 1)
            with dve.Fori(1, KF // 3) as m:
                ff(m)
            ff(KF // 3, KF % 3)

            def dn_evac(b):
                for t in range(TT):
                    residual(N_DN + 2 * b + t, H_DN + 22 * b + 21, t, b)

            for c in range(4 * (KF // 2)):
                split_lo(0, H_DN + c)
                if c == 1:
                    up(KF - 1, KF % 3 - 1, H_DN)
                if c == 3:
                    mid_low(KF - 1, (KF - 1) % 3)
                    dve.wait_ge(h_step, 4)
                if c >= 24 and (c - 24) % 22 == 0:
                    dn_evac((c - 24) // 22)
            dn_evac(3)
            dve.wait_ge(ln2_landed, 32)
            moments(1, lambda: centre(LN2_DVE[0]))
            for n, i in enumerate(LN2_DVE):
                if n > 0:
                    centre(i)
                t, b = i // 4, slice(i % 4 * 512, i % 4 * 512 + 512)
                dve.wait_ge(ln2_gain, n + 1)
                dve.scalar_tensor_tensor(out=hp[:, t, b], in0=hp[:, t, b], scalar=lnm[:, t, 2:3], in1=lnrow[:, 1, b],
                                         op0=ALU.mult, op1=ALU.add).then_inc(ln2_dve, 1)

        @block.tensor
        def _(pe):
            def wait_split(m, c):
                pe.wait_ge(lo_ready, 12 * m + (c + 1))

            def prod_a(m, c, act, k0, kn, bank, start, stop, ready=None):
                s = c % SPL
                for i in range(kn):
                    if ready:
                        ready(k0 + i)
                    hi, lo = (w[:, s, i * P:(i + 1) * P] for w in (whi, wlo))
                    pe.matmul(bank[:, 0:T], hi, act[:, k0 + i, 0, :], start=start and i == 0, stop=False)
                    pe.matmul(bank[:, 0:T], hi, act[:, k0 + i, 1, :], start=False, stop=False)
                    mm = pe.matmul(bank[:, 0:T], lo, act[:, k0 + i, 0, :], start=False, stop=stop and i == kn - 1)
                mm.then_inc(w_used, 1)

            def prod_b(c, act, k0, banks, start, stop):
                s = c % SPL
                for i in range(2):
                    hi, lo = (w[:, s, i * 512:(i + 1) * 512] for w in (whi, wlo))
                    for t in range(TT):
                        a = act[:, k0 + i, 0, t * P:(t + 1) * P]
                        b = act[:, k0 + i, 1, t * P:(t + 1) * P]
                        pe.matmul(banks[t][:, :], a, hi, start=start and i == 0, stop=False)
                        pe.matmul(banks[t][:, :], a, lo, start=False, stop=False)
                        mm = pe.matmul(banks[t][:, :], b, hi, start=False, stop=stop and i == 1)
                mm.then_inc(w_used, 1)

            def wait_bank(n):
                o = bank_before(n)
                if o is not None:
                    pe.wait_ge(*taken(o))

            def x_split(kt):
                if kt % 2 == 0:
                    pe.wait_ge(x_lo, kt // 2 + 1)

            for j, (n, h) in enumerate(U_ORDER):
                if h == 0:
                    wait_bank(N_U + n)
                wait_split(0, j)
                prod_a(0, j, act16, 8 * h, 8, ps[bank_of(N_U + n)], h == 0, h == 1,
                       x_split if n == 0 else None)
            for j in range(16):
                n = N_V + 2 * (j // 8)
                if j % 8 == 0:
                    wait_bank(n)
                    wait_bank(n + 1)
                wait_split(0, H_V + j)
                prod_b(H_V + j, act16, 2 * (j % 8), [ps[bank_of(n)], ps[bank_of(n + 1)]], j % 8 == 0, j % 8 == 7)

            def s5_in(k, p, i):
                f = 2 * k + p
                s = TILES * f + i
                d, q = i // 4, i % 4
                if i == 0:
                    pe.wait_ge(pk_staged[p], 16 * k + 16)
                    pe.wait_ge(ucur_ready, 2 * f + 2)
                if not (isinstance(s, int) and s < 2):
                    pe.wait_ge(bu_read, 2 * s - 2)
                rows = slice(32 * q, 32 * q + 32)
                for c in range(2):
                    o = (2 * d + c) * P
                    mm = pe.matmul(ps[BU0 + i % 2][:, c * T:(c + 1) * T], pk[rows, p, o:o + P], ucur[rows, p, d, :],
                                   start=True, stop=True)
                mm.then_inc(bu_ready, 1)

            def s5_out(f, p, d):
                pe.wait_ge(prod_ready, 16 * f + (8 * d + 8))
                pe.wait_ge(c_step, 7 * f + 7)
                if d == 0 and not (isinstance(f, int) and f == 0):
                    pe.wait_ge(fin_step, 2 * f)
                for e in range(4):
                    for q in range(4):
                        mm = pe.matmul(ps[YB][32 * q:32 * q + 32, d * T:(d + 1) * T],
                                       cmat[:, p, 4 * d + q, (0, 1, 1, 2)[e], :], prod[:, q, e, :],
                                       start=e == 0, stop=e == 3)
                mm.then_inc(y_done, 1)

            def scores(k, p):
                f = 2 * k + p
                pe.wait_ge(loop_copied, 6 * f + 2)
                if not (isinstance(f, int) and f == 0):
                    pe.wait_ge(att_lo, f)
                for t in range(TT):
                    mm = pe.matmul(ps[AB][:, t * T:(t + 1) * T], qk[:, p, 0, t * P:(t + 1) * P], qk[:, p, 1, :],
                                   start=True, stop=True)
                mm.then_inc(sc_ready, 1)

            def transposes(k, p):
                f = 2 * k + p
                pe.wait_ge(p_ready, 3 * f + 3)
                if isinstance(f, int) and f == 0:
                    pe.wait_ge(const_step, 4)
                else:
                    pe.wait_ge(pt_ready, f)
                for b in range(TT):
                    for t in range(TT):
                        mm = pe.transpose(ps[TB][:, (b * TT + t) * P:(b * TT + t + 1) * P], S[:, t, b * P:(b + 1) * P],
                                          ident[:, :])
                mm.then_inc(tr_ready, 1)

            def attend(f, k, p):
                pe.wait_ge(pt_ready, f + 1)
                pe.wait_ge(v_staged[p], 16 * k + 16)
                for b in range(TT):
                    mm = pe.matmul(ps[AB][:, 0:T], vcur[:, p, b, :], PT[:, b, :], start=b == 0, stop=b == TT - 1)
                mm.then_inc(pv_done, 1)

            def before(k, p):
                return (2 * k, k, 0) if p else (2 * k - 1, k - 1, 1)

            def one_pass(k, p, first):
                for j in range(PER_F):
                    o = j // 2
                    n = N_LOOP + o
                    if j % 2 == 0:
                        if first and o < 3:
                            wait_bank(n)
                        else:
                            pe.wait_ge(loop_copied, 6 * (2 * k + p) + (o - 2))
                    c = H_LOOP + PER_F * p + j
                    wait_split(2 * k, c)
                    prod_a(2 * k, c, act16, 8 * (j % 2), 8, ps[bank_of(n)], j % 2 == 0, j % 2 == 1)
                    if not first:
                        f1, k1, p1 = before(k, p)
                        if j == 1:
                            s5_out(f1, p1, 1)
                    if j == 5:
                        scores(k, p)
                    if j == 8:
                        s5_out(2 * k + p, p, 0)
                    for i in range(TILES):
                        if BU_SLOT[i] == j:
                            s5_in(k, p, i)
                    if j == 9:
                        transposes(k, p)
                    if j == 11:
                        attend(2 * k + p, k, p)

            one_pass(0, 0, True)
            one_pass(0, 1, False)
            with pe.Fori(1, HEADS // 2) as k:
                one_pass(k, 0, False)
                one_pass(k, 1, False)

            def last_head(kt):
                if kt == HEADS - 1:
                    pe.wait_ge(att_lo, HEADS)

            for j in range(24):
                h, n = H_NA1 + j, N_NA1 + j
                if j == 8:
                    pe.wait_ge(ys_lo, 1)
                wait_bank(n)
                wait_split(0, h)
                prod_a(0, h, act8b if 8 <= j < 16 else act8a, 0, 8, ps[bank_of(n)], True, True,
                       last_head if j == 0 else None)
                if j == 2:
                    s5_out(HEADS - 1, 1, 1)
            for j in range(KD):
                wait_bank(N_S5O + j)
                wait_split(0, H_S5O + j)
                if j == 0:
                    pe.wait_ge(glu_lo, KS)
                prod_a(0, H_S5O + j, act8b, 0, 8, ps[bank_of(N_S5O + j)], True, True)
            for j in range(32):
                n = N_WO + 2 * (j // 8)
                if j % 8 == 0:
                    wait_bank(n)
                    wait_bank(n + 1)
                wait_split(0, H_WO + j)
                if j < 8:
                    pe.wait_ge(mix_lo, 2 * j + 2)
                prod_b(H_WO + j, act16, 2 * (j % 8), [ps[bank_of(n)], ps[bank_of(n + 1)]], j % 8 == 0, j % 8 == 7)
            def h_rows(g):
                pe.wait_ge(norm_ready, 2 * (g // 2) + 2)
                if g < 4:
                    pe.wait_ge(res_added, 8)
                else:
                    pe.wait_ge(hT_hi, g - 3)
                for e in range(2):
                    for t in range(TT):
                        mm = pe.transpose(ps[4 + g % 4][:, e * T + t * P:e * T + (t + 1) * P],
                                          hp[:, t, (2 * g + e) * P:(2 * g + e + 1) * P], ident[:, :])
                mm.then_inc(hT_psum, 1)

            def h_split(kt):
                if kt % 2 == 0:
                    pe.wait_ge(hT_lo, kt // 2 + 1)
                    if kt < 8:
                        h_rows(4 + kt // 2)

            for g in range(4):
                h_rows(g)
            for c, (o, h) in enumerate(FF_ORDER):
                if h == 0:
                    wait_bank(N_FF + o)
                wait_split(0, H_FF + c)
                prod_a(0, H_FF + c, act16, 8 * h, 8, ps[bank_of(N_FF + o)], h == 0, h == 1,
                       h_split if o == 0 else None)

            def ff(m, count=3):
                for i in range(count):
                    for q in range(4):
                        n = N_FF + 2 * i + q // 2
                        if q % 2 == 0:
                            pe.wait_ge(g_silu if q == 0 else mid_ready, 3 * m + (i - 2))
                        wait_split(m, H_FF + 4 * i + q)
                        prod_a(m, H_FF + 4 * i + q, act16, 8 * (q % 2), 8, ps[bank_of(n)], q % 2 == 0, q % 2 == 1)

            with pe.Fori(1, KF // 3) as m:
                ff(m)
            ff(KF // 3, KF % 3)
            for j in range(4 * (KF // 2)):
                b, i = divmod(j, KF // 2)
                n = N_DN + 2 * b
                if i == 0:
                    wait_bank(n)
                    wait_bank(n + 1)
                wait_split(0, H_DN + j)
                if b == 0:
                    pe.wait_ge(mid_lo, 2 * i + 2)
                prod_b(H_DN + j, mid, 2 * i, [ps[bank_of(n)], ps[bank_of(n + 1)]], i == 0, i == KF // 2 - 1)


def kernel(**inputs):
    import concourse.bacc as bacc
    from concourse.bass_utils import run_bass_kernel_spmd

    a = {n: np.asarray(v) for n, v in inputs.items()}
    w = a["w_in"][0]

    def kind_a(m):
        k, n = m.shape
        return m.reshape(k // 1024, 8, P, n // P, P).transpose(3, 0, 2, 1, 4).reshape(-1, P, HC)

    def kind_b(m):
        k, n = m.shape
        return m.reshape(k // 256, 2, P, n // 512, 512).transpose(3, 0, 2, 1, 4).reshape(-1, P, HC)

    q, k, v, u, g1, g2 = np.split(w, [NW, 2 * NW, 3 * NW, 3 * NW + SW, 3 * NW + SW + D], axis=1)
    qa, ka = kind_a(q).reshape(8, 2, P, HC), kind_a(k).reshape(8, 2, P, HC)
    g1a, g2a = kind_a(g1).reshape(8, 4, P, HC), kind_a(g2).reshape(8, 4, P, HC)
    loop = np.concatenate([qa, ka, g1a, g2a], axis=1).reshape(-1, P, HC)
    na = kind_a(a["w_na_out"][0])
    ff = np.concatenate([kind_a(a["w_ffn_gate"][0]).reshape(KF, 2, P, HC),
                         kind_a(a["w_ffn_up"][0]).reshape(KF, 2, P, HC)], axis=1).reshape(-1, P, HC)
    ff[0:12] = ff[[2 * n + h for n, h in FF_ORDER]]
    wstream = np.concatenate([kind_a(u)[[2 * n + h for n, h in U_ORDER]], kind_b(v), loop, na[:8], kind_a(a["w_glu"][0]), na[8:],
                              kind_a(a["w_s5_out"][0]), kind_b(a["w_out"][0]), ff, kind_b(a["w_ffn_down"][0])])

    x = a["x"][0]
    xT = x.T.reshape(KD, P, T).transpose(1, 0, 2)

    def states(m):
        return m.reshape(2, KS, 4, 2, NS).transpose(3, 4, 1, 0, 2).reshape(P, GROUPS)

    log_dt = np.broadcast_to(a["s5_log_dt"][0][:, :, None], (2, GROUPS, NS))
    params = np.stack([states(a["s5_a_re"][0]), states(a["s5_a_im"][0]), states(log_dt)], axis=1)
    pack = np.zeros((KS, P, PACK), np.float32)
    for ri, name in enumerate(("s5_b_re", "s5_b_im")):
        b = a[name][0].reshape(2, KS, 4, 2, NS, GC)
        for g in range(2):
            dst = pack[:, :, 0:512].reshape(KS, 4, 2, GC, 2, 2, 2, NS)
            dst[:, :, g, :, :, ri, g, :] = b[:, :, :, g].transpose(1, 2, 4, 0, 3)
            pack[:, :, 0:512] = dst.reshape(KS, P, 512)
    for ri, name in enumerate(("s5_c_re", "s5_c_im")):
        c = a[name][0].reshape(2, KS, 4, 2, GC, NS)
        dst = pack[:, :, 512:1024].reshape(KS, 2, NS, 2, 4, 2, 2, GC)
        for g in range(2):
            dst[:, g, :, :, :, ri, g, :] = c[:, :, :, g].transpose(1, 4, 0, 2, 3)
        pack[:, :, 512:1024] = dst.reshape(KS, P, 512)
    pack[:, :, 1024] = a["s5_d"][0].reshape(KS, P)

    rpb = np.pad(a["na_rpb"][0], ((0, 0), (0, 0), (GRID_W - WIN, GRID_W - WIN)))
    slide = np.lib.stride_tricks.sliding_window_view(rpb, GRID_W, axis=2)[:, :, ::-1]
    bias = np.empty((HEADS, 2, GRID_W, TT, ROWS, GRID_W), np.float32)
    for t in range(TT):
        for rl in range(2):
            for i in range(ROWS):
                bias[:, rl, :, t, i, :] = slide[:, i - (2 * t + rl) + 7]
    bias = bias.reshape(HEADS, P, TT * T)

    cols = np.concatenate([a["b_gate"][0].reshape(32, P), a["b_glu"][0].reshape(8, P), a["ln1_g"][0].reshape(KD, P),
                           a["ln1_b"][0].reshape(KD, P)]).T
    lnrows = np.stack([a["ln1_g"][0], a["ln1_b"][0], a["ln2_g"][0], a["ln2_b"][0]])

    arrays = {"wstream": wstream, "xT": xT, "xtok": x, "pack": pack, "params": params, "bias": bias, "cols": cols,
              "lnrows": lnrows}
    arrays = {n: np.ascontiguousarray(v) for n, v in arrays.items()}
    nc = bacc.Bacc("TRN2", target_bir_lowering=False, num_devices=1)
    args = {n: nc.dram_tensor(n, v.shape, F32, kind="ExternalInput").ap() for n, v in arrays.items()}
    out = nc.dram_tensor("out", (T, D), F32, kind="ExternalOutput").ap()
    build(nc, out=out, **args)
    r = run_bass_kernel_spmd(nc, [arrays], core_ids=[0])
    return r.results[0]["out"].reshape(1, T, D)
```

```python
from contextlib import ExitStack

import numpy as np

import concourse.bass as bass
from concourse import mybir

F32 = mybir.dt.float32
F32R = mybir.dt.float32r
I32 = mybir.dt.int32
ALU = mybir.AluOpType
ACT = mybir.ActivationFunctionType
AX = mybir.AxisListType

P = 128
T = 256
TT = T // P
D = 2048
KD = D // P
HEADS = 8
DH = 128
GRID_W = 64
ROWS = T // GRID_W
NA_ROWS = 8
WIN = 16
NW = HEADS * DH
SW = 1024
KS = SW // P
GROUPS = 64
GC = 16
NS = 64
DFF = 5632
KF = DFF // P
EPS = 1e-5
ALPHA = 2.0 ** 0.25
SCALE = DH ** -0.5

X_TO_W = {0: 0, 3: 1, 5: 2, 7: 3}
Y_SLOT = 7
LAG_P = 3
LAG = 2
XP = 8
HC = 1024
RAW = 4
SPL = 3
PER_F = 12
TILES = 8
AT = 8
BT = 16
BASE = 3 * AT + 2 * BT + 4
O_A, O_B, O_R, O_KR, O_KI, O_NKI = 0, 3 * AT, BASE - 4, BASE - 3, BASE - 2, BASE - 1

H_U = 0
H_V = H_U + 2 * KS
H_LOOP = H_V + 2 * KS
H_NA1 = H_LOOP + PER_F * HEADS
H_GLU = H_NA1 + 8
H_NA2 = H_GLU + 8
H_S5O = H_NA2 + 8
H_WO = H_S5O + KD
H_FF = H_WO + 4 * (KD // 2)
H_DN = H_FF + 4 * KF
H_END = H_DN + 4 * (KF // 2)

N_U, N_V, N_LOOP = 0, 8, 12
N_NA1 = N_LOOP + 6 * HEADS
N_GLU, N_NA2, N_S5O = N_NA1 + 8, N_NA1 + 16, N_NA1 + 24
N_WO = N_S5O + KD
N_FF = N_WO + 8
N_DN = N_FF + 2 * KF

U_ORDER = [(0, 0), (1, 0), (2, 0), (0, 1), (1, 1), (2, 1)] + [(n, h) for n in range(3, KS) for h in range(2)]
FF_ORDER = [(0, 0), (1, 0), (2, 0), (3, 0), (0, 1), (1, 1), (2, 1), (3, 1), (4, 0), (4, 1), (5, 0), (5, 1)]

LN2_DVE, LN2_POOL = [0, 1, 2, 4, 5], [3, 6, 7]
LN2_STORES = [0, 3, 1, 2, 6, 4, 7, 5]

U_EVAC = [i + LAG for i, (_, h) in enumerate(U_ORDER) if h == 1]

EXP_C = [1 / 2, 1 / 6, 1 / 24, 1 / 120, 1 / 720, 1 / 5040]
SIN_C = [-1 / 6, 1 / 120, -1 / 5040, 1 / 362880, -1 / 39916800, 1 / 6227020800]
COS_C = [-1 / 2, 1 / 24, -1 / 720, 1 / 40320, -1 / 3628800, 1 / 479001600]
MAGIC = 12582912.0
LN2_HI, LN2_LO = 0.693359375, -2.12194440e-4
TWO_PI = [6.28125, 0.0019340515136718750, 1.2556659146753e-06]

BU_SLOT = [0, 1, 3, 4, 5, 7, 8, 9]


def build(nc, wstream, xT, xtok, b_rows, c_rows, params, bias, cols, lnrows, out):
    ctx = ExitStack()
    with ctx:
        B0 = (nc.sbuf_base + 63) // 32 * 32

        def at(name, shape, dt, kb):
            return nc.alloc_sbuf_tensor_at(name, shape, dt, offset=B0 + int(kb * 1024))

        def sem(name):
            return ctx.enter_context(nc.semaphore(name))

        raw = at("raw", [P, RAW, HC], F32, 0)
        whi = at("whi", [P, SPL, HC], F32R, 16)
        wlo = at("wlo", [P, SPL, HC], F32R, 28)
        act16 = at("act16", [P, KD, 2, T], F32R, 40)
        ident = at("ident", [P, P], F32, 72)
        col = at("col", [P, 80], F32, 72.75)
        stats = at("stats", [P, TT, 4, 6], F32, 73.125)
        lnm = at("lnm", [P, TT, 6], F32, 73.375)
        eps1 = at("eps1", [P, 1], F32, 73.75)
        act8a = at("act8a", [P, KS, 2, T], F32R, 74)
        u = at("u", [P, KS, T], F32, 90)
        ga = at("ga", [P, KD, T], F32, 98)
        gs = at("gs", [P, KD, T], F32, 114)
        xraw = at("xraw", [P, KD, T], F32, 98)
        cm_all = at("cm_all", [P, KS, 3, TILES, 32], F32, 98)
        vout = at("vout", [P, TT, 512], F32, 122)
        ctmp = at("ctmp", [P, 2, 2 * TILES, 32], F32, 126)
        b_all = at("b_all", [P, KS, 512], F32, 74)
        b_lo_all = at("b_lo_all", [P, KS, 512], F32R, 74)
        b_hi_all = at("b_hi_all", [P, KS, 512], F32R, 133.75)
        u_all = at("u_all", [P, KS, 2, T], F32R, 149.75)
        c_all = at("c_all", [P, KS, 512], F32, 165.75)
        scratch = at("scratch", [P, 32, GROUPS], F32, 181.75)
        base_all = at("base_all", [P, GROUPS, BASE], F32, 190)
        base = at("base", [P, 2, TILES, BASE], F32, 130)
        b3 = at("b3", [P, 2, 4, 256], F32R, 133.75)
        u3 = at("u3", [P, 2, 4, T], F32R, 141.75)
        b3_f32 = at("b3_f32", [P, 2, 4, 256], F32, 133.75)
        u3_f32 = at("u3_f32", [P, 2, 4, T], F32, 141.75)
        cmat = at("cmat", [P, 2, 3, TILES, 32], F32, 149.75)
        vcur = at("vcur", [P, 2, TT, DH], F32, 155.75)
        qk = at("qk", [P, 2, 2, T], F32, 157.75)
        bm = at("bm", [P, 2, TT, T], F32, 161.75)
        S = at("S", [P, TT, T], F32, 165.75)
        PT = at("PT", [P, TT, T], F32, 167.75)
        sm = at("sm", [P, 4, TT], F32, 169.75)
        E = at("E", [P, 4, 2, T], F32, 170)
        tt12 = at("tt12", [P, 2, 2, P], F32, 178)
        m12 = at("m12", [P, 2, 2, T], F32, 180)
        wz = at("wz", [P, 2, T], F32, 184)
        z = at("z", [P, 2, 2, T], F32, 186)
        prod = at("prod", [P, 4, 4, T], F32, 190)
        fin_t = at("fin_t", [P, T], F32, 206)
        act8b = at("act8b", [P, KS, 2, T], F32R, 130)
        mid = at("mid", [P, KF, 2, T], F32R, 74)
        hp = at("hp", [P, TT, D], F32, 162)
        lnrow = at("lnrow", [P, 2, D], F32, 178)
        ev = at("ev", [P, 4, T], F32, 194)
        ev2 = at("ev2", [P, 4, T], F32, 198)
        hT = at("hT", [P, 2, 2, T], F32, 202)

        ps = [ctx.enter_context(nc.psum_tensor(f"bank{i}", [P, 512], F32)) for i in range(8)]
        BU0, YB, AB, TB = 3, 5, 6, 7

        base_dram = nc.dram_tensor("base_dram", [P, GROUPS, BASE], F32, kind="Internal").ap()
        b_dram = nc.dram_tensor("b_dram", [P, KS, 2, 512], F32, kind="Internal").ap()
        u_dram = nc.dram_tensor("u_dram", [P, KS, 2, T], F32, kind="Internal").ap()
        cm_dram = nc.dram_tensor("cm_dram", [P, KS, 3 * TILES * 32], F32, kind="Internal").ap()
        v_dram = nc.dram_tensor("v_dram", [T, NW], F32, kind="Internal").ap()

        raw_landed = [sem(f"raw_landed{i}") for i in range(RAW)]
        hi_ready, lo_ready, w_used = sem("hi_ready"), sem("lo_ready"), sem("w_used")
        uv_copied, loop_copied, res_added = sem("uv_copied"), sem("loop_copied"), sem("res_added")
        x_landed = [sem(f"x_landed{i}") for i in range(XP)]
        x_hi, x_lo = sem("x_hi"), sem("x_lo")
        col_landed, par_landed = sem("col_landed"), sem("par_landed")
        const_step = sem("const_step")
        par_step, par_done, tab_step, base_stored = sem("par_step"), sem("par_done"), sem("tab_step"), sem("base_stored")
        v_stored = [sem("v_stored0"), sem("v_stored1")]
        b_landed, b_hi, b_lo, b_stored = [sem(f"b_landed{i}") for i in range(4)], sem("b_hi"), sem("b_lo"), sem("b_stored")
        u_hi, u_lo, u_stored = sem("u_hi"), sem("u_lo"), sem("u_stored")
        c_landed, cm_step, cm_neg, cm_stored = [sem(f"c_landed{i}") for i in range(4)], sem("cm_step"), sem("cm_neg"), sem("cm_stored")
        cm_staged, u3_staged = [sem("cm_staged0"), sem("cm_staged1")], [sem("u3_staged0"), sem("u3_staged1")]
        u3_ready, b3_ready = sem("u3_ready"), sem("b3_ready")
        b3_staged = [sem("b3_staged_fwd"), sem("b3_staged_bwd")]
        base_staged = [sem("base_staged0"), sem("base_staged1")]
        v_staged = [sem("v_staged0"), sem("v_staged1")]
        bias_staged = [sem("bias_staged0"), sem("bias_staged1")]
        bu_ready, bu_read = sem("bu_ready"), sem("bu_read")
        w_turned, z_ready = sem("w_turned"), sem("z_ready")
        tab_prod, tab_half, tab_ready = sem("tab_prod"), sem("tab_half"), sem("tab_ready")
        prod_ready, y_done, fin_step = sem("prod_ready"), sem("y_done"), sem("fin_step")
        sc_ready, soft_step, exp_ready, sum_inv = sem("sc_ready"), sem("soft_step"), sem("exp_ready"), sem("sum_inv")
        p_ready, tr_ready, pt_ready, pv_done = sem("p_ready"), sem("tr_ready"), sem("pt_ready"), sem("pv_done")
        att_hi, att_lo = sem("att_hi"), sem("att_lo")
        gelu_done, ys_hi, ys_lo = sem("gelu_done"), sem("ys_hi"), sem("ys_lo")
        ga_sig, gs_sig, na_gated = sem("ga_sig"), sem("gs_sig"), sem("na_gated")
        glu_sig, glu_y, glu_hi, glu_lo = (sem(n) for n in ("glu_sig", "glu_y", "glu_hi", "glu_lo"))
        so_gated, mix_ready, mix_hi, mix_lo = sem("so_gated"), sem("mix_ready"), sem("mix_hi"), sem("mix_lo")
        xtok_landed, ln1_landed, ln2_landed = sem("xtok_landed"), sem("ln1_landed"), sem("ln2_landed")
        stat_ready, sqrt_loaded, var_ready, sd_ready, ln_step, norm_ready = (
            sem(n) for n in ("stat_ready", "sqrt_loaded", "var_ready", "sd_ready", "ln_step", "norm_ready"))
        hT_psum, hT_f32, hT_hi, hT_lo, h_step = (sem(n) for n in ("hT_psum", "hT_f32", "hT_hi", "hT_lo", "h_step"))
        g_silu, mid_ready, mid_hi, mid_lo = (sem(n) for n in ("g_silu", "mid_ready", "mid_hi", "mid_lo"))
        ln2_norm, ln2_gain, ln2_mul = sem("ln2_norm"), sem("ln2_gain"), sem("ln2_mul")
        ln2_dve, ln2_pool, stored = sem("ln2_dve"), sem("ln2_pool"), sem("stored")

        block = ctx.enter_context(nc.Block())

        def bank_of(n):
            if n < N_V:
                return n
            if n < N_LOOP:
                return (5, 6, 7, 2)[n - N_V]
            if n < N_NA1:
                return n % 3
            if n < N_WO:
                return (0, 1, 2, 3, 4, 7)[(n - N_NA1) % 6]
            if n < N_FF:
                return (3 + n - N_WO) % 8
            if n < N_DN:
                return (n - N_FF) % 6
            return (6 + n - N_DN) % 8

        def bank_before(n):
            return next((o for o in range(n - 1, -1, -1) if bank_of(o) == bank_of(n)), None)

        def taken(n):
            if n < N_LOOP:
                return uv_copied, n + 1
            if n < N_NA1:
                return loop_copied, n - N_LOOP + 1
            if n < N_GLU:
                return na_gated, n - N_NA1 + 1
            if n < N_NA2:
                return glu_sig, n - N_GLU + 1
            if n < N_S5O:
                return na_gated, n - N_NA2 + 9
            if n < N_WO:
                return so_gated, n - N_S5O + 1
            if n < N_FF:
                return res_added, n - N_WO + 1
            if n < N_DN:
                return (g_silu, mid_ready)[(n - N_FF) % 2], (n - N_FF) // 2 + 1
            return res_added, 8 + n - N_DN + 1

        @block.sync
        def _(sp):
            def load(m, c):
                if not (isinstance(m, int) and 12 * m + c < RAW):
                    sp.wait_ge(lo_ready, 12 * m + (c - RAW + 1))
                sp.dma_start(raw[:, c % RAW, :], wstream[bass.ds(12 * m + c, 1), :, :].rearrange("o p n -> p (o n)")
                             ).then_inc(raw_landed[c % RAW], 16)

            def stage_u(f, p):
                for r, h in enumerate((0, 1, 0)):
                    sp.dma_start(u3_f32[32 * r:32 * r + 32, p, :, :], u_dram[:, bass.ds(f, 1), h, :]
                                 .rearrange("(q p) o n -> p q (o n)", p=32)).then_inc(u3_staged[p], 16)

            def stage(f, p):
                sp.dma_start(cmat[:, p, :, :, :].rearrange("p a b c -> p (a b c)"), cm_dram[:, bass.ds(f, 1), :]
                             .rearrange("p o n -> p (o n)")).then_inc(cm_staged[p], 16)
                sp.dma_start(bm[:, p, :, :], bias[bass.ds(f, 1), :, :].rearrange("o p (t n) -> p (o t) n", t=TT)
                             ).then_inc(bias_staged[p], 16)
                if not (isinstance(f, int) and f < 2):
                    sp.dma_start(base[:, p, :, :], base_dram[:, bass.ds(TILES * f, TILES), :]).then_inc(base_staged[p], 16)
                    sp.dma_start(vcur[:, p, :, :], v_dram[:, bass.ds(DH * f, DH)].rearrange("(t p) n -> p t n", p=P)
                                 ).then_inc(v_staged[p], 16)

            def stage_b(f, d):
                for r, h in enumerate((0, 0, 1)):
                    sp.dma_start(b3_f32[32 * r:32 * r + 32, d, :, :], b_dram[:, bass.ds(f, 1), h, 256 * d:256 * d + 256]
                                 .rearrange("(q p) o n -> p q (o n)", p=32)).then_inc(b3_staged[d], 16)

            for i in range(XP):
                sp.dma_start(xraw[:, 2 * i:2 * i + 2, :], xT[:, 2 * i:2 * i + 2, :]).then_inc(x_landed[i], 16)
                if i in X_TO_W:
                    load(0, X_TO_W[i])
            sp.dma_start(col[:, :], cols).then_inc(col_landed, 16)
            for c in range(RAW, H_LOOP):
                load(0, c)
                if c in (4, 6, 8, 10):
                    g = (c - 4) // 2
                    sp.dma_start(b_all[:, 2 * g:2 * g + 2, :], b_rows[:, 2 * g:2 * g + 2, :]).then_inc(b_landed[g], 16)
                if c in (12, 14, 16, 18):
                    g = (c - 12) // 2
                    sp.dma_start(c_all[:, 2 * g:2 * g + 2, :], c_rows[:, 2 * g:2 * g + 2, :]).then_inc(c_landed[g], 16)
                if c == 27:
                    sp.wait_ge(b_stored, 16 * KS)
                    sp.wait_ge(u_stored, 16 * KS)
                    stage_b(0, 0)
                    stage_u(0, 0)
                if c == 29:
                    stage_b(0, 1)

            def passes(k, last):
                for p in range(2):
                    for j in range(PER_F):
                        first = p == 0 and isinstance(k, int) and k == 0
                        if j == 3 and first:
                            sp.wait_ge(cm_stored, 16 * (KS // 2))
                            sp.wait_ge(base_stored, 16)
                            stage(0, 0)
                        if j == 2 and not first:
                            sp.wait_ge(bu_ready, TILES * (2 * k + p))
                            stage_b(2 * k + p, 1)
                        if j == 10 and not (p == 1 and last):
                            if not first:
                                sp.wait_ge(fin_step, 2 * (2 * k + p))
                                sp.wait_ge(att_lo, 2 * k + p)
                            stage_u(2 * k + p + 1, 1 - p)
                            stage(2 * k + p + 1, 1 - p)
                        if j == 11 and not (p == 1 and last):
                            sp.wait_ge(bu_ready, TILES * (2 * k + p) + 4)
                            stage_b(2 * k + p + 1, 0)
                        load(2 * k, H_LOOP + PER_F * p + j)

            passes(0, False)
            with sp.Fori(1, HEADS // 2 - 1) as k:
                passes(k, False)
            passes(HEADS // 2 - 1, True)

            for c in range(H_NA1, H_S5O + KD):
                if c == H_S5O:
                    sp.wait_ge(ys_lo, 1)
                if c in (H_S5O, H_S5O + 2, H_S5O + 4, H_S5O + 6):
                    b = slice(256 * (c - H_S5O), 256 * (c - H_S5O) + 512)
                    sp.dma_start(hp[:, :, b], xtok[:, b].rearrange("(t p) n -> p t n", p=P)).then_inc(xtok_landed, 16)
                if c in (H_S5O + 8, H_S5O + 11):
                    n = (c - H_S5O - 8) // 3
                    sp.dma_start(lnrow[:, n, :], lnrows[n:n + 1, :].to_broadcast([P, D])).then_inc(ln1_landed, 16)
                load(0, c)
            for c in range(H_WO, H_FF + 4):
                load(0, c)
            n0 = (H_END - H_FF - 4) // 12
            c0 = H_FF + 4
            with sp.Fori(0, n0 // 2) as m:
                for c in range(c0, c0 + 12):
                    load(m, c)
            sp.wait_ge(h_step, 4)
            for r in range(2):
                sp.dma_start(lnrow[:, r, :], lnrows[2 + r:3 + r, :].to_broadcast([P, D])).then_inc(ln2_landed, 16)
            with sp.Fori(n0 // 2, n0) as m:
                for c in range(c0, c0 + 12):
                    load(m, c)
            for c in range(c0 + 12 * n0, H_END):
                load(0, c)
            for i in LN2_STORES:
                if i in LN2_DVE:
                    sp.wait_ge(ln2_dve, LN2_DVE.index(i) + 1)
                else:
                    sp.wait_ge(ln2_pool, LN2_POOL.index(i) + 1)
                t, b = i // 4, slice(i % 4 * 512, i % 4 * 512 + 512)
                sp.dma_start(out[t * P:(t + 1) * P, b], hp[:, t, b]).then_inc(stored, 16)
            sp.wait_ge(stored, 16 * len(LN2_STORES))

        @block.gpsimd
        def _(pool):
            pool.memset(ident[:, :], 0.0).then_inc(const_step, 1)
            pool.memset(eps1[:, :], EPS).then_inc(const_step, 1)
            pool.wait_ge(const_step, 2)
            pool.affine_select(out=ident[:, :], in_=ident[:, :], compare_op=ALU.not_equal, fill=1.0, base=0,
                               pattern=[[-1, P]], channel_multiplier=1).then_inc(const_step, 1)

            pool.dma_start(scratch[:, 0:3, :], params).then_inc(par_landed, 16)
            for n in range(KS):
                pool.wait_ge(b_hi, n + 1)
                pool.tensor_tensor(b_lo_all[:, n, :], b_all[:, n, :], b_hi_all[:, n, :].bitcast(F32), ALU.subtract
                                   ).then_inc(b_lo, 1)
            pool.wait_ge(par_done, 1)
            done = [0]

            def step(ins):
                ins.then_inc(tab_step, 1)
                done[0] += 1
                pool.wait_ge(tab_step, done[0])

            def tt(o, a, b, op):
                step(pool.tensor_tensor(o, a, b, op))

            q1 = [scratch[:, 22 + i, :].rearrange("p (g o) -> p g o", o=1) for i in range(2)]
            big = [scratch[:, 24 + 4 * i:28 + 4 * i, :].rearrange("p a b -> p (a b)") for i in range(2)]

            def cmul(ore, oim, are, aim, bre, bim, n):
                t1, t2 = (b[:, 0:GROUPS * min(n, 4)].rearrange("p (g n) -> p g n", n=min(n, 4)) for b in big)
                for s in range(0, n, 4):
                    e = min(n, s + 4)
                    sl = lambda a: a[:, :, s:e]
                    bb = [b.to_broadcast([P, GROUPS, e - s]) for b in (bre, bim)]
                    tt(t1, sl(are), bb[0], ALU.mult)
                    tt(t2, sl(aim), bb[1], ALU.mult)
                    tt(sl(ore), t1, t2, ALU.subtract)
                    tt(t1, sl(are), bb[1], ALU.mult)
                    tt(t2, sl(aim), bb[0], ALU.mult)
                    tt(sl(oim), t1, t2, ALU.add)

            def square():
                t1 = big[0][:, 0:GROUPS].rearrange("p (g o) -> p g o", o=1)
                t2 = big[1][:, 0:GROUPS].rearrange("p (g o) -> p g o", o=1)
                tt(t1, q1[1], q1[1], ALU.mult)
                tt(t2, q1[0], q1[1], ALU.mult)
                tt(t2, t2, t2, ALU.add)
                tt(q1[0], q1[0], q1[0], ALU.mult)
                tt(q1[0], q1[0], t1, ALU.subtract)
                step(pool.tensor_copy(q1[1], t2))

            bc = base_all[:, :, O_B:O_B + BT]
            bs = base_all[:, :, O_B + BT:O_B + 2 * BT]
            ac = base_all[:, :, O_A + AT:O_A + 2 * AT]
            as_ = base_all[:, :, O_A + 2 * AT:O_A + 3 * AT]
            ans = base_all[:, :, O_A:O_A + AT]
            step(pool.tensor_copy(q1[0], bc[:, :, 1:2]))
            step(pool.tensor_copy(q1[1], bs[:, :, 1:2]))
            n = 2
            while n < BT:
                square()
                cmul(bc[:, :, n:2 * n], bs[:, :, n:2 * n], bc[:, :, 0:n], bs[:, :, 0:n], q1[0], q1[1], n)
                n *= 2
            square()
            n = 1
            while n < AT:
                cmul(ac[:, :, n:2 * n], as_[:, :, n:2 * n], ac[:, :, 0:n], as_[:, :, 0:n], q1[0], q1[1], n)
                n *= 2
                if n < AT:
                    square()
            step(pool.tensor_scalar(ans, as_, -1.0, None, ALU.mult))
            pool.dma_start(base_dram, base_all[:, :, :]).then_inc(base_stored, 16)
            for f in range(2):
                step(pool.tensor_copy(base[:, f, :, :], base_all[:, TILES * f:TILES * f + TILES, :]))

            def table(f, p, i):
                s = TILES * f + i
                row = base[:, p, i, :]
                a = [row[:, O_A + AT * j:O_A + AT * j + 2 * AT].rearrange("p (c a o) -> p c a o", c=2, o=1)
                     .to_broadcast([P, 2, AT, BT]) for j in (1, 0)]
                for j in range(2):
                    b = row[:, O_B + BT * j:O_B + BT * j + BT].rearrange("p (c a b) -> p c a b", c=1, a=1)
                    pool.tensor_tensor(tt12[:, j, :, :].rearrange("p c (a b) -> p c a b", b=BT), a[j],
                                       b.to_broadcast([P, 2, AT, BT]), ALU.mult).then_inc(tab_prod, 1)
                pool.wait_ge(tab_prod, 2 * s + 2)
                pool.tensor_tensor(E[:, i % 4, :, P:T], tt12[:, 0, :, :], tt12[:, 1, :, :], ALU.add).then_inc(tab_half, 1)
                pool.wait_ge(tab_half, s + 1)

            def products(f, p, i):
                s = TILES * f + i
                if isinstance(s, int) and s == 0:
                    pool.wait_ge(base_stored, 16)
                pool.wait_ge(z_ready, 2 * s + 2)
                if i >= 4 or not (isinstance(f, int) and f == 0):
                    pool.wait_ge(y_done, 2 * f + i // 4)
                zc, e, o = z[:, i % 2, :, :], E[:, i % 4, :, :], prod[:, i % 4, :, :]
                for j in range(2):
                    pool.tensor_tensor(o[:, 2 * j:2 * j + 2, :], zc, e[:, j:j + 1, :].to_broadcast([P, 2, T]), ALU.mult
                                       ).then_inc(prod_ready, 1)
                pool.wait_ge(prod_ready, 2 * s + 2)

            def one_pass(k, p, last=False):
                f = 2 * k + p
                kn, pn = (k + 1, 0) if p else (k, 1)
                for i in range(TILES):
                    if i + 2 < TILES:
                        table(f, p, i + 2)
                    elif not last:
                        if i + 2 == TILES and not (isinstance(kn, int) and kn == 0):
                            pool.wait_ge(base_staged[pn], 16 * kn)
                        table(2 * kn + pn, pn, i + 2 - TILES)
                    products(f, p, i)

            pool.wait_ge(cm_step, 24)
            table(0, 0, 0)
            table(0, 0, 1)
            one_pass(0, 0)
            one_pass(0, 1)
            with pool.Fori(1, HEADS // 2 - 1) as k:
                one_pass(k, 0)
                one_pass(k, 1)
            one_pass(HEADS // 2 - 1, 0)
            one_pass(HEADS // 2 - 1, 1, last=True)

            pool.wait_ge(ln1_landed, 32)
            pool.wait_ge(hT_psum, 8)
            for t in range(TT):
                pool.tensor_tensor(hp[:, t, :], hp[:, t, :], lnrow[:, 0, :], ALU.mult).then_inc(h_step, 1)
                pool.wait_ge(h_step, 2 * t + 1)
                pool.tensor_tensor(hp[:, t, :], hp[:, t, :], lnrow[:, 1, :], ALU.add).then_inc(h_step, 1)
            pool.wait_ge(ln2_landed, 32)
            for n, i in enumerate(LN2_POOL):
                v, b = hp[:, i // 4, i % 4 * 512:i % 4 * 512 + 512], slice(i % 4 * 512, i % 4 * 512 + 512)
                pool.wait_ge(ln2_norm, n + 1)
                pool.tensor_tensor(v, v, lnrow[:, 0, b], ALU.mult).then_inc(ln2_mul, 1)
                pool.wait_ge(ln2_mul, n + 1)
                pool.tensor_tensor(v, v, lnrow[:, 1, b], ALU.add).then_inc(ln2_pool, 1)

        @block.scalar
        def _(act):
            def split_hi(m, c):
                act.wait_ge(raw_landed[c % RAW], 48 * m + 16 * (c // RAW + 1))
                if not (isinstance(m, int) and 12 * m + c < SPL):
                    act.wait_ge(w_used, 12 * m + (c - SPL + 1))
                act.activation(whi[:, c % SPL, :], raw[:, c % RAW, :], ACT.Copy).then_inc(hi_ready, 1)

            def store_v(b):
                act.wait_ge(uv_copied, KS + 2 * b + 2)
                act.dma_start(v_dram[:, 512 * b:512 * b + 512].rearrange("(t p) n -> p t n", p=P), vout[:, :, :]
                              ).then_inc(v_stored[b], 16)

            for i in range(XP):
                act.wait_ge(x_landed[i], 16)
                act.activation(act16[:, 2 * i:2 * i + 2, 0, :], xraw[:, 2 * i:2 * i + 2, :], ACT.Copy).then_inc(x_hi, 1)
                if i in X_TO_W and X_TO_W[i] < 3:
                    split_hi(0, X_TO_W[i])
            for c in range(3, H_LOOP):
                split_hi(0, c)
                if 0 <= c - 7 < KS:
                    act.wait_ge(b_landed[(c - 7) // 2], 16)
                    act.activation(b_hi_all[:, c - 7, :], b_all[:, c - 7, :], ACT.Copy).then_inc(b_hi, 1)
                if c in (11, 13, 15, 17):
                    g = (c - 11) // 2
                    act.wait_ge(b_lo, 2 * g + 2)
                    for h, v in enumerate((b_hi_all, b_lo_all)):
                        act.dma_start(b_dram[:, 2 * g:2 * g + 2, h, :], v[:, 2 * g:2 * g + 2, :].bitcast(F32)
                                      ).then_inc(b_stored, 16)
                if c - 2 in U_EVAC:
                    t = U_EVAC.index(c - 2)
                    act.wait_ge(uv_copied, t + 1)
                    act.activation(u_all[:, t, 0, :], u[:, t, :], ACT.Copy).then_inc(u_hi, 1)
                if c - 4 in U_EVAC:
                    t = U_EVAC.index(c - 4)
                    act.wait_ge(u_lo, t + 1)
                    act.dma_start(u_dram[:, t, :, :], u_all[:, t, :, :].bitcast(F32)).then_inc(u_stored, 16)
                if c in (18, 21, 24, 27):
                    g = (c - 18) // 3
                    act.wait_ge(cm_step, 6 * g + 3)
                    act.activation(cm_all[:, 2 * g:2 * g + 2, 2, :, :], cm_all[:, 2 * g:2 * g + 2, 0, :, :], ACT.Copy,
                                   scale=-1.0).then_inc(cm_neg, 1)
                if c in (20, 23, 26, 29):
                    g = (c - 20) // 3
                    act.wait_ge(cm_step, 6 * g + 6)
                    act.wait_ge(cm_neg, g + 1)
                    act.dma_start(cm_dram[:, 2 * g:2 * g + 2, :],
                                  cm_all[:, 2 * g:2 * g + 2, :, :, :].rearrange("p f a b c -> p f (a b c)")
                                  ).then_inc(cm_stored, 16)
                if c == H_V + 12:
                    store_v(0)

            def ready_u(f, k, p):
                act.wait_ge(u3_staged[p], 48 * k + 48)
                act.activation(u3[0:96, p, :, :], u3_f32[0:96, p, :, :], ACT.Copy).then_inc(u3_ready, 1)

            def ready_b(f, d):
                act.wait_ge(b3_staged[d], 48 * f + 48)
                act.activation(b3[0:96, d, :, :], b3_f32[0:96, d, :, :], ACT.Copy).then_inc(b3_ready, 1)

            def stage_v01():
                for b in range(2):
                    act.wait_ge(v_stored[b], 16)
                for f in range(2):
                    act.dma_start(vcur[:, f, :, :], v_dram[:, DH * f:DH * f + DH].rearrange("(t p) n -> p t n", p=P)
                                  ).then_inc(v_staged[f], 16)

            def table_rev(k, p, i):
                s = TILES * (2 * k + p) + i
                act.wait_ge(tab_half, s + 1)
                act.activation(E[:, i % 4, 0, 0:P], E[:, i % 4, 0, T - 1:P - 1:-1], ACT.Copy).then_inc(tab_ready, 1)
                act.activation(E[:, i % 4, 1, 0:P], E[:, i % 4, 1, T - 1:P - 1:-1], ACT.Copy, scale=-1.0).then_inc(tab_ready, 1)

            def softmax_norm(k, p):
                f = 2 * k + p
                act.wait_ge(sum_inv, f + 1)
                for t in range(TT):
                    act.activation(S[:, t, :], S[:, t, :], ACT.Copy, scale=sm[:, 3, t:t + 1]).then_inc(p_ready, 1)

            def softmax_exp(k, p):
                f = 2 * k + p
                act.wait_ge(soft_step, 3 * f + 3)
                for t in range(TT):
                    act.activation(S[:, t, :], S[:, t, :], ACT.Exp, bias=sm[:, 1, t:t + 1],
                                   accum_out=sm[:, 2, t:t + 1]).then_inc(exp_ready, 1)

            def pt_copy(f):
                act.wait_ge(tr_ready, f + 1)
                if not (isinstance(f, int) and f == 0):
                    act.wait_ge(pv_done, f)
                act.activation(PT[:, :, :].rearrange("p t n -> p (t n)"), ps[TB][:, :], ACT.Copy).then_inc(pt_ready, 1)

            def attn_hi(f):
                act.wait_ge(pv_done, f + 1)
                act.activation(act8a[:, bass.ds(f, 1), 0, :], ps[AB][:, 0:T].rearrange("p (o n) -> p o n", o=1), ACT.Copy
                               ).then_inc(att_hi, 1)

            def loop_copy(k, p, o):
                f = 2 * k + p
                act.wait_ge(w_used, PER_F * f + (H_LOOP + 2 * o + 2))
                src = ps[bank_of(N_LOOP + o)][:, 0:T].rearrange("p (o n) -> p o n", o=1)
                if o < 2:
                    if not (isinstance(f, int) and f < 2):
                        act.wait_ge(sc_ready, f - 1)
                    dst = qk[:, p, o:o + 1, :]
                else:
                    g = ga if o < 4 else gs
                    dst = g[:, bass.ds(2 * f + o % 2, 1), :]
                act.activation(dst, src, ACT.Copy).then_inc(loop_copied, 1)

            def one_pass(k, p, first, last=False):
                c0 = H_LOOP + PER_F * p
                for j in range(PER_F):
                    split_hi(2 * k, c0 + j)
                    if j == 0 and first:
                        ready_b(0, 0)
                        ready_u(0, 0, 0)
                    if j == 2:
                        ready_b(2 * k + p, 1)
                    if j == 10 and not last:
                        ready_u(2 * k + p + 1, *((k + 1, 0) if p else (k, 1)))
                    if j == 11 and not last:
                        ready_b(2 * k + p + 1, 0)
                    if j == 1 and not first:
                        loop_copy(*((k, 0) if p else (k - 1, 1)), 5)
                    if j >= 1 + LAG and (j - 1 - LAG) % 2 == 0:
                        loop_copy(k, p, (j - 1 - LAG) // 2)
                    if j == 3 and first:
                        store_v(1)
                    if j == 7 and first:
                        stage_v01()
                    if j == 11:
                        pt_copy(2 * k + p)
                    if j == 1 and not first:
                        attn_hi(2 * k + p - 1)
                    if j == 8:
                        softmax_exp(k, p)
                    if j == 9:
                        softmax_norm(k, p)
                    for i in range(TILES):
                        if BU_SLOT[i] + LAG - 1 == j:
                            table_rev(k, p, i)

            act.wait_ge(u_stored, 16 * KS)
            one_pass(0, 0, True)
            one_pass(0, 1, False)
            with act.Fori(1, HEADS // 2 - 1) as k:
                one_pass(k, 0, False)
                one_pass(k, 1, False)
            one_pass(HEADS // 2 - 1, 0, False)
            one_pass(HEADS // 2 - 1, 1, False, last=True)

            act.wait_ge(col_landed, 16)
            loop_copy(HEADS // 2 - 1, 1, 5)
            for j in range(8):
                split_hi(0, H_NA1 + j)
                if j == 0:
                    attn_hi(HEADS - 1)
                if j == 5:
                    act.wait_ge(fin_step, 2 * KS)
                    uf = u[:, :, :]
                    act.activation(uf, uf, ACT.Gelu_apprx_tanh).then_inc(gelu_done, 1)
                    act.wait_ge(gelu_done, 1)
                    act.activation(act8b[:, :, 0, :], uf, ACT.Copy).then_inc(ys_hi, 1)
                if j < 4:
                    for t in (2 * j, 2 * j + 1):
                        g = ga[:, t, :]
                        act.activation(g, g, ACT.Sigmoid, bias=col[:, t:t + 1]).then_inc(ga_sig, 1)

            def glu_act(t):
                act.wait_ge(w_used, H_GLU + t + 1)
                if t >= 4:
                    act.wait_ge(glu_y, t - 3)
                act.activation(ev2[:, t % 4, :], ps[bank_of(N_GLU + t)][:, 0:T], ACT.Sigmoid, bias=col[:, 32 + t:33 + t]
                               ).then_inc(glu_sig, 1)

            def glu_split(t):
                act.wait_ge(glu_y, t + 1)
                act.activation(act8b[:, t, 0, :], u[:, t, :], ACT.Copy).then_inc(glu_hi, 1)

            def mix_split(t):
                act.wait_ge(mix_ready, t + 1)
                act.activation(act16[:, t, 0, :], ga[:, t, :], ACT.Copy).then_inc(mix_hi, 1)

            for j in range(8):
                split_hi(0, H_GLU + j)
                t = 8 + j
                act.activation(ga[:, t, :], ga[:, t, :], ACT.Sigmoid, bias=col[:, t:t + 1]).then_inc(ga_sig, 1)
                if j >= LAG_P:
                    glu_act(j - LAG_P)
            for j in range(8):
                split_hi(0, H_NA2 + j)
                if j < LAG_P:
                    glu_act(8 - LAG_P + j)
                if j == 3:
                    act.wait_ge(w_used, H_NA2)
                if 3 <= j < 7:
                    glu_split(2 * (j - 3))
                    glu_split(2 * (j - 3) + 1)
                for t in (2 * j, 2 * j + 1):
                    act.activation(gs[:, t, :], gs[:, t, :], ACT.Sigmoid, bias=col[:, 16 + t:17 + t]).then_inc(gs_sig, 1)
            for j in range(KD):
                split_hi(0, H_S5O + j)
                if j >= LAG_P + 1:
                    mix_split(j - LAG_P - 1)
            for j in range(32):
                split_hi(0, H_WO + j)
                if j < LAG_P + 1:
                    mix_split(KD - LAG_P - 1 + j)

            def sd(e):
                if e > 0:
                    act.wait_ge(sqrt_loaded, e)
                act.activation(lnm[:, 0, 5:6], eps1[:, :], ACT.Sqrt).then_inc(sqrt_loaded, 1)
                act.wait_ge(var_ready, 2 * e + 2)
                if e > 0:
                    act.wait_ge(ln_step, 2 * e)
                act.activation(lnm[:, :, 4:5], lnm[:, :, 1:2], ACT.Sqrt, bias=eps1[:, :]).then_inc(sd_ready, 1)

            def mid_split_hi(n, b):
                act.wait_ge(mid_ready, n + 1)
                act.activation(mid[:, bass.ds(n, 1), 0, :], ev2[:, b:b + 1, :], ACT.Copy).then_inc(mid_hi, 1)

            def gate(m, i, c):
                act.wait_ge(w_used, 12 * m + (H_FF + c + 1))
                if not isinstance(m, int) or m > 0:
                    act.wait_ge(mid_ready, 3 * m + i - 2)
                act.activation(ev[:, i, :], ps[bank_of(N_FF + 2 * i)][:, 0:T], ACT.Silu).then_inc(g_silu, 1)

            for c in range(3):
                split_hi(0, H_FF + c)
            act.wait_ge(const_step, 2)
            sd(0)
            for g in range(8):
                act.wait_ge(hT_psum, g + 1)
                if g >= 2:
                    act.wait_ge(hT_lo, g - 1)
                for e in range(2):
                    t = 2 * g + e
                    act.activation(hT[:, g % 2, e, :], ps[4 + g % 4][:, e * T:(e + 1) * T], ACT.Identity,
                                   scale=col[:, 40 + t:41 + t], bias=col[:, 56 + t:57 + t]).then_inc(hT_f32, 1)
                act.wait_ge(hT_f32, 2 * g + 2)
                act.activation(act16[:, 2 * g:2 * g + 2, 0, :], hT[:, g % 2, :, :], ACT.Copy).then_inc(hT_hi, 1)
                if g == 5:
                    split_hi(0, H_FF + 3)
            for c in range(4, 12):
                split_hi(0, H_FF + c)
                if c == 8:
                    mid_split_hi(0, 0)
                if c in (6, 8, 11):
                    gate(0, (c - 5) // 2 if c < 11 else 2, (4, 6, 9)[(c - 5) // 2 if c < 11 else 2])
                if c == 10:
                    mid_split_hi(1, 1)

            def ff(m, count=3):
                for i in range(count):
                    for q in range(4):
                        split_hi(m, H_FF + 4 * i + q)
                        if q == 2:
                            mid_split_hi(3 * m + i - 1, (i - 1) % 3)
                        if q == 3:
                            gate(m, i, 4 * i + 1)

            with act.Fori(1, KF // 3) as m:
                ff(m)
            ff(KF // 3, KF % 3)
            for c in range(4):
                split_hi(0, H_DN + c)
                if c == 2:
                    mid_split_hi(KF - 1, (KF - 1) % 3)
            with act.Fori(0, (H_END - H_DN - 4) // 12) as m:
                for c in range(12):
                    split_hi(m, H_DN + 4 + c)
            sd(1)
            act.wait_ge(ln_step, 4)
            for i in LN2_POOL:
                t = i // 4
                v = hp[:, t, i % 4 * 512:i % 4 * 512 + 512]
                act.activation(v, v, ACT.Identity, scale=lnm[:, t, 2:3], bias=lnm[:, t, 3:4]).then_inc(ln2_norm, 1)

        @block.vector
        def _(dve):
            def split_lo(m, c):
                dve.wait_ge(hi_ready, 12 * m + (c + 1))
                dve.tensor_tensor(wlo[:, c % SPL, :], raw[:, c % RAW, :], whi[:, c % SPL, :].bitcast(F32), ALU.subtract
                                  ).then_inc(lo_ready, 1)

            def low(o, full, hi, s):
                dve.tensor_tensor(o, full, hi.bitcast(F32), ALU.subtract).then_inc(s, 1)

            done = [0]

            def step(ins):
                ins.then_inc(par_step, 1)
                done[0] += 1
                dve.wait_ge(par_step, done[0])

            (ARE, AIM, DT, X, Y, NI, RR, EM, EX, H1, H2, SH, CH, CY, SY, KR, KI, T0, T1, T2, P0, P1) = (
                scratch[:, i, :] for i in range(22))

            def ts(o, a, s1, s2, *ops):
                step(dve.tensor_scalar(o, a, s1, s2, *ops))

            def tt(o, a, b, op):
                step(dve.tensor_tensor(o, a, b, op))

            def stt(o, a, s, b, op0, op1):
                step(dve.scalar_tensor_tensor(out=o, in0=a, scalar=s, in1=b, op0=op0, op1=op1))

            def reduce_exp(v):
                ts(T0, v, -87.0, 88.5, ALU.max, ALU.min)
                ts(NI, T0, 1.4426950408889634, MAGIC, ALU.mult, ALU.add)
                ts(NI, NI, MAGIC, None, ALU.subtract)
                stt(RR, NI, -LN2_HI, T0, ALU.mult, ALU.add)
                stt(RR, NI, -LN2_LO, RR, ALU.mult, ALU.add)

            def expm1(o_em, o_ex):
                ts(P0, RR, EXP_C[-1], None, ALU.mult)
                for c in EXP_C[-2::-1]:
                    stt(P0, P0, c, RR, ALU.add, ALU.mult)
                stt(P0, P0, 1.0, RR, ALU.add, ALU.mult)
                ts(T1.bitcast(I32), NI, 127.0, 8388608.0, ALU.add, ALU.mult)
                if o_em is not None:
                    ts(T2, T1, -1.0, None, ALU.add)
                    tt(o_em, P0, T1, ALU.mult)
                    tt(o_em, o_em, T2, ALU.add)
                stt(o_ex, P0, 1.0, T1, ALU.add, ALU.mult)

            def time_steps(part):
                if part == 0:
                    reduce_exp(DT)
                else:
                    expm1(None, DT)

            def decays(part):
                if part == 0:
                    tt(X, ARE, DT, ALU.mult)
                    tt(Y, AIM, DT, ALU.mult)
                    reduce_exp(X)
                else:
                    expm1(EM, EX)

            def sines():
                ts(NI, Y, 1.0 / (2 * np.pi), MAGIC, ALU.mult, ALU.add)
                ts(NI, NI, MAGIC, None, ALU.subtract)
                for c in TWO_PI:
                    stt(Y, NI, -c, Y, ALU.mult, ALU.add)
                ts(H1, Y, 0.5, None, ALU.mult)
                tt(H2, H1, H1, ALU.mult)
                ts(P0, H2, SIN_C[-1], None, ALU.mult)
                for c in SIN_C[-2::-1]:
                    stt(P0, P0, c, H2, ALU.add, ALU.mult)
                stt(SH, P0, 1.0, H1, ALU.add, ALU.mult)

            def cosines():
                ts(P0, H2, COS_C[-1], None, ALU.mult)
                for c in COS_C[-2::-1]:
                    stt(P0, P0, c, H2, ALU.add, ALU.mult)
                ts(CH, P0, 1.0, None, ALU.add)
                stt(SY, SH, 2.0, CH, ALU.mult, ALU.mult)
                stt(P1, SH, -2.0, SH, ALU.mult, ALU.mult)
                ts(CY, P1, 1.0, None, ALU.add)

            def gains():
                tt(H1, EM, CY, ALU.mult)
                tt(H1, H1, P1, ALU.add)
                tt(H2, EX, SY, ALU.mult)
                tt(T0, ARE, ARE, ALU.mult)
                tt(T1, AIM, AIM, ALU.mult)
                tt(T2, T0, T1, ALU.add)
                step(dve.reciprocal(T2, T2))
                tt(T0, H1, ARE, ALU.mult)
                tt(T1, H2, AIM, ALU.mult)
                tt(T0, T0, T1, ALU.add)
                tt(KR, T0, T2, ALU.mult)
                tt(T0, H2, ARE, ALU.mult)
                tt(T1, H1, AIM, ALU.mult)
                tt(T0, T0, T1, ALU.subtract)
                tt(KI, T0, T2, ALU.mult)

            def first_entries():
                def put(o, src):
                    step(dve.tensor_copy(base_all[:, :, o], src))

                put(O_R, EX)
                put(O_KR, KR)
                put(O_KI, KI)
                step(dve.tensor_scalar(base_all[:, :, O_NKI], KI, -1.0, None, ALU.mult))
                step(dve.memset(base_all[:, :, O_B], 1.0))
                step(dve.memset(base_all[:, :, O_B + BT], 0.0))
                put(O_B + 1, CY)
                put(O_B + BT + 1, SY)
                put(O_A + AT, CH)
                dve.tensor_copy(base_all[:, :, O_A + 2 * AT], SH).then_inc(par_done, 1)

            def u_low(t):
                dve.wait_ge(u_hi, t + 1)
                low(u_all[:, t, 1, :], u[:, t, :], u_all[:, t, 0, :], u_lo)

            c4 = c_all[:, :, :].rearrange("p f (i r n) -> p (f i) r n", i=TILES, r=2)

            def c_product(n):
                g, o = divmod(n, 6)
                t = slice(2 * TILES * g, 2 * TILES * g + 2 * TILES)
                cr, ci = c4[:, t, 0, :], c4[:, t, 1, :]
                kr, ki = (v[:, t].rearrange("p (i o) -> p i o", o=1).to_broadcast([P, 2 * TILES, 32]) for v in (KR, KI))
                t1, t2 = ctmp[:, 0, :, :], ctmp[:, 1, :, :]
                f1, f2 = (v.rearrange("p (f i) n -> p f i n", f=2) for v in (t1, t2))
                if o == 0:
                    dve.wait_ge(c_landed[g], 16)
                if n == 0:
                    dve.wait_ge(x_hi, XP)
                    dve.wait_ge(x_lo, XP)
                if n > 0:
                    dve.wait_ge(cm_step, n)
                if o == 0:
                    i = dve.tensor_tensor(t1, cr, kr, ALU.mult)
                elif o == 1:
                    i = dve.tensor_tensor(t2, ci, ki, ALU.mult)
                elif o == 2:
                    i = dve.tensor_tensor(cm_all[:, 2 * g:2 * g + 2, 0, :, :], f1, f2, ALU.subtract)
                elif o == 3:
                    i = dve.tensor_tensor(t1, cr, ki, ALU.mult)
                elif o == 4:
                    i = dve.tensor_tensor(t2, ci, kr, ALU.mult)
                else:
                    i = dve.scalar_tensor_tensor(out=cm_all[:, 2 * g:2 * g + 2, 1, :, :], in0=f1, scalar=-1.0, in1=f2,
                                                 op0=ALU.mult, op1=ALU.subtract)
                i.then_inc(cm_step, 1)

            def parameters(j):
                if j == 3:
                    time_steps(0)
                elif j == 4:
                    time_steps(1)
                elif j == 6:
                    decays(0)
                elif j == 7:
                    decays(1)
                elif j == 9:
                    sines()
                elif j == 11:
                    cosines()
                elif j == 13:
                    gains()
                elif j == 14:
                    first_entries()

            for i in range(XP):
                dve.wait_ge(x_hi, i + 1)
                low(act16[:, 2 * i:2 * i + 2, 1, :], xraw[:, 2 * i:2 * i + 2, :], act16[:, 2 * i:2 * i + 2, 0, :], x_lo)
                if i in X_TO_W and X_TO_W[i] < 3:
                    split_lo(0, X_TO_W[i])
            for j in range(3, H_V + LAG):
                split_lo(0, j)
                if j - 3 in U_EVAC:
                    u_low(U_EVAC.index(j - 3))
                if j >= 16:
                    c_product(2 * (j - 16))
                    c_product(2 * (j - 16) + 1)
                if j in U_EVAC:
                    t = U_EVAC.index(j)
                    dve.wait_ge(w_used, j - LAG + 1)
                    dve.tensor_copy(u[:, t, :], ps[bank_of(N_U + t)][:, 0:T]).then_inc(uv_copied, 1)
                if j == 3:
                    dve.wait_ge(par_landed, 16)
                parameters(j)
            for j in range(LAG, 16):
                split_lo(0, H_V + j)
                if H_V + j - 3 in U_EVAC:
                    u_low(U_EVAC.index(H_V + j - 3))
                if j < 12:
                    c_product(2 * j)
                    c_product(2 * j + 1)
                if j == 8 + LAG:
                    dve.wait_ge(w_used, H_V + 8)
                    for t in range(TT):
                        dve.tensor_copy(vout[:, t, :], ps[bank_of(N_V + t)][:, :]).then_inc(uv_copied, 1)

            def v_last():
                dve.wait_ge(w_used, H_V + 16)
                dve.wait_ge(v_stored[0], 16)
                for t in range(TT):
                    dve.tensor_copy(vout[:, t, :], ps[bank_of(N_V + 2 + t)][:, :]).then_inc(uv_copied, 1)

            def turn(k, p, i):
                s = TILES * (2 * k + p) + i
                dve.wait_ge(tab_ready, 2 * s + 2)
                dve.wait_ge(bu_ready, s + 1)
                bu = ps[BU0 + i % 2][:, :].rearrange("p (c n) -> p c n", c=2)
                for j in range(2):
                    dve.tensor_tensor(m12[:, j, :, :], bu, E[:, i % 4, j:j + 1, :].to_broadcast([P, 2, T]), ALU.mult
                                      ).then_inc(bu_read, 1)
                dve.wait_ge(bu_read, 2 * s + 2)
                if not (isinstance(s, int) and s == 0):
                    dve.wait_ge(z_ready, 2 * s)
                dve.tensor_tensor(wz[:, 0, :], m12[:, 0, 0, :], m12[:, 1, 1, :], ALU.add).then_inc(w_turned, 1)
                dve.tensor_tensor(wz[:, 1, :], m12[:, 0, 1, :], m12[:, 1, 0, :], ALU.subtract).then_inc(w_turned, 1)
                dve.wait_ge(w_turned, 2 * s + 2)
                if not (isinstance(s, int) and s < 2):
                    dve.wait_ge(prod_ready, 2 * s - 2)
                r = base[:, p, i, O_R:O_R + 1].to_broadcast([P, T])
                for j in range(2):
                    dve.tensor_tensor_scan(z[:, i % 2, j, :], r, wz[:, j, :], 0.0, ALU.mult, ALU.add).then_inc(z_ready, 1)

            def finish(f, p):
                dve.wait_ge(y_done, 2 * f + 2)
                uf = u[:, bass.ds(f, 1), :]
                ft = fin_t[:, :].rearrange("p (o n) -> p o n", o=1)
                dve.scalar_tensor_tensor(out=ft, in0=uf, scalar=col[:, bass.ds(72 + f, 1)],
                                         in1=ps[YB][:, 0:T].rearrange("p (o n) -> p o n", o=1), op0=ALU.mult,
                                         op1=ALU.add).then_inc(fin_step, 1)
                dve.wait_ge(fin_step, 2 * f + 1)
                dve.tensor_tensor(uf, ft, ps[YB][:, T:2 * T][:, ::-1].rearrange("p (o n) -> p o n", o=1), ALU.add
                                  ).then_inc(fin_step, 1)

            def softmax_max(k, p):
                f = 2 * k + p
                dve.wait_ge(bias_staged[p], 16 * k + 16)
                dve.wait_ge(sc_ready, f + 1)
                if not (isinstance(f, int) and f == 0):
                    dve.wait_ge(tr_ready, f)
                dve.scalar_tensor_tensor(out=S[:, :, :], in0=ps[AB][:, :].rearrange("p (t n) -> p t n", t=TT), scalar=SCALE,
                                         in1=bm[:, p, :, :], op0=ALU.mult, op1=ALU.add).then_inc(soft_step, 1)
                dve.wait_ge(soft_step, 3 * f + 1)
                dve.tensor_reduce(sm[:, 0, :], S[:, :, :], AX.X, ALU.max).then_inc(soft_step, 1)
                dve.wait_ge(soft_step, 3 * f + 2)
                dve.tensor_scalar(sm[:, 1, :], sm[:, 0, :], -1.0, None, ALU.mult).then_inc(soft_step, 1)

            def softmax_inverse(k, p):
                f = 2 * k + p
                dve.wait_ge(exp_ready, 2 * f + 2)
                dve.reciprocal(sm[:, 3, :], sm[:, 2, :]).then_inc(sum_inv, 1)

            def attn_low(f):
                dve.wait_ge(att_hi, f + 1)
                low(act8a[:, bass.ds(f, 1), 1, :], ps[AB][:, 0:T].rearrange("p (o n) -> p o n", o=1),
                    act8a[:, bass.ds(f, 1), 0, :], att_lo)

            dve.wait_ge(col_landed, 16)

            def one_pass(k, p, first):
                c0 = H_LOOP + PER_F * p
                for j in range(PER_F):
                    split_lo(2 * k, c0 + j)
                    if j == 1 and first:
                        v_last()
                    if j == 4 and not first:
                        finish(2 * k + p - 1, 1 - p)
                    if j == 2 and not first:
                        attn_low(2 * k + p - 1)
                    if j == 7:
                        softmax_max(k, p)
                    if j == 8:
                        softmax_inverse(k, p)
                    for i in range(TILES):
                        if BU_SLOT[i] + LAG == j:
                            turn(k, p, i)

            one_pass(0, 0, True)
            one_pass(0, 1, False)
            with dve.Fori(1, HEADS // 2) as k:
                one_pass(k, 0, False)
                one_pass(k, 1, False)

            def na_gate(t, h):
                dve.wait_ge(w_used, h + 1)
                dve.wait_ge(ga_sig, t + 1)
                dve.tensor_tensor(ga[:, t, :], ps[bank_of(N_NA1 + t if t < 8 else N_NA2 + t - 8)][:, 0:T], ga[:, t, :],
                                  ALU.mult).then_inc(na_gated, 1)

            for j in range(8):
                split_lo(0, H_NA1 + j)
                if j == 0:
                    attn_low(HEADS - 1)
                if j == 4:
                    finish(HEADS - 1, 1)
                if j == 6:
                    dve.wait_ge(ys_hi, 1)
                    low(act8b[:, :, 1, :], u[:, :, :], act8b[:, :, 0, :], ys_lo)
                if j >= LAG_P:
                    na_gate(j - LAG_P, H_NA1 + j - LAG_P)

            def glu_mult(t):
                dve.wait_ge(glu_sig, t + 1)
                dve.tensor_tensor(u[:, t, :], u[:, t, :], ev2[:, t % 4, :], ALU.mult).then_inc(glu_y, 1)

            for j in range(8):
                split_lo(0, H_GLU + j)
                if j < LAG_P:
                    na_gate(8 - LAG_P + j, H_GLU - LAG_P + j)
                if j >= LAG_P + 1:
                    glu_mult(j - LAG_P - 1)
            for j in range(8):
                split_lo(0, H_NA2 + j)
                if j >= LAG_P:
                    na_gate(8 + j - LAG_P, H_NA2 + j - LAG_P)
                if j < LAG_P + 1:
                    glu_mult(8 - LAG_P - 1 + j)
                if j >= 4:
                    for t in (2 * (j - 4), 2 * (j - 4) + 1):
                        dve.wait_ge(glu_hi, t + 1)
                        low(act8b[:, t, 1, :], u[:, t, :], act8b[:, t, 0, :], glu_lo)
            for t in range(16 - LAG_P, 16):
                na_gate(t, H_NA2 + t - 8)

            def s5o_evac(t):
                dve.wait_ge(w_used, H_S5O + t + 1)
                dve.wait_ge(gs_sig, t + 1)
                dve.tensor_tensor(gs[:, t, :], ps[bank_of(N_S5O + t)][:, 0:T], gs[:, t, :], ALU.mult).then_inc(so_gated, 1)
                dve.wait_ge(so_gated, t + 1)
                dve.tensor_tensor(ga[:, t, :], gs[:, t, :], ga[:, t, :], ALU.add).then_inc(mix_ready, 1)

            def mix_low(t):
                dve.wait_ge(mix_hi, t + 1)
                low(act16[:, t, 1, :], ga[:, t, :], act16[:, t, 0, :], mix_lo)

            for j in range(KD):
                split_lo(0, H_S5O + j)
                if j >= LAG_P:
                    s5o_evac(j - LAG_P)
                if j >= LAG_P + 2:
                    mix_low(j - LAG_P - 2)

            def residual(n, h, t, b):
                dve.wait_ge(w_used, h + 1)
                v = hp[:, t, b * 512:(b + 1) * 512]
                dve.scalar_tensor_tensor(out=v, in0=v, scalar=ALPHA, in1=ps[bank_of(n)][:, :], op0=ALU.mult, op1=ALU.add
                                         ).then_inc(res_added, 1)
                dve.wait_ge(*taken(n))
                dve.bn_stats(stats[:, t, b, :], v).then_inc(stat_ready, 1)

            def centre(i):
                t, b = i // 4, slice(i % 4 * 512, i % 4 * 512 + 512)
                dve.scalar_tensor_tensor(out=hp[:, t, b], in0=hp[:, t, b], scalar=lnm[:, t, 0:1], in1=lnrow[:, 0, b],
                                         op0=ALU.subtract, op1=ALU.mult).then_inc(ln2_gain, 1)

            def moments(e, between=None):
                dve.wait_ge(stat_ready, 8 * (e + 1))
                for t in range(TT):
                    dve.bn_aggr(lnm[:, t, 0:2], stats[:, t, :, :].rearrange("p a b -> p (a b)")).then_inc(var_ready, 1)
                dve.wait_ge(var_ready, TT * (e + 1))
                if between:
                    between()
                dve.wait_ge(sd_ready, e + 1)
                dve.reciprocal(lnm[:, :, 2:3], lnm[:, :, 4:5]).then_inc(ln_step, 1)
                dve.wait_ge(ln_step, 2 * e + 1)
                dve.scalar_tensor_tensor(out=lnm[:, :, 3:4], in0=lnm[:, :, 0:1], scalar=-1.0, in1=lnm[:, :, 2:3],
                                         op0=ALU.mult, op1=ALU.mult).then_inc(ln_step, 1)
                dve.wait_ge(ln_step, 2 * e + 2)

            for j in range(32):
                split_lo(0, H_WO + j)
                if j < LAG_P:
                    s5o_evac(KD - LAG_P + j)
                if j < LAG_P + 2:
                    mix_low(KD - LAG_P - 2 + j)
                if j == 4:
                    dve.wait_ge(xtok_landed, 64)
                if j % 8 == 1 and j > 8:
                    for t in range(TT):
                        b = j // 8 - 1
                        residual(N_WO + 2 * b + t, H_WO + 8 * b + 7, t, b)
            for c in range(3):
                split_lo(0, H_FF + c)
            for t in range(TT):
                residual(N_WO + 6 + t, H_WO + 31, t, 3)
            moments(0)
            for b in range(4):
                for t in range(TT):
                    v = hp[:, t, b * 512:(b + 1) * 512]
                    dve.tensor_scalar(v, v, lnm[:, t, 2:3], lnm[:, t, 3:4], ALU.mult, ALU.add).then_inc(norm_ready, 1)
            for g in range(8):
                dve.wait_ge(hT_hi, g + 1)
                low(act16[:, 2 * g:2 * g + 2, 1, :], hT[:, g % 2, :, :], act16[:, 2 * g:2 * g + 2, 0, :], hT_lo)
                if g == 5:
                    split_lo(0, H_FF + 3)

            def ff(m, count=3):
                for i in range(count):
                    for q in range(4):
                        split_lo(m, H_FF + 4 * i + q)
                        if q == 1:
                            up(3 * m + i - 1, i - 1, 12 * m + (H_FF + 4 * i))
                        if q == 3:
                            mid_low(3 * m + i - 1, (i - 1) % 3)

            def up(n, i, used):
                dve.wait_ge(w_used, used)
                dve.wait_ge(g_silu, n + 1)
                dve.tensor_tensor(ev2[:, i % 3, :], ps[bank_of(N_FF + (2 * i + 1) % 6)][:, 0:T], ev[:, i % 3, :], ALU.mult
                                  ).then_inc(mid_ready, 1)

            def mid_low(n, r):
                dve.wait_ge(mid_hi, n + 1)
                low(mid[:, bass.ds(n, 1), 1, :], ev2[:, r:r + 1, :], mid[:, bass.ds(n, 1), 0, :], mid_lo)

            for c in range(4, 12):
                split_lo(0, H_FF + c)
                if c == 7:
                    up(0, 0, H_FF + 6)
                if c == 9:
                    mid_low(0, 0)
                    up(1, 1, H_FF + 8)
                if c == 11:
                    mid_low(1, 1)
            with dve.Fori(1, KF // 3) as m:
                ff(m)
            ff(KF // 3, KF % 3)

            def dn_evac(b):
                for t in range(TT):
                    residual(N_DN + 2 * b + t, H_DN + 22 * b + 21, t, b)

            for c in range(4 * (KF // 2)):
                split_lo(0, H_DN + c)
                if c == 1:
                    up(KF - 1, KF % 3 - 1, H_DN)
                if c == 3:
                    mid_low(KF - 1, (KF - 1) % 3)
                    dve.wait_ge(h_step, 4)
                if c >= 24 and (c - 24) % 22 == 0:
                    dn_evac((c - 24) // 22)
            dn_evac(3)
            dve.wait_ge(ln2_landed, 32)
            moments(1, lambda: centre(LN2_DVE[0]))
            for n, i in enumerate(LN2_DVE):
                if n > 0:
                    centre(i)
                t, b = i // 4, slice(i % 4 * 512, i % 4 * 512 + 512)
                dve.wait_ge(ln2_gain, n + 1)
                dve.scalar_tensor_tensor(out=hp[:, t, b], in0=hp[:, t, b], scalar=lnm[:, t, 2:3], in1=lnrow[:, 1, b],
                                         op0=ALU.mult, op1=ALU.add).then_inc(ln2_dve, 1)

        @block.tensor
        def _(pe):
            def wait_split(m, c):
                pe.wait_ge(lo_ready, 12 * m + (c + 1))

            def prod_a(m, c, act, k0, kn, bank, start, stop, ready=None):
                s = c % SPL
                for i in range(kn):
                    if ready:
                        ready(k0 + i)
                    hi, lo = (w[:, s, i * P:(i + 1) * P] for w in (whi, wlo))
                    pe.matmul(bank[:, 0:T], hi, act[:, k0 + i, 0, :], start=start and i == 0, stop=False)
                    pe.matmul(bank[:, 0:T], hi, act[:, k0 + i, 1, :], start=False, stop=False)
                    mm = pe.matmul(bank[:, 0:T], lo, act[:, k0 + i, 0, :], start=False, stop=stop and i == kn - 1)
                mm.then_inc(w_used, 1)

            def prod_b(c, act, k0, banks, start, stop):
                s = c % SPL
                for i in range(2):
                    hi, lo = (w[:, s, i * 512:(i + 1) * 512] for w in (whi, wlo))
                    for t in range(TT):
                        a = act[:, k0 + i, 0, t * P:(t + 1) * P]
                        b = act[:, k0 + i, 1, t * P:(t + 1) * P]
                        pe.matmul(banks[t][:, :], a, hi, start=start and i == 0, stop=False)
                        pe.matmul(banks[t][:, :], a, lo, start=False, stop=False)
                        mm = pe.matmul(banks[t][:, :], b, hi, start=False, stop=stop and i == 1)
                mm.then_inc(w_used, 1)

            def wait_bank(n):
                o = bank_before(n)
                if o is not None:
                    pe.wait_ge(*taken(o))

            def x_split(kt):
                if kt % 2 == 0:
                    pe.wait_ge(x_lo, kt // 2 + 1)

            for j, (n, h) in enumerate(U_ORDER):
                if h == 0:
                    wait_bank(N_U + n)
                wait_split(0, j)
                prod_a(0, j, act16, 8 * h, 8, ps[bank_of(N_U + n)], h == 0, h == 1,
                       x_split if n == 0 else None)
            for j in range(16):
                n = N_V + 2 * (j // 8)
                if j % 8 == 0:
                    wait_bank(n)
                    wait_bank(n + 1)
                wait_split(0, H_V + j)
                prod_b(H_V + j, act16, 2 * (j % 8), [ps[bank_of(n)], ps[bank_of(n + 1)]], j % 8 == 0, j % 8 == 7)

            def s5_in(k, p, i):
                f = 2 * k + p
                s = TILES * f + i
                d, q = i // 4, i % 4
                if i == 0:
                    pe.wait_ge(u3_ready, f + 1)
                if q == 0:
                    pe.wait_ge(b3_ready, 2 * f + (d + 1))
                if not (isinstance(s, int) and s < 2):
                    pe.wait_ge(bu_read, 2 * s - 2)
                ut = u3[0:96, p, q, ::-1] if d else u3[0:96, p, q, :]
                for c in range(2):
                    mm = pe.matmul(ps[BU0 + i % 2][:, c * T:(c + 1) * T], b3[0:96, d, q, c * P:(c + 1) * P], ut,
                                   start=True, stop=True)
                mm.then_inc(bu_ready, 1)

            def s5_out(f, k, p, d):
                pe.wait_ge(prod_ready, 16 * f + (8 * d + 8))
                if d == 0:
                    pe.wait_ge(cm_staged[p], 16 * k + 16)
                if d == 0 and not (isinstance(f, int) and f == 0):
                    pe.wait_ge(fin_step, 2 * f)
                for e in range(4):
                    for q in range(4):
                        mm = pe.matmul(ps[YB][32 * q:32 * q + 32, d * T:(d + 1) * T],
                                       cmat[:, p, (0, 1, 1, 2)[e], 4 * d + q, :], prod[:, q, e, :],
                                       start=e == 0, stop=e == 3)
                mm.then_inc(y_done, 1)

            def scores(k, p):
                f = 2 * k + p
                pe.wait_ge(loop_copied, 6 * f + 2)
                if not (isinstance(f, int) and f == 0):
                    pe.wait_ge(att_lo, f)
                for t in range(TT):
                    mm = pe.matmul(ps[AB][:, t * T:(t + 1) * T], qk[:, p, 0, t * P:(t + 1) * P], qk[:, p, 1, :],
                                   start=True, stop=True)
                mm.then_inc(sc_ready, 1)

            def transposes(k, p):
                f = 2 * k + p
                pe.wait_ge(p_ready, 2 * f + 2)
                if isinstance(f, int) and f == 0:
                    pe.wait_ge(const_step, 3)
                else:
                    pe.wait_ge(pt_ready, f)
                for b in range(TT):
                    for t in range(TT):
                        mm = pe.transpose(ps[TB][:, (b * TT + t) * P:(b * TT + t + 1) * P], S[:, t, b * P:(b + 1) * P],
                                          ident[:, :])
                mm.then_inc(tr_ready, 1)

            def attend(f, k, p):
                pe.wait_ge(pt_ready, f + 1)
                pe.wait_ge(v_staged[p], 16 * k + 16)
                for b in range(TT):
                    mm = pe.matmul(ps[AB][:, 0:T], vcur[:, p, b, :], PT[:, b, :], start=b == 0, stop=b == TT - 1)
                mm.then_inc(pv_done, 1)

            def before(k, p):
                return (2 * k, k, 0) if p else (2 * k - 1, k - 1, 1)

            def one_pass(k, p, first):
                for j in range(PER_F):
                    o = j // 2
                    n = N_LOOP + o
                    if j % 2 == 0:
                        if first and o < 3:
                            wait_bank(n)
                        else:
                            pe.wait_ge(loop_copied, 6 * (2 * k + p) + (o - 2))
                    c = H_LOOP + PER_F * p + j
                    wait_split(2 * k, c)
                    prod_a(2 * k, c, act16, 8 * (j % 2), 8, ps[bank_of(n)], j % 2 == 0, j % 2 == 1)
                    if not first:
                        f1, k1, p1 = before(k, p)
                        if j == 0:
                            s5_out(f1, k1, p1, 1)
                    if j == 4:
                        scores(k, p)
                    if j == Y_SLOT:
                        s5_out(2 * k + p, k, p, 0)
                    for i in range(TILES):
                        if BU_SLOT[i] == j:
                            s5_in(k, p, i)
                    if j == 8:
                        transposes(k, p)
                    if j == 11:
                        attend(2 * k + p, k, p)

            one_pass(0, 0, True)
            one_pass(0, 1, False)
            with pe.Fori(1, HEADS // 2) as k:
                one_pass(k, 0, False)
                one_pass(k, 1, False)

            def last_head(kt):
                if kt == HEADS - 1:
                    pe.wait_ge(att_lo, HEADS)

            for j in range(24):
                h, n = H_NA1 + j, N_NA1 + j
                if j == 8:
                    pe.wait_ge(ys_lo, 1)
                if j == 3:
                    pe.wait_ge(bu_read, 2 * TILES * KS)
                if j == 5:
                    pe.wait_ge(pt_ready, HEADS)
                wait_bank(n)
                wait_split(0, h)
                prod_a(0, h, act8b if 8 <= j < 16 else act8a, 0, 8, ps[bank_of(n)], True, True,
                       last_head if j == 0 else None)
                if j == 2:
                    s5_out(HEADS - 1, HEADS // 2 - 1, 1, 1)
            for j in range(KD):
                wait_bank(N_S5O + j)
                wait_split(0, H_S5O + j)
                if j == 0:
                    pe.wait_ge(glu_lo, KS)
                prod_a(0, H_S5O + j, act8b, 0, 8, ps[bank_of(N_S5O + j)], True, True)
            for j in range(32):
                n = N_WO + 2 * (j // 8)
                if j % 8 == 0:
                    wait_bank(n)
                    wait_bank(n + 1)
                wait_split(0, H_WO + j)
                if j < 8:
                    pe.wait_ge(mix_lo, 2 * j + 2)
                prod_b(H_WO + j, act16, 2 * (j % 8), [ps[bank_of(n)], ps[bank_of(n + 1)]], j % 8 == 0, j % 8 == 7)
            def h_rows(g):
                pe.wait_ge(norm_ready, 2 * (g // 2) + 2)
                if g < 4:
                    pe.wait_ge(res_added, 8)
                else:
                    pe.wait_ge(hT_hi, g - 3)
                for e in range(2):
                    for t in range(TT):
                        mm = pe.transpose(ps[4 + g % 4][:, e * T + t * P:e * T + (t + 1) * P],
                                          hp[:, t, (2 * g + e) * P:(2 * g + e + 1) * P], ident[:, :])
                mm.then_inc(hT_psum, 1)

            def h_split(kt):
                if kt % 2 == 0:
                    pe.wait_ge(hT_lo, kt // 2 + 1)
                    if kt < 8:
                        h_rows(4 + kt // 2)

            for g in range(4):
                h_rows(g)
            for c, (o, h) in enumerate(FF_ORDER):
                if h == 0:
                    wait_bank(N_FF + o)
                wait_split(0, H_FF + c)
                prod_a(0, H_FF + c, act16, 8 * h, 8, ps[bank_of(N_FF + o)], h == 0, h == 1,
                       h_split if o == 0 else None)

            def ff(m, count=3):
                for i in range(count):
                    for q in range(4):
                        n = N_FF + 2 * i + q // 2
                        if q % 2 == 0:
                            pe.wait_ge(g_silu if q == 0 else mid_ready, 3 * m + (i - 2))
                        wait_split(m, H_FF + 4 * i + q)
                        prod_a(m, H_FF + 4 * i + q, act16, 8 * (q % 2), 8, ps[bank_of(n)], q % 2 == 0, q % 2 == 1)

            with pe.Fori(1, KF // 3) as m:
                ff(m)
            ff(KF // 3, KF % 3)
            for j in range(4 * (KF // 2)):
                b, i = divmod(j, KF // 2)
                n = N_DN + 2 * b
                if i == 0:
                    wait_bank(n)
                    wait_bank(n + 1)
                wait_split(0, H_DN + j)
                if b == 0:
                    pe.wait_ge(mid_lo, 2 * i + 2)
                prod_b(H_DN + j, mid, 2 * i, [ps[bank_of(n)], ps[bank_of(n + 1)]], i == 0, i == KF // 2 - 1)


def kernel(**inputs):
    import concourse.bacc as bacc
    from concourse.bass_utils import run_bass_kernel_spmd

    a = {n: np.asarray(v) for n, v in inputs.items()}
    w = a["w_in"][0]

    def kind_a(m):
        k, n = m.shape
        return m.reshape(k // 1024, 8, P, n // P, P).transpose(3, 0, 2, 1, 4).reshape(-1, P, HC)

    def kind_b(m):
        k, n = m.shape
        return m.reshape(k // 256, 2, P, n // 512, 512).transpose(3, 0, 2, 1, 4).reshape(-1, P, HC)

    q, k, v, u, g1, g2 = np.split(w, [NW, 2 * NW, 3 * NW, 3 * NW + SW, 3 * NW + SW + D], axis=1)
    qa, ka = kind_a(q).reshape(8, 2, P, HC), kind_a(k).reshape(8, 2, P, HC)
    g1a, g2a = kind_a(g1).reshape(8, 4, P, HC), kind_a(g2).reshape(8, 4, P, HC)
    loop = np.concatenate([qa, ka, g1a, g2a], axis=1).reshape(-1, P, HC)
    na = kind_a(a["w_na_out"][0])
    ff = np.concatenate([kind_a(a["w_ffn_gate"][0]).reshape(KF, 2, P, HC),
                         kind_a(a["w_ffn_up"][0]).reshape(KF, 2, P, HC)], axis=1).reshape(-1, P, HC)
    ff[0:12] = ff[[2 * n + h for n, h in FF_ORDER]]
    wstream = np.concatenate([kind_a(u)[[2 * n + h for n, h in U_ORDER]], kind_b(v), loop, na[:8], kind_a(a["w_glu"][0]), na[8:],
                              kind_a(a["w_s5_out"][0]), kind_b(a["w_out"][0]), ff, kind_b(a["w_ffn_down"][0])])

    x = a["x"][0]
    xT = x.T.reshape(KD, P, T).transpose(1, 0, 2)

    def states(m):
        return m.reshape(2, KS, 4, 2, NS).transpose(3, 4, 1, 0, 2).reshape(P, GROUPS)

    log_dt = np.broadcast_to(a["s5_log_dt"][0][:, :, None], (2, GROUPS, NS))
    params = np.stack([states(a["s5_a_re"][0]), states(a["s5_a_im"][0]), states(log_dt)], axis=1)
    b_rows = np.zeros((4, 2, GC, KS, 2, 2, 2, NS), np.float32)
    c_rows = np.zeros((2, NS, KS, 2, 4, 2, 2, GC), np.float32)
    for ri in range(2):
        b = a[("s5_b_re", "s5_b_im")[ri]][0].reshape(2, KS, 4, 2, NS, GC)
        c = a[("s5_c_re", "s5_c_im")[ri]][0].reshape(2, KS, 4, 2, GC, NS)
        for g in range(2):
            b_rows[:, g, :, :, :, ri, g, :] = b[:, :, :, g].transpose(2, 4, 1, 0, 3)
            c_rows[g, :, :, :, :, ri, g, :] = c[:, :, :, g].transpose(4, 1, 0, 2, 3)
    b_rows = b_rows.reshape(P, KS, 512)
    c_rows = c_rows.reshape(P, KS, 512)

    rpb = a["na_rpb"][0]
    bias = np.full((HEADS, 2, GRID_W, TT, ROWS, GRID_W), -1e30, np.float32)
    for t in range(TT):
        for rl in range(2):
            row = NA_ROWS - 1 - (2 * t + rl)
            for qc in range(GRID_W):
                c0 = min(max(qc - WIN // 2, 0), GRID_W - WIN)
                bias[:, rl, qc, t, :, c0:c0 + WIN] = rpb[:, row:row + ROWS, c0 - qc + WIN - 1:c0 - qc + 2 * WIN - 1]
    bias = bias.reshape(HEADS, P, TT * T)

    cols = np.concatenate([a["b_gate"][0].reshape(32, P), a["b_glu"][0].reshape(8, P), a["ln1_g"][0].reshape(KD, P),
                           a["ln1_b"][0].reshape(KD, P), a["s5_d"][0].reshape(KS, P)]).T
    lnrows = np.stack([a["ln1_g"][0], a["ln1_b"][0], a["ln2_g"][0], a["ln2_b"][0]])

    arrays = {"wstream": wstream, "xT": xT, "xtok": x, "b_rows": b_rows, "c_rows": c_rows, "params": params, "bias": bias, "cols": cols,
              "lnrows": lnrows}
    arrays = {n: np.ascontiguousarray(v) for n, v in arrays.items()}
    nc = bacc.Bacc("TRN2", target_bir_lowering=False, num_devices=1)
    args = {n: nc.dram_tensor(n, v.shape, F32, kind="ExternalInput").ap() for n, v in arrays.items()}
    out = nc.dram_tensor("out", (T, D), F32, kind="ExternalOutput").ap()
    build(nc, out=out, **args)
    r = run_bass_kernel_spmd(nc, [arrays], core_ids=[0])
    return r.results[0]["out"].reshape(1, T, D)
```
